# Optimizing a Trainium2 kernel written in Bass

```python
import math
import jax
import jax.numpy as jnp
from jax import lax
import numpy as np

D_MODEL = 1024
BATCH = 1
SEQ = 512
DEPTH = 1
DEC_BATCH = 8
DEC_SEQ = 8
PAST_LEN = 4096
PAGE_SIZE = 128

D_MIX = D_MODEL
D_A = D_MIX // 2
D_B = D_MIX - D_A
DH_A = 128
H_A = D_A // DH_A
DH_B = 64
H_B = D_B // DH_B
CONV_W = 4
CHUNK = 64
R_DECAY = 64
R_AAA = 64
R_GATE = 128
D_A_IN = 4 * D_A + 2 * H_A
D_B_IN = 3 * D_B + R_DECAY + R_AAA + R_GATE
D_IN = D_A_IN + D_B_IN
N_EXPERTS = 16
N_GROUPS = 4
EXPERTS_PER_GROUP = N_EXPERTS // N_GROUPS
TOP_K = 2
D_EXP = 512
ALPHA = (2 * DEPTH) ** 0.25
BETA = (8 * DEPTH) ** -0.25
LN_EPS = 1e-5
GN_EPS_A = 1e-6
GN_EPS_B = 64e-5

kernel_name = 'hybrid_mlstm_rwkv7_moe_step'

def layer_norm(x, g, b, eps=LN_EPS):
    xf = x.astype(jnp.float32)
    mu = xf.mean(-1, keepdims=True)
    var = jnp.square(xf - mu).mean(-1, keepdims=True)
    return ((xf - mu) * lax.rsqrt(var + eps)).astype(x.dtype) * g + b

def head_norm(x, eps):
    xf = x.astype(jnp.float32)
    mu = xf.mean(-1, keepdims=True)
    var = jnp.square(xf - mu).mean(-1, keepdims=True)
    return (xf - mu) * lax.rsqrt(var + eps)

def causal_conv(u, buf, w, b):
    L = u.shape[1]
    full = jnp.concatenate([buf.astype(u.dtype), u], axis=1)
    out = b + sum(full[:, j:j + L] * w[j] for j in range(CONV_W))
    return out, full[:, L:]

def token_shift(p, prev, mu):
    prev_seq = jnp.concatenate([prev[:, None].astype(p.dtype), p[:, :-1]], axis=1)
    return p + (prev_seq - p) * mu, p[:, -1]

def mlstm_chunked(q, k, v, li, lf, C0, n0, m0):
    f32 = jnp.float32
    B, L, H, dh = q.shape
    c = math.gcd(L, CHUNK)
    nc = L // c
    to_chunks = lambda t: t.astype(f32).reshape(B, nc, c, H, -1).transpose(1, 0, 3, 2, 4)
    gate_chunks = lambda t: t.astype(f32).reshape(B, nc, c, H).transpose(1, 0, 3, 2)
    causal = jnp.tril(jnp.ones((c, c), bool))

    def step(carry, inp):
        C, n, m = carry
        qc, kc, vc, lic, lfc = inp
        b = jnp.cumsum(lfc, -1)
        dmat = jnp.where(causal, b[..., :, None] - b[..., None, :] + lic[..., None, :], -jnp.inf)
        m_inter = b + m[..., None]
        m_t = jnp.maximum(m_inter, dmat.max(-1))
        s = jnp.einsum('bhtd,bhsd->bhts', qc, kc) * jnp.exp(dmat - m_t[..., None])
        w_inter = jnp.exp(m_inter - m_t)
        num = w_inter[..., None] * jnp.einsum('bhtd,bhde->bhte', qc, C) + jnp.einsum('bhts,bhse->bhte', s, vc)
        den = w_inter * jnp.einsum('bhtd,bhd->bht', qc, n) + s.sum(-1)
        h = num / jnp.maximum(jnp.abs(den), jnp.exp(-m_t))[..., None]
        b_last = b[..., -1]
        g_s = b_last[..., None] - b + lic
        m_new = jnp.maximum(b_last + m, g_s.max(-1))
        w_s = jnp.exp(g_s - m_new[..., None])
        w_old = jnp.exp(b_last + m - m_new)
        C = w_old[..., None, None] * C + jnp.einsum('bhs,bhsd,bhse->bhde', w_s, kc, vc)
        n = w_old[..., None] * n + jnp.einsum('bhs,bhsd->bhd', w_s, kc)
        return (C, n, m_new), h

    (C, n, m), h = lax.scan(step, (C0.astype(f32), n0.astype(f32), m0.astype(f32)),
                            (to_chunks(q), to_chunks(k), to_chunks(v), gate_chunks(li), gate_chunks(lf)))
    h = h.transpose(1, 0, 3, 2, 4).reshape(B, L, H, dh)
    return h, C, n, m

def rwkv7_recurrence(r, decay, k, v, kk, a, S0):
    f32 = jnp.float32
    seq = tuple(jnp.moveaxis(t.astype(f32), 1, 0) for t in (r, decay, k, v, kk, a))

    def step(S, inp):
        r_t, w_t, k_t, v_t, kk_t, a_t = inp
        sa = jnp.einsum('bhvk,bhk->bhv', S, -kk_t)
        S = (S * w_t[..., None, :] + sa[..., :, None] * (kk_t * a_t)[..., None, :]
             + v_t[..., :, None] * k_t[..., None, :])
        return S, jnp.einsum('bhvk,bhk->bhv', S, r_t)

    S, out = lax.scan(step, S0.astype(f32), seq)
    return jnp.moveaxis(out, 0, 1), S

def mixer_block(x, C0, n0, m0, conv0, S0, shift0, w_in, conv_w, conv_b, b_i, b_f, gn_a_g,
                mu_shift, w0, w2, a0, a2, g2, k_k, k_a, r_k, lnx_g, lnx_b, w_out):
    f32 = jnp.float32
    B, L, _ = x.shape
    p = x @ w_in
    pa = p[..., :D_A_IN]
    qk, conv_new = causal_conv(pa[..., :2 * D_A], conv0, conv_w, conv_b)
    qk = jax.nn.silu(qk)
    q = qk[..., :D_A].reshape(B, L, H_A, DH_A)
    k = qk[..., D_A:].reshape(B, L, H_A, DH_A) * (DH_A ** -0.5)
    v = pa[..., 2 * D_A:3 * D_A].reshape(B, L, H_A, DH_A)
    o_pre = pa[..., 3 * D_A:4 * D_A]
    i_pre = (pa[..., 4 * D_A:4 * D_A + H_A] + b_i).astype(f32)
    f_pre = (pa[..., 4 * D_A + H_A:] + b_f).astype(f32)
    h, C, n, m = mlstm_chunked(q, k, v, i_pre, jax.nn.log_sigmoid(f_pre), C0, n0, m0)
    h_a = (head_norm(h, GN_EPS_A).reshape(B, L, D_A).astype(x.dtype) * gn_a_g) * jax.nn.sigmoid(o_pre)
    pb, shift_new = token_shift(p[..., D_A_IN:], shift0, mu_shift)
    r = pb[..., :D_B]
    kr = pb[..., D_B:2 * D_B]
    vr = pb[..., 2 * D_B:3 * D_B]
    o = 3 * D_B
    wl = pb[..., o:o + R_DECAY]
    al = pb[..., o + R_DECAY:o + R_DECAY + R_AAA]
    gl = pb[..., o + R_DECAY + R_AAA:]
    wlog = (-jax.nn.softplus(-(w0 + jnp.tanh(wl) @ w2)) - 0.5).astype(f32)
    decay = jnp.exp(-jnp.exp(wlog))
    a = jax.nn.sigmoid(a0 + al @ a2)
    g = jax.nn.sigmoid(gl) @ g2
    heads = lambda t: t.reshape(B, L, H_B, DH_B)
    kk = heads(kr * k_k).astype(f32)
    kk = kk / jnp.maximum(jnp.sqrt(jnp.sum(kk * kk, -1, keepdims=True)), 1e-12)
    kr = kr * (1 + (a - 1) * k_a)
    rh, kh, vh = heads(r), heads(kr), heads(vr)
    out, S = rwkv7_recurrence(rh, heads(decay), kh, vh, kk, heads(a), S0)
    out = (head_norm(out, GN_EPS_B).reshape(B, L, D_B).astype(x.dtype) * lnx_g + lnx_b)
    bonus = (jnp.sum(rh * kh * r_k, -1, keepdims=True) * vh).reshape(B, L, D_B)
    h_b = (out + bonus) * g
    y = jnp.concatenate([h_a, h_b], axis=-1) @ w_out
    sd = C0.dtype
    return y, (C.astype(sd), n.astype(sd), m.astype(sd), conv_new.astype(sd), S.astype(sd), shift_new.astype(sd))

def moe(x, w_router, b_router, wg, wu, wd):
    f32 = jnp.float32
    B, L, D = x.shape
    xf = x.reshape(B * L, D)
    probs = jax.nn.softmax((xf @ w_router).astype(f32), axis=-1)
    sel = (probs + b_router.astype(f32)).reshape(-1, N_GROUPS, EXPERTS_PER_GROUP)
    grp_score = lax.top_k(sel, TOP_K)[0].sum(-1)
    g_idx = jnp.argmax(grp_score, axis=-1)
    in_grp = jnp.take_along_axis(sel, g_idx[:, None, None], axis=1)[:, 0]
    _, local = lax.top_k(in_grp, TOP_K)
    e_idx = g_idx[:, None] * EXPERTS_PER_GROUP + local
    wts = jnp.take_along_axis(probs, e_idx, axis=1)
    wts = wts / wts.sum(-1, keepdims=True)
    gate = jnp.einsum('nk,nke->ne', wts, jax.nn.one_hot(e_idx, N_EXPERTS, dtype=f32)).astype(x.dtype)
    y = jnp.zeros_like(xf)
    for e in range(N_EXPERTS):
        hid = jax.nn.silu(xf @ wg[e]) * (xf @ wu[e])
        y = y + gate[:, e:e + 1] * (hid @ wd[e])
    return y.reshape(B, L, D)

def setup_inputs(seed: int = 0) -> dict:
    key = jax.random.key(seed)
    ks = iter(jax.random.split(key, 48))
    f32 = jnp.float32
    nrm = lambda shape, s=1.0: jax.random.normal(next(ks), shape, f32) * s
    return {
        'x_prompt': nrm((BATCH, SEQ, D_MODEL)),
        'x_sample': nrm((DEC_BATCH, DEC_SEQ, D_MODEL)),
        'state_mlstm_C': nrm((DEPTH, DEC_BATCH, H_A, DH_A, DH_A), 0.1),
        'state_mlstm_n': nrm((DEPTH, DEC_BATCH, H_A, DH_A), 0.1),
        'state_mlstm_m': nrm((DEPTH, DEC_BATCH, H_A)),
        'state_mlstm_conv': nrm((DEPTH, DEC_BATCH, CONV_W - 1, 2 * D_A)),
        'state_rwkv_S': nrm((DEPTH, DEC_BATCH, H_B, DH_B, DH_B), 0.1),
        'state_rwkv_shift': nrm((DEPTH, DEC_BATCH, D_B_IN)),
        'ln0_g': 1.0 + nrm((D_MODEL,), 0.02),
        'ln0_b': nrm((D_MODEL,), 0.02),
        'w_in': nrm((DEPTH, D_MODEL, D_IN), D_MODEL ** -0.5),
        'conv_w': nrm((DEPTH, CONV_W, 2 * D_A), CONV_W ** -0.5),
        'conv_b': nrm((DEPTH, 2 * D_A), 0.02),
        'b_i': nrm((DEPTH, H_A), 0.1),
        'b_f': 3.0 + nrm((DEPTH, H_A), 0.5),
        'gn_a_g': 1.0 + nrm((DEPTH, D_A), 0.02),
        'mu_shift': jax.random.uniform(next(ks), (DEPTH, D_B_IN), f32),
        'w0': jax.random.uniform(next(ks), (DEPTH, D_B), f32, minval=-4.0, maxval=0.0),
        'w2': nrm((DEPTH, R_DECAY, D_B), 0.5 * R_DECAY ** -0.5),
        'a0': nrm((DEPTH, D_B), 0.1),
        'a2': nrm((DEPTH, R_AAA, D_B), 0.5 * R_AAA ** -0.5),
        'g2': nrm((DEPTH, R_GATE, D_B), R_GATE ** -0.5),
        'k_k': 1.0 + nrm((DEPTH, D_B), 0.1),
        'k_a': 1.0 + nrm((DEPTH, D_B), 0.1),
        'r_k': nrm((DEPTH, H_B, DH_B), 0.1),
        'lnx_g': 1.0 + nrm((DEPTH, D_B), 0.02),
        'lnx_b': nrm((DEPTH, D_B), 0.02),
        'w_out': nrm((DEPTH, D_MIX, D_MODEL), BETA * D_MIX ** -0.5),
        'ln1_g': 1.0 + nrm((DEPTH, D_MODEL), 0.02),
        'ln1_b': nrm((DEPTH, D_MODEL), 0.02),
        'w_router': nrm((D_MODEL, N_EXPERTS), D_MODEL ** -0.5),
        'b_router': nrm((N_EXPERTS,), 0.01),
        'we_gate': nrm((DEPTH, N_EXPERTS, D_MODEL, D_EXP), D_MODEL ** -0.5),
        'we_up': nrm((DEPTH, N_EXPERTS, D_MODEL, D_EXP), D_MODEL ** -0.5),
        'we_down': nrm((DEPTH, N_EXPERTS, D_EXP, D_MODEL), BETA * D_EXP ** -0.5),
        'ln2_g': 1.0 + nrm((DEPTH, D_MODEL), 0.02),
        'ln2_b': nrm((DEPTH, D_MODEL), 0.02),
    }

def reference(x_prompt, x_sample, state_mlstm_C, state_mlstm_n, state_mlstm_m, state_mlstm_conv,
              state_rwkv_S, state_rwkv_shift, ln0_g, ln0_b, w_in, conv_w, conv_b, b_i, b_f, gn_a_g,
              mu_shift, w0, w2, a0, a2, g2, k_k, k_a, r_k, lnx_g, lnx_b, w_out, ln1_g, ln1_b,
              w_router, b_router, we_gate, we_up, we_down, ln2_g, ln2_b):
    def run(x, states):
        nb = x.shape[0]
        dt = x.dtype
        x = layer_norm(x, ln0_g, ln0_b)
        outs = []
        for l in range(DEPTH):
            if states is None:
                st = (jnp.zeros((nb, H_A, DH_A, DH_A), dt), jnp.zeros((nb, H_A, DH_A), dt),
                      jnp.zeros((nb, H_A), dt), jnp.zeros((nb, CONV_W - 1, 2 * D_A), dt),
                      jnp.zeros((nb, H_B, DH_B, DH_B), dt), jnp.zeros((nb, D_B_IN), dt))
            else:
                st = tuple(s[l] for s in states)
            mix, new_st = mixer_block(x, *st, w_in[l], conv_w[l], conv_b[l], b_i[l], b_f[l], gn_a_g[l],
                                      mu_shift[l], w0[l], w2[l], a0[l], a2[l], g2[l], k_k[l], k_a[l],
                                      r_k[l], lnx_g[l], lnx_b[l], w_out[l])
            x = layer_norm(ALPHA * x + mix, ln1_g[l], ln1_b[l])
            x = layer_norm(ALPHA * x + moe(x, w_router, b_router, we_gate[l], we_up[l], we_down[l]),
                           ln2_g[l], ln2_b[l])
            outs.append(new_st)
        return x, [jnp.stack(s) for s in zip(*outs)]

    y_prompt, (p_C, p_n, p_m, p_conv, p_S, p_shift) = run(x_prompt, None)
    y_sample, (s_C, s_n, s_m, s_conv, s_S, s_shift) = run(
        x_sample, (state_mlstm_C, state_mlstm_n, state_mlstm_m, state_mlstm_conv, state_rwkv_S, state_rwkv_shift))
    return (y_prompt, y_sample, p_C, p_n, p_m, p_conv, p_S, p_shift, s_C, s_n, s_m, s_conv, s_S, s_shift)


_drawn_inputs = setup_inputs


def setup_inputs(seed=0):
    import zlib

    import numpy as np

    out = dict(_drawn_inputs(seed))
    spreads = {}
    factors = {'gn_a_g': 5.922, 'lnx_g': 8.0, 'lnx_b': 16.962, 'ln2_g': 8.645, 'ln2_b': 7.896}
    for name, (base, spread) in spreads.items():
        noise = np.random.default_rng([zlib.crc32(name.encode()), seed]).standard_normal(out[name].shape)
        drawn = base * np.exp(spread * noise) if base else spread * noise
        out[name] = jnp.asarray(drawn.astype(out[name].dtype))
    for name, factor in factors.items():
        out[name] = (out[name] * factor).astype(out[name].dtype)
    return out
```

```python
from contextlib import ExitStack
import math

import numpy as np
import concourse.bass as bass
import concourse.mybir as mybir
from concourse.alu_op_type import AluOpType as ALU

F32 = mybir.dt.float32
ACT = mybir.ActivationFunctionType
AX = mybir.AxisListType

D, SEQ, NB, LS = 1024, 512, 8, 8
NS = NB * LS
N = SEQ + NS
TILES = SEQ // 128 + 1
PT = TILES - 1
KD = D // 128
DA, DB = 512, 512
HA, DHA = 4, 128
HB, DHB = 8, 64
NJ = DB // 128
DA_IN = 4 * DA + 2 * HA
NE, EG, NG, DE = 16, 4, 4, 512
ALPHA = 2 ** 0.25
SQRT_E = math.exp(-0.5)
NEG = -1e30
CW = 4
SCRATCH = {"x_kept": (N, D)}


def rows(i):
    return 128 if i < PT else NS


def cols(i):
    return slice(128 * i, 128 * i + rows(i))


def build(nc, dr, stage=9):
    with ExitStack() as ctx:
        def sem(name):
            return ctx.enter_context(nc.semaphore(name))

        arena = ctx.enter_context(nc.sbuf_tensor("arena", [128, 53200], F32))
        bank = [ctx.enter_context(nc.psum_tensor(f"bank{i}", [128, 512], F32)) for i in range(8)]
        ends = {}

        class Region:
            def __init__(self, at, size):
                self.at, self.end = at, at + size

            def __call__(self, *dims):
                n = int(np.prod(dims))
                ap = arena[:, self.at:self.at + n]
                self.at += n
                assert self.at <= self.end, (self.at, self.end)
                if len(dims) == 2:
                    ap = ap.rearrange("p (a b) -> p a b", a=dims[0])
                if len(dims) == 3:
                    ap = ap.rearrange("p (a b c) -> p a b c", a=dims[0], b=dims[1])
                return ap

        KEEP, T1, T2 = 26500, 13300, 10800
        keep = Region(0, KEEP)
        ident = keep(128)
        blockones = keep(128)
        neg_p = keep(128)
        neg_s = keep(64)
        tri_p = keep(2, 128)
        tri_s = keep(2, 64)
        lvl = keep(7, 128)
        resets = keep(N)
        sel = keep(HA, 128)
        headsel = keep(2)
        seqmask = keep(NB)
        NPRM = 74
        prmc = keep(NPRM)
        shiftc = keep(14, NB)
        convc = keep(8, NB * 3)
        ncol = keep(NB * HA)
        dprm = keep(24)
        gn_a, lnx_g, lnx_b = keep(DA), keep(DB), keep(DB)
        hg = keep(TILES, D)
        arr = keep(NJ, 2, N)
        nbeta = keep(NJ, N)
        kap = keep(NJ, N)
        vtok = keep(TILES, DB)
        sgl = keep(N)
        g2w = keep(DB)
        bon = keep(TILES, HB)
        S = keep(NJ, 128)
        Sh = keep(NJ, 128)
        shnew = keep(NB + 1, 14)
        cvnew = keep(NB + 1, 3, 8)
        nnew = keep(NB + 1, HA)
        rbm = keep(N)
        wint = keep(N)
        woldb = keep(HA, 12)
        colg = keep(3, TILES, HA)
        em = keep(NJ, PT)
        ec = keep(NJ, 12)
        lmid = keep(NJ, PT)
        pend = keep(NJ, PT)
        mrow = keep(12)
        outs = keep(5, 128)
        mv = keep(TILES, 2)
        st6 = keep(2, 6)
        rstd = keep(TILES)
        prow = keep(128)
        ln_g = arena[:, arr_off(arr):arr_off(arr) + D]
        ln_b = arena[:, arr_off(arr) + D:arr_off(arr) + 2 * D]
        x = hg

        t1 = Region(KEEP, T1)
        raw = [t1(604) for _ in range(2)]
        t1_after_raw = t1.at
        wlal = t1(N)
        w2a2 = t1(DB)
        dt = t1(585)
        r_, kr, vr, ld, a_, L, E1, E2, E3, kk, tmp, sq, nrm, kr2 = (t1(N) for _ in range(14))
        g = Region(t1_after_raw + N + DB + 585, T1)
        shrows, cvrows, nrows = g(14, 128), g(8, 128), g(128)
        g = Region(t1_after_raw + N + DB + 585 + 14 * 128, T1)
        LI, LF, bb, mm, d0, d1, wsr, emt, ta_, tb_ = (g(N) for _ in range(10))
        m0r, mprev, blast, mlast, wold = g(8), g(12), g(12), g(12), g(12)
        gbias, gtok, gw = keep(8), keep(TILES, 8), g(8, 8)
        assert g.at <= KEEP + T1

        b = Region(t1_after_raw, T1 - 1208)
        zc, th = b(604), b(604)
        qT, kT = [b(N) for _ in range(2)], [b(N) for _ in range(2)]
        qt = b(N)
        kw, dm, sT = b(TILES, 128), b(TILES, 128), b(TILES, 128)
        C = b(129)
        C0 = b(NB, 129)
        qpad = b(NB, NS)
        vpad = b(NB, 129)
        hh = b(TILES, 129)
        den, rec = b(TILES), b(TILES)
        vext = b(TILES, HA, 129)
        c = Region(KEEP, T1)
        xwm = c.at
        X = [c(4, 128) for _ in range(2)]
        W = [c(4, 128) for _ in range(2)]
        MT = [c(4, 128) for _ in range(2)]
        p = Region(xwm, 3072)
        arpad = p(2, NB, NS)
        kppad = [p(2, NB, 64) for _ in range(2)]
        kpt = [c(2, DB) for _ in range(2)]
        ktmp = c(2, NJ, 128)
        Zs, Us = c(DB), c(DB)
        Sld = c(NJ, NB, 64)
        pS = c(NJ, 64)
        gtk = c(DB)
        ssum, sqs = c(HB), c(HB)
        t2 = Region(KEEP + T1, T2)
        xT = t2(KD, N)
        NW = 6
        wring = t2(NW, KD, 128)
        c = Region(KEEP + T1, T2)
        G = [c(2, HB, 256) for _ in range(2)]
        Y = [c(HB, 128) for _ in range(2)]
        SsT = Region(arr_off(G[1]), 4096)(NJ, NB, 128)
        o = Region(KEEP, T1)
        xln = o(TILES, D)
        l1g, l1b, l2g, l2b = o(D), o(D), o(D), o(D)
        wrt = o(KD, NE)
        hT = xT
        wout = arena[:, arr_off(arr):arr_off(arr) + KD * D].rearrange("p (a b) -> p a b", a=KD)
        x1T = Region(arr_off(hg), TILES * D)(KD, N)
        e = Region(o.at, KEEP + T1 - o.at)
        hs, hid = e(N), e(DE // 128, N)
        probs, sl, gate = e(TILES, NE), e(TILES, NE), e(TILES, NE)
        gmax, gsum, t80a, t80b, brr = e(TILES, NG), e(TILES, NG), e(TILES, NE), e(TILES, NE), e(NE)
        one5 = e(TILES)
        gtop = e(TILES, NG)
        NF = DE // 128
        wexp = []
        for at in (arr_off(arr), KEEP + T1):
            w = Region(at, 12288)
            wexp.append((w(KD, DE), w(KD, DE), w(DE // 128, D)))

        class Sems(dict):
            def __missing__(self, name):
                self[name] = ctx.enter_context(nc.semaphore(name))
                return self[name]

        q_ = Sems()
        x_loaded = [q_[f"x_loaded{i}"] for i in range(TILES)]
        w_loaded = [q_[f"w_loaded{i}"] for i in range(NW)]
        wexp_loaded = [q_[f"wexp_loaded{i}"] for i in range(2)]
        block = ctx.enter_context(nc.Block())

        def wcol(n):
            if n < 2:
                return DA_IN + 3 * DB + 128 * n
            if n < 14:
                return DA_IN + DB * ((n - 2) % 3) + 128 * ((n - 2) // 3)
            if n < 22:
                return 2 * DA + 128 * (n - 14)
            return DA * ((n - 22) % 2) + 128 * ((n - 22) // 2)

        def shift_tile(n):
            return 12 + n if n < 2 else 4 * ((n - 2) % 3) + (n - 2) // 3

        SLOTS = 30

        def LV(i):
            return 7 if i < PT else 3

        def ix(i, l, q):
            return 14 * i + 2 * l + q

        def ix2(i, l, q):
            return 12 * i + 2 * (l - 1) + q

        def hooks(i, l):
            return ("Z", "U", "O", "G")[l - (1 if i < PT else 0)] if i and 0 <= l - (1 if i < PT else 0) < 4 else None
        MU, CWR, CBR, KKR, KAR, W0R, A0R, RKR = 0, 14, 46, 54, 58, 62, 66, 70
        HW0, HA0, OMKA = 0, 4, 8
        UNITS = PT + 1

        def P(n):
            return prmc[:, n:n + 1]

        def pr(ap):
            return ap[:, 0:SEQ].rearrange("p (c t) -> p c t", c=PT)

        def sa(ap):
            return ap[:, SEQ:N].rearrange("p (b t) -> p b t", b=NB)

        def wide(ap, n):
            return ap.unsqueeze(2).to_broadcast([ap.shape[0], ap.shape[1], n])

        @block.sync
        def _(sp):
            for k, (name, at) in enumerate((("mu_shift", MU), ("conv_w", CWR), ("conv_b", CBR), ("k_k", KKR),
                                            ("k_a", KAR), ("w0", W0R), ("a0", A0R), ("r_k", RKR))):
                src = dr[name]
                n = int(np.prod(src.shape)) // 128
                sp.dma_start(prow[at:at + n, :], flat(src, n)).then_inc(q_["prm_loaded"], 16)
            for i in range(TILES):
                src = dr["x_prompt"][0, 128 * i:128 * i + 128, :] if i < PT else dr["x_sample"].rearrange("b t d -> (b t) d")
                sp.dma_start(x[0:rows(i), i, :], src).then_inc(x_loaded[i], 16)
                if i == 0:
                    for ap, name in ((ln_g, "ln0_g"), (ln_b, "ln0_b")):
                        sp.dma_start(ap, brow(dr[name], D)).then_inc(q_["ln0_loaded"], 16)
            sp.dma_start(shrows[0:NB, :, :], dr["state_rwkv_shift"][0].rearrange("b (a f) -> b a f", f=128)).then_inc(q_["hist_loaded"], 16)
            sp.dma_start(cvrows[0:24, :, :], dr["state_mlstm_conv"][0].rearrange("b w (a f) -> (b w) a f", f=128)).then_inc(q_["hist_loaded"], 16)
            sp.dma_start(nrows[0:NB * HA, :], dr["state_mlstm_n"][0].rearrange("b h d -> (b h) d")).then_inc(q_["hist_loaded"], 16)
            sp.dma_start(gw, dr["w_in"][0, :, 4 * DA:DA_IN].rearrange("(k p) c -> p k c", p=128)).then_inc(q_["gate_loaded"], 16)
            sp.dma_start(gbias[:, 0:HA], brow(dr["b_i"][0], HA)).then_inc(q_["gate_loaded"], 16)
            sp.dma_start(gbias[:, HA:8], brow(dr["b_f"][0], HA)).then_inc(q_["gate_loaded"], 16)
            sp.dma_start(m0r[0:HA, :], dr["state_mlstm_m"][0].rearrange("b h -> h b"), allow_slow_non_contiguous=True).then_inc(q_["gate_loaded"], 16)
            for n in range(SLOTS):
                if n >= NW:
                    sp.wait_ge(q_["slot_projected"], n - NW + 1)
                c = wcol(n)
                sp.dma_start(wring[:, n % NW, :, :], dr["w_in"][0, :, c:c + 128].rearrange("(k p) c -> p k c", p=128)).then_inc(w_loaded[n % NW], 16)
                if n == 5:
                    sp.wait_ge(q_["ln0_done"], TILES)
                    for i in range(TILES):
                        sp.dma_start(dr["x_kept"][128 * i:128 * i + rows(i), :], x[0:rows(i), i, :]).then_inc(q_["x_kept"], 16)
                if n == 1:
                    sp.dma_start(w2a2[0:64, :], dr["w2"][0]).then_inc(q_["lora_loaded"], 16)
                    sp.dma_start(w2a2[64:128, :], dr["a2"][0]).then_inc(q_["lora_loaded"], 16)
                    sp.dma_start(g2w, dr["g2"][0]).then_inc(q_["lora_loaded"], 16)
                    for ap, name, w in ((gn_a, "gn_a_g", DA), (lnx_g, "lnx_g", DB), (lnx_b, "lnx_b", DB)):
                        sp.dma_start(ap, brow(dr[name][0], w)).then_inc(q_["gn_loaded"], 16)

            stored = 0

            def store(dst, src, **kw):
                nonlocal stored
                stored += 1
                sp.dma_start(dst, src, **kw).then_inc(q_["stored"], 16)

            sp.wait_ge(q_["outs_ready"], 1)
            store(dr["s_shift"][0].rearrange("b (t f) -> (b t) f", f=128), outs[0:112, 0, :])
            store(dr["p_shift"][0].rearrange("b (t f) -> (b t) f", f=128), outs[112:126, 0, :])
            sc = dr["s_conv"][0].rearrange("b w (c f) -> (b w c) f", f=128)
            store(sc[0:96], outs[0:96, 1, :])
            store(sc[96:192], outs[0:96, 2, :])
            store(dr["p_conv"][0, 0].rearrange("w (c f) -> (w c) f", f=128), outs[0:24, 3, :])
            store(dr["s_n"][0].rearrange("b h d -> (b h) d"), outs[0:32, 4, :])
            store(dr["p_n"][0, 0], outs[32:36, 4, :])
            store(dr["p_m"][0].rearrange("b h -> h b"), mrow[0:HA, 3:4], allow_slow_non_contiguous=True)
            store(dr["s_m"][0].rearrange("b h -> h b"), mrow[0:HA, 4:12], allow_slow_non_contiguous=True)
            sp.wait_ge(q_["ktmp_made"], 1)
            sp.wait_ge(q_["unit_projected"], HA)
            sp.wait_ge(q_["ha_done"], HA)
            for h in range(HB):
                sp.dma_start(Sld[64 * (h % 2):64 * (h % 2) + 64, h // 2, :, :], dr["state_rwkv_S"][0, :, h].rearrange("b v k -> v b k")).then_inc(q_["sst_loaded"], 16)
            sp.wait_ge(q_["pads_made"], NJ)
            sp.wait_ge(q_["grams"], 4 * TILES)
            sp.wait_ge(q_["ktmp_made"], TILES)
            sp.dma_start(wout, dr["w_out"][0].rearrange("(k p) c -> p k c", p=128)).then_inc(q_["wout_loaded"], 16)
            sp.wait_ge(q_["ps_ready"], 1)
            store(dr["p_S"][0, 0].rearrange("(j h) v k -> (h v) j k", h=2), pS)
            for h in range(HB):
                sp.wait_ge(q_["ss_read"], h + 1)
                store(dr["s_S"][0, :, h].rearrange("b v k -> v b k"), Sld[64 * (h % 2):64 * (h % 2) + 64, h // 2, :, :])
            sp.wait_ge(q_["stored"], 16 * stored)
            sp.wait_ge(q_["hb_done"], TILES)
            sp.wait_ge(q_["x_kept"], 16 * TILES)
            for i in range(TILES):
                sp.dma_start(xln[0:rows(i), i, :], dr["x_kept"][128 * i:128 * i + rows(i), :]).then_inc(q_["x_back"], 16)
            for ap, src, w in ((l1g, dr["ln1_g"][0], D), (l1b, dr["ln1_b"][0], D), (l2g, dr["ln2_g"][0], D), (l2b, dr["ln2_b"][0], D), (brr, dr["b_router"], NE)):
                sp.dma_start(ap, brow(src, w)).then_inc(q_["ln_loaded"], 16)
            sp.dma_start(wrt, dr["w_router"].rearrange("(k p) c -> p k c", p=128)).then_inc(q_["ln_loaded"], 16)
            sp.wait_ge(q_["mix_projected"], TILES)
            for e_ in range(NE):
                if e_ >= 2:
                    sp.wait_ge(q_["down"], TILES * (e_ - 1))
                wg, wu, wd = wexp[e_ % 2]
                for w, name in ((wg, "we_gate"), (wu, "we_up"), (wd, "we_down")):
                    sp.dma_start(w, dr[name][0, e_].rearrange("(k p) c -> p k c", p=128)).then_inc(wexp_loaded[e_ % 2], 16)
            for i in range(TILES):
                sp.wait_ge(q_["y_ready"], i + 1)
                dst = dr["y_prompt"][0, 128 * i:128 * i + 128, :] if i < PT else dr["y_sample"].rearrange("b t d -> (b t) d")
                store(dst, xln[0:rows(i), i, :])
            sp.wait_ge(q_["stored"], 16 * stored)
            sp.wait_ge(q_["cs_stored"], 32 * HA)

        @block.gpsimd
        def _(pool):
            step = [0]

            def link(ins):
                step[0] += 1
                ins.then_inc(q_["pool_step"], 1)
                pool.wait_ge(q_["pool_step"], step[0])

            def keep_where(ap, pattern, base, cm, op=ALU.is_ge, fill=0.0):
                link(pool.affine_select(out=ap, in_=ap, pattern=pattern, compare_op=op, fill=fill, base=base,
                                        channel_multiplier=cm))

            link(pool.memset(ident, 0.0))
            keep_where(ident, [[-1, 128]], 0, 1, ALU.not_equal, 1.0)
            pool.nop().then_inc(q_["ident_ready"], 1)
            for ap in (raw[0], raw[1]):
                link(pool.memset(ap, 0.0))
            link(pool.memset(resets, 1.0))
            link(pool.memset(resets[:, 0:SEQ:128], 0.0))
            link(pool.memset(resets[:, SEQ:N:LS], 0.0))
            link(pool.memset(sel[0:HA], 0.0))
            keep_where(sel[0:HA], [[-1, HA], [0, 128]], 0, 1, ALU.not_equal, 1.0)
            bo = blockones.rearrange("p (a b) -> p a b", a=2)
            link(pool.memset(blockones, 1.0))
            keep_where(bo, [[-64, 2], [0, 64]], 0, 1)
            keep_where(bo, [[64, 2], [0, 64]], 63, -1)
            link(pool.memset(headsel, 1.0))
            keep_where(headsel, [[-64, 2]], 0, 1)
            keep_where(headsel, [[64, 2]], 63, -1)
            link(pool.memset(seqmask, 1.0))
            keep_where(seqmask, [[-LS, NB]], 0, 1)
            keep_where(seqmask, [[LS, NB]], LS - 1, -1)
            link(pool.memset(neg_p, 0.0))
            keep_where(neg_p, [[1, 128]], 0, -1, fill=NEG)
            link(pool.memset(neg_s, 0.0))
            keep_where(neg_s, [[1, NS]], 0, -1, fill=NEG)
            keep_where(neg_s.rearrange("p (b t) -> p b t", b=NB), [[-LS, NB], [0, LS]], 0, 1, fill=NEG)
            keep_where(neg_s.rearrange("p (b t) -> p b t", b=NB), [[LS, NB], [0, LS]], LS - 1, -1, fill=NEG)
            link(pool.memset(tri_p, 1.0))
            link(pool.memset(tri_s, 1.0))
            for tri, n in ((tri_p, 128), (tri_s, NS)):
                keep_where(tri[:, 0, :], [[1, n]], 0, -1, ALU.is_gt)
                keep_where(tri[:, 1, :], [[1, n]], 0, -1)
            for v in range(2):
                ts = tri_s[:, v, :].rearrange("p (b t) -> p b t", b=NB)
                keep_where(ts, [[-LS, NB], [0, LS]], 0, 1)
                keep_where(ts, [[LS, NB], [0, LS]], LS - 1, -1)
            link(pool.memset(lvl, 0.0))
            for l in range(7):
                m = 2 ** l
                up = lvl[:, l, :].rearrange("p (a c b) -> p a c b", c=2, b=m)[:, :, 1, :]
                link(pool.memset(up, 1.0))
                keep_where(up, [[-2 * m, 64 // m], [0, m]], 0, 1)
                keep_where(up, [[2 * m, 64 // m], [0, m]], m - 1, -1)
            pool.nop().then_inc(q_["masks_ready"], 1)

            def collect(n, k):
                pool.wait_ge(q_["slot_read"], n + 1)
                rw = raw[k % 2]
                if n < 14:
                    t = shift_tile(n)
                    pool.tensor_copy(shnew[:, NB, t:t + 1], rw[:, SEQ:SEQ + 1])
                    pool.tensor_copy(shnew[:, 0:NB, t], rw[:, 513:585].rearrange("p (b t) -> p b t", b=NB)[:, :, LS]).then_inc(q_["raw_collected"], 1)
                else:
                    c = 4 * ((n - 22) % 2) + (n - 22) // 2
                    pool.tensor_copy(cvnew[:, NB, :, c], rw[:, SEQ:SEQ + 3])
                    pool.tensor_copy(cvnew[:, 0:NB, :, c], rw[:, 515:603].rearrange("p (b t) -> p b t", b=NB)[:, :, LS:LS + 3]).then_inc(q_["raw_collected"], 1)

            def mlstm_io(h):
                pool.wait_ge(q_["cs_new"], h + 1)
                pool.dma_start(dr["s_C"][0, :, h].rearrange("b d e -> d b e"), C0[:, :, 0:128]).then_inc(q_["cs_stored"], 16)
                pool.wait_ge(q_["c_state"], PT * (h + 1))
                pool.dma_start(dr["p_C"][0, 0, h], C[:, 0:128]).then_inc(q_["cs_stored"], 16)
                if h < HA - 1:
                    pool.wait_ge(q_["cs_stored"], 32 * (h + 1))
                    pool.dma_start(C0[:, :, 0:128], dr["state_mlstm_C"][0, :, h + 1].rearrange("b d e -> d b e")).then_inc(q_["c0_loaded"], 16)

            for n in range(14):
                collect(n, n)
            pool.wait_ge(q_["rwkv_made"], NJ)
            pool.wait_ge(q_["post_projected"], NJ)
            pool.dma_start(C0[:, :, 0:128], dr["state_mlstm_C"][0, :, 0].rearrange("b d e -> d b e")).then_inc(q_["c0_loaded"], 16)
            pool.memset(vext[:, :, :, 128:129], 1.0).then_inc(q_["ones_set"], 1)
            pool.memset(qpad, 0.0).then_inc(q_["ones_set"], 1)
            collect(22, 14)
            collect(23, 15)
            for h in range(HA):
                if h < HA - 1:
                    collect(24 + 2 * h, 16 + 2 * h)
                    collect(25 + 2 * h, 17 + 2 * h)
                mlstm_io(h)


            pool.wait_ge(q_["ec_ready"], 1)
            pool.wait_ge(q_["unit_projected"], HA)
            pool.wait_ge(q_["ha_done"], HA)
            pool.wait_ge(q_["cs_stored"], 32 * HA)
            for i in range(TILES):
                n = rows(i)
                if i:
                    pool.wait_ge(q_["kt_turned"], i)
                for w, src in enumerate((nbeta, kap)):
                    if i < PT:
                        ins = pool.tensor_tensor(ktmp[:, w, :, :], src[:, :, cols(i)], wide(ec[:, :, i], 128), ALU.mult)
                    else:
                        for j in range(NJ):
                            ins = pool.tensor_tensor(ktmp[:, w, j, 0:NS].rearrange("p (b t) -> p b t", b=NB), sa(src[:, j, :]), wide(ec[:, j, 4:12], LS), ALU.mult)
                ins.then_inc(q_["ktmp_made"], 1)
                for l in range(LV(i)):
                    for q in range(2):
                        k = ix(i, l, q)
                        if l == 0:
                            pool.wait_ge(q_["gram_read"], 4 * i + 2 * q + 1)
                        if k >= 2:
                            pool.wait_ge(q_["w_projected"], k - 1)
                        if l == 1:
                            pool.wait_ge(q_["yx_read"], k - 1)
                        pool.tensor_tensor(MT[q][0:n, :, 0:n], G[i % 2][0:n, 0, 4 * q:4 * q + 4, 0:n],
                                           lvl[0:n, l, 0:n].unsqueeze(1).to_broadcast([n, 4, n]), ALU.mult).then_inc(q_["mt_ready"], 1)
            pool.wait_ge(q_["o_projected"], PT)
            link(pool.memset(SsT, 0.0))
            pool.wait_ge(q_["yx_read"], ix(PT, 2, 1) + 1)
            pool.wait_ge(q_["w_projected"], ix(PT, 2, 1) + 1)
            pool.wait_ge(q_["yx_projected"], ix2(PT, 2, 1) + 1)
            link(pool.memset(arpad, 0.0))
            pool.nop().then_inc(q_["sst_zero"], 1)
            for h in range(HB):
                if h == 0:
                    pool.wait_ge(q_["kt_read"], TILES)
                if h >= 2:
                    pool.wait_ge(q_["ss_projected"], h - 1)
                for w in range(2):
                    ins = pool.tensor_tensor(kppad[h % 2][0:NS, w], kpt[PT % 2][0:NS, w, 64 * h:64 * h + 64].unsqueeze(1).to_broadcast([NS, NB, 64]),
                                             seqmask[0:NS].unsqueeze(2).to_broadcast([NS, NB, 64]), ALU.mult)
                ins.then_inc(q_["kp_spread"], 1)

        @block.scalar
        def _(act):
            step = [0]

            def link(ins):
                step[0] += 1
                ins.then_inc(q_["act_step"], 1)
                act.wait_ge(q_["act_step"], step[0])

            act.wait_ge(q_["x_moments"], 1)
            act.activation(rstd, mv[:, :, 1], ACT.Sqrt).then_inc(q_["x_std"], 1)
            for i in range(TILES):
                act.wait_ge(q_["x_turned"], i + 1)
                for q in range(2):
                    v = bank[2 * (i % 2) + q].rearrange("p (a b) -> p a b", a=4)[:, :, 0:rows(i)]
                    ins = act.copy(xT[:, 4 * q:4 * q + 4, cols(i)], v)
                ins.then_inc(q_["xt_ready"], 1)

            def to_raw(n, k):
                act.wait_ge(q_["slot_projected"], n + 1)
                if k >= 2:
                    act.wait_ge(q_["raw_used"], k - 1)
                    act.wait_ge(q_["raw_collected"], k - 1)
                elif k == 0:
                    act.wait_ge(q_["masks_ready"], 1)
                    act.wait_ge(q_["cols_ready"], 1)
                rw, A, B = raw[k % 2], bank[2 * (n % 2)], bank[2 * (n % 2) + 1]
                if n < 14:
                    sv = rw[:, 513:585].rearrange("p (b t) -> p b t", b=NB)
                    act.copy(sv[:, :, 0], shiftc[:, shift_tile(n), :])
                    act.copy(rw[:, 1:513], A[:, :])
                    act.copy(sv[:, :, 1:9], B[:, 0:NS].rearrange("p (b t) -> p b t", b=NB)).then_inc(q_["slot_read"], 1)
                else:
                    sv = rw[:, 515:603].rearrange("p (b t) -> p b t", b=NB)
                    c = 4 * ((n - 22) % 2) + (n - 22) // 2
                    if k < 16:
                        act.copy(rw[:, 0:3], resets[:, 0:SEQ:128][:, 0:3])
                    act.copy(sv[:, :, 0:3], convc[:, c, :].rearrange("p (b w) -> p b w", b=NB))
                    act.copy(rw[:, 3:515], A[:, :])
                    act.copy(sv[:, :, 3:11], B[:, 0:NS].rearrange("p (b t) -> p b t", b=NB)).then_inc(q_["slot_read"], 1)

            to_raw(0, 0)
            act.wait_ge(q_["gate_abs"], 1)
            act.activation(ta_[0:HA, :], ta_[0:HA, :], ACT.Exp).then_inc(q_["gate_exp"], 1)
            act.wait_ge(q_["gate_one"], 1)
            act.activation(tb_[0:HA, :], ta_[0:HA, :], ACT.Ln).then_inc(q_["gate_ln"], 1)
            to_raw(1, 1)
            act.wait_ge(q_["gate_args"], 1)
            act.activation(wint[0:HA, :], wint[0:HA, :], ACT.Exp)
            act.activation(wsr[0:HA, :], wsr[0:HA, :], ACT.Exp)
            act.activation(emt[0:HA, :], mm[0:HA, :], ACT.Exp, scale=-1.0)
            act.activation(wold[0:HA, :], wold[0:HA, :], ACT.Exp).then_inc(q_["gate_rows"], 1)
            act.wait_ge(q_["cols_turned"], 1)
            for a in range(3):
                act.copy(colg[:, a, 0:PT, :], bank[5][:, 20 * a:20 * a + 16].rearrange("p (i h) -> p i h", h=HA))
                act.copy(colg[0:NS, a, PT, :], bank[5][0:NS, 20 * a + 16:20 * a + 20])
            act.copy(woldb, bank[5][:, 64:112].rearrange("p (h c) -> p h c", h=HA)).then_inc(q_["gate_cols"], 1)
            act.wait_ge(q_["shifted"], 2)
            act.activation(wlal[0:64, :], wlal[0:64, :], ACT.Tanh)
            act.activation(sgl, sgl, ACT.Tanh, scale=0.5).then_inc(q_["lora_in"], 1)

            def exps(j):
                act.wait_ge(q_["decay_args"], j + 1)
                act.activation(E1, tmp, ACT.Exp)
                act.activation(E2, L, ACT.Exp)
                act.activation(E3, L, ACT.Exp, scale=-1.0)
                act.activation(em[:, j, :], lmid[:, j, :], ACT.Exp).then_inc(q_["decays"], 1)

            def post(j):
                act.wait_ge(q_["post_projected"], j + 1)
                act.copy(bon[:, 0:PT, 2 * j:2 * j + 2], bank[7][:, 0:8].rearrange("p (i h) -> p i h", h=2))
                act.copy(bon[0:NS, PT, 2 * j:2 * j + 2], bank[7][0:NS, 8:10])
                act.copy(vtok[:, 0:PT, 128 * j:128 * j + 128], bank[6].rearrange("p (i f) -> p i f", i=PT))
                act.copy(vtok[0:NS, PT, 128 * j:128 * j + 128], bank[7][0:NS, 128:256]).then_inc(q_["post_read"], 1)

            for j in range(NJ):
                to_raw(2 + 3 * j, 2 + 3 * j)
                to_raw(3 + 3 * j, 3 + 3 * j)
                if j:
                    post(j - 1)
                act.wait_ge(q_["lora_projected"], j + 1)
                if j:
                    act.wait_ge(q_["rwkv_made"], j)
                for dst, A, B, hb in ((ld, bank[4], bank[5][:, 0:NS], HW0), (a_, bank[6], bank[7][:, 256:256 + NS], HA0)):
                    act.activation(dst[:, 0:SEQ], A[:, :], ACT.Tanh, bias=dprm[:, hb + j:hb + j + 1], scale=0.5)
                    ins = act.activation(dst[:, SEQ:N], B, ACT.Tanh, bias=dprm[:, hb + j:hb + j + 1], scale=0.5)
                ins.then_inc(q_["tanhs"], 1)
                to_raw(4 + 3 * j, 4 + 3 * j)
                exps(j)
                act.wait_ge(q_["norms_projected"], j + 1)
                act.activation(nrm[:, 0:SEQ], bank[4][:, :], ACT.Sqrt)
                act.activation(nrm[:, SEQ:N], bank[5][:, 0:NS], ACT.Sqrt).then_inc(q_["norms"], 1)
            act.wait_ge(q_["rwkv_made"], NJ)
            for n in range(14, 22):
                act.wait_ge(q_["slot_projected"], n + 1)
                h = (n - 14) % 4
                A, B = bank[2 * (n % 2)].rearrange("p (i f) -> p i f", i=PT), bank[2 * (n % 2) + 1][0:NS, 0:128]
                if n < 18:
                    act.copy(vext[:, 0:PT, h, 0:128], A)
                    act.copy(vext[0:NS, PT, h, 0:128], B).then_inc(q_["slot_read"], 1)
                else:
                    act.activation(hg[:, 0:PT, 128 * h:128 * h + 128], A, ACT.Tanh, scale=0.5)
                    act.activation(hg[0:NS, PT, 128 * h:128 * h + 128], B, ACT.Tanh, scale=0.5).then_inc(q_["slot_read"], 1)
                if n == 14:
                    post(NJ - 1)

            def silu_tanh(k):
                act.wait_ge(q_["raw_used"], 15 + k)
                act.activation(th, zc, ACT.Tanh, scale=0.5).then_inc(q_["silu_tanh"], 1)

            def unit(h):
                act.wait_ge(q_["k_turned"], h + 1)
                if h:
                    act.wait_ge(q_["unit_projected"], h)
                for i in range(TILES):
                    n = rows(i)
                    src = bank[6][:, 128 * i:128 * i + 128] if i < PT else bank[7][0:NS, 0:128]
                    ins = act.activation(kw[0:n, i, :], src, ACT.Copy, scale=colg[0:n, 1, i, h:h + 1])
                ins.then_inc(q_["k_tokens"], 1)
                act.wait_ge(q_["scores"], h + 1)
                for i in range(TILES):
                    n = rows(i)
                    src = bank[6][:, 128 * i:128 * i + 128] if i < PT else bank[7][0:NS, 128:192]
                    ins = act.activation(dm[0:n, i, 0:n], src, ACT.Exp, bias=colg[0:n, 0, i, h:h + 1])
                ins.then_inc(q_["weights"], 1)
                for i in range(TILES):
                    act.wait_ge(q_["numerator"], TILES * h + i + 1)
                    if h and i == 0:
                        act.wait_ge(q_["ha_done"], h)
                    act.copy(hh[0:rows(i), i, :], bank[4 + i % 2][0:rows(i), 128:257]).then_inc(q_["num_read"], 1)
                act.wait_ge(q_["ha_moments"], h + 1)
                act.activation(rstd, mv[:, :, 1], ACT.Sqrt).then_inc(q_["ha_std"], 1)

            for h in range(HA):
                for p_ in range(2):
                    n, k = 22 + 2 * h + p_, 14 + 2 * h + p_
                    to_raw(n, k)
                    silu_tanh(2 * h + p_)
                if h:
                    unit(h - 1)
            unit(HA - 1)


            act.wait_ge(q_["rwkv_made"], NJ)
            act.activation(ec, ec, ACT.Exp).then_inc(q_["ec_ready"], 1)

            def recur(i, what):
                if what is None:
                    return
                n = rows(i)
                if what == "Z":
                    act.wait_ge(q_["z_projected"], i + 1)
                    act.copy(Zs[0:n], bank[6][0:n, :]).then_inc(q_["z_read"], 1)
                if what == "O":
                    act.wait_ge(q_["o_projected"], i + 1)
                    act.copy(hg[0:n, i, DA:D], bank[6 if i < PT else 4][0:n, :]).then_inc(q_["o_read"], 1)
                if what == "G":
                    act.wait_ge(q_["hb_moments"], i + 1)
                    act.activation(sqs[0:n], sqs[0:n], ACT.Sqrt, scale=1.0 / DHB).then_inc(q_["hb_std"], 1)

            for i in range(TILES):
                act.wait_ge(q_["kt_turned"], i + 1)
                n = rows(i)
                if i >= 2:
                    act.wait_ge(q_["s_projected"], i - 1)
                for w in range(2):
                    ins = act.copy(kpt[i % 2][0:n, w, :], bank[2 + w][0:n, :])
                ins.then_inc(q_["kt_read"], 1)
                for l in range(LV(i)):
                    for q in range(2):
                        act.wait_ge(q_["w_projected"], ix(i, l, q) + 1)
                        act.copy(W[q][0:n, :, 0:n], bank[q][0:n, :].rearrange("p (h t) -> p h t", h=4)[:, :, 0:n]).then_inc(q_["w_read"], 1)
                    recur(i - 1, hooks(i, l))
            recur(PT - 1, "G")
            for j in range(NJ):
                act.wait_ge(q_["st_turned"], j + 1)
                act.wait_ge(q_["sst_zero"], 1)
                act.copy(SsT[0:64, j, :, 0:64], bank[2 * (j % 2)][0:64, :].rearrange("p (b v) -> p b v", b=NB))
                act.copy(SsT[64:128, j, :, 64:128], bank[2 * (j % 2) + 1][64:128, :].rearrange("p (b v) -> p b v", b=NB)).then_inc(q_["st_read"], 1)
            recur(PT, "Z")
            recur(PT, "O")
            recur(PT, "G")


            for i in range(TILES):
                n = rows(i)
                act.wait_ge(q_["h_turned"], i + 1)
                if i == 0:
                    act.wait_ge(q_["ss_projected"], HB)
                for q in range(2):
                    v = bank[4 + 2 * (i % 2) + q].rearrange("p (a b) -> p a b", a=4)[:, :, 0:n]
                    ins = act.copy(hT[:, 4 * q:4 * q + 4, cols(i)], v)
                ins.then_inc(q_["ht_ready"], 1)

            def row_std(stat, n):
                act.wait_ge(q_["ln_moments"], stat)
                act.activation(rstd[0:n, 0:1], mv[0:n, 0, 1:2], ACT.Sqrt).then_inc(q_["ln_std"], 1)

            for i in range(TILES):
                row_std(i + 1, rows(i))
            for i in range(TILES):
                n = rows(i)
                act.wait_ge(q_["x1_in_psum"], i + 1)
                for q in range(2):
                    v = bank[4 + 2 * (i % 2) + q].rearrange("p (a b) -> p a b", a=4)[:, :, 0:n]
                    ins = act.copy(x1T[:, 4 * q:4 * q + 4, cols(i)], v)
                ins.then_inc(q_["x1_turned"], 1)
            act.wait_ge(q_["logits_shifted"], 1)
            act.activation(probs, probs, ACT.Exp).then_inc(q_["probs_exp"], 1)
            for k in range(NE * NF):
                act.wait_ge(q_["hidden"], k + 1)
                if k:
                    act.wait_ge(q_["hid_ready"], k)
                act.activation(hs[:, 0:SEQ], bank[0][:, :], ACT.Silu)
                act.activation(hs[:, SEQ:N], bank[1][:, 0:NS], ACT.Silu).then_inc(q_["hid_silu"], 1)
            for i in range(TILES):
                row_std(TILES + i + 1, rows(i))
        @block.vector
        def _(dve):
            step = [0]

            def link(ins):
                step[0] += 1
                ins.then_inc(q_["dve_step"], 1)
                dve.wait_ge(q_["dve_step"], step[0])

            link(dve.memset(mv, 1.0))
            link(dve.memset(colg, 1.0))
            dve.memset(hg[64:128, PT, :], 0.0)
            st2 = st6
            for i in range(TILES):
                dve.wait_ge(x_loaded[i], 16)
                n = rows(i)
                for q in range(2):
                    ins = dve.bn_stats(out=st2[0:n, q, :], in_=x[0:n, i, 512 * q:512 * q + 512])
                link(ins)
                link(dve.bn_aggr(out=mv[0:n, i, :], in_=st2[0:n]))
            link(dve.tensor_scalar(mv[:, :, 1], mv[:, :, 1], 1e-5, None, ALU.add))
            dve.nop().then_inc(q_["x_moments"], 1)
            dve.wait_ge(q_["x_std"], 1)
            link(dve.reciprocal(rstd, rstd))
            dve.wait_ge(q_["ln0_loaded"], 32)
            for i in range(TILES):
                n = rows(i)
                xi = x[0:n, i, :]
                link(dve.tensor_scalar(xi, xi, mv[0:n, i, 0:1], rstd[0:n, i:i + 1], ALU.subtract, ALU.mult))
                link(dve.tensor_tensor(xi, xi, ln_g[0:n], ALU.mult))
                dve.tensor_tensor(xi, xi, ln_b[0:n], ALU.add).then_inc(q_["ln0_done"], 1)
            dve.wait_ge(q_["prm_turned"], 1)
            dve.tensor_copy(prmc, bank[4][:, 0:NPRM])
            dve.tensor_copy(shiftc, bank[4][:, 74:186].rearrange("p (a b) -> p a b", a=14))
            dve.tensor_copy(convc, bank[4][:, 186:378].rearrange("p (a b) -> p a b", a=8))
            dve.tensor_copy(ncol, bank[4][:, 378:410]).then_inc(q_["cols_ready"], 1)
            dve.wait_ge(q_["cols_ready"], 1)
            dve.tensor_scalar(dprm[:, HW0:HW0 + 4], prmc[:, W0R:W0R + 4], 0.5, None, ALU.mult)
            dve.tensor_scalar(dprm[:, HA0:HA0 + 4], prmc[:, A0R:A0R + 4], 0.5, None, ALU.mult)
            link(dve.tensor_scalar(dprm[:, OMKA:OMKA + 4], prmc[:, KAR:KAR + 4], -1.0, 1.0, ALU.mult, ALU.add))

            def shift(n, dst):
                dve.wait_ge(q_["slot_read"], n + 1)
                rw, m = raw[n % 2], P(MU + shift_tile(n))
                rs = rw[:, 513:585].rearrange("p (b t) -> p b t", b=NB)
                link(dve.tensor_tensor(dt[:, 0:584], rw[:, 0:584], rw[:, 1:585], ALU.subtract))
                ds = dt[:, 513:585].rearrange("p (b t) -> p b t", b=NB)
                dve.scalar_tensor_tensor(out=dst[:, 0:SEQ], in0=dt[:, 0:SEQ], scalar=m, in1=rw[:, 1:513], op0=ALU.mult, op1=ALU.add)
                dve.scalar_tensor_tensor(out=sa(dst), in0=ds[:, :, 0:LS], scalar=m, in1=rs[:, :, 1:9], op0=ALU.mult, op1=ALU.add).then_inc(q_["raw_used"], 1)
                dve.wait_ge(q_["raw_used"], n + 1)

            def gate_rows():
                R = slice(0, HA)
                dve.wait_ge(q_["gates_projected"], 1)
                dve.wait_ge(q_["gate_loaded"], 64)
                gv = bank[7][:, 0:40].rearrange("p (i c) -> p i c", i=TILES)
                dve.tensor_tensor(gtok[:, 0:PT, :], gv[:, 0:PT, :], gbias.unsqueeze(1).to_broadcast([128, PT, 8]), ALU.add)
                dve.tensor_tensor(gtok[0:NS, PT, :], gv[0:NS, PT, :], gbias[0:NS], ALU.add).then_inc(q_["gate_tokens"], 1)
                dve.wait_ge(q_["gates_turned"], 1)
                dve.tensor_copy(LI[R, 0:SEQ], bank[4][R, :])
                dve.tensor_copy(LI[R, SEQ:N], bank[5][R, 0:NS])
                dve.tensor_copy(LF[R, 0:SEQ], bank[6][R, :])
                dve.tensor_copy(LF[R, SEQ:N], bank[5][R, NS:2 * NS]).then_inc(q_["gate_rows_read"], 1)
                dve.wait_ge(q_["gate_rows_read"], 1)
                dve.scalar_tensor_tensor(out=ta_[R], in0=LF[R], scalar=-1.0, in1=LF[R], op0=ALU.mult, op1=ALU.min).then_inc(q_["gate_abs"], 1)
                dve.wait_ge(q_["gate_exp"], 1)
                dve.tensor_scalar(ta_[R], ta_[R], 1.0, None, ALU.add).then_inc(q_["gate_one"], 1)
                dve.wait_ge(q_["gate_ln"], 1)
                link(dve.scalar_tensor_tensor(out=LF[R], in0=LF[R], scalar=0.0, in1=tb_[R], op0=ALU.min, op1=ALU.subtract))
                dve.wait_ge(q_["masks_ready"], 1)
                dve.tensor_tensor_scan(bb[R], resets[R], LF[R], 0.0, ALU.mult, ALU.add)
                dve.tensor_copy(d0[R], LF[R])
                dve.tensor_copy(d1[R], LI[R])
                link(dve.tensor_tensor(mprev[R, 4:12], LF[R, SEQ:N:LS], m0r[R], ALU.add))
                link(dve.tensor_tensor(d1[R, SEQ:N:LS], mprev[R, 4:12], LI[R, SEQ:N:LS], ALU.max))
                link(dve.memset(d0[R, SEQ:N:LS], NEG))
                link(dve.tensor_tensor_scan(mm[R], d0[R], d1[R], 0.0, ALU.add, ALU.max))
                dve.memset(mprev[R, 0:1], 0.0)
                dve.tensor_copy(mprev[R, 1:4], mm[R, 127:384:128])
                dve.tensor_copy(mprev[R, 4:12], m0r[R])
                for dst, src in ((blast, bb), (mlast, mm)):
                    dve.tensor_copy(dst[R, 0:4], src[R, 127:SEQ:128])
                    ins = dve.tensor_copy(dst[R, 4:12], src[R, SEQ + LS - 1:N:LS])
                link(ins)
                dve.tensor_copy(mrow[R], mlast[R]).then_inc(q_["m_rows"], 1)
                link(dve.tensor_tensor(blast[R], blast[R], mlast[R], ALU.subtract))
                dve.tensor_tensor(wold[R], blast[R], mprev[R], ALU.add)
                link(dve.tensor_tensor(rbm[R], bb[R], mm[R], ALU.subtract))
                dve.tensor_tensor(pr(wint[R]), pr(rbm[R]), wide(mprev[R, 0:4], 128), ALU.add)
                dve.tensor_tensor(sa(wint[R]), sa(rbm[R]), wide(mprev[R, 4:12], LS), ALU.add)
                link(dve.tensor_tensor(LI[R], LI[R], bb[R], ALU.subtract))
                dve.tensor_tensor(pr(wsr[R]), pr(LI[R]), wide(blast[R, 0:4], 128), ALU.add)
                dve.tensor_tensor(sa(wsr[R]), sa(LI[R]), wide(blast[R, 4:12], LS), ALU.add).then_inc(q_["gate_args"], 1)

            gate_rows()
            dve.wait_ge(q_["lora_loaded"], 48)
            dve.wait_ge(q_["cols_turned"], 1)
            shift(0, wlal)
            shift(1, sgl)
            dve.nop().then_inc(q_["shifted"], 2)
            dve.wait_ge(q_["lora_in"], 1)
            dve.tensor_scalar(sgl, sgl, 0.5, 0.5, ALU.mult, ALU.add).then_inc(q_["gate_low"], 1)

            c1 = 0.5 * SQRT_E
            for j in range(NJ):
                if j:
                    dve.wait_ge(q_["post_projected"], j)
                shift(2 + 3 * j, r_)
                shift(3 + 3 * j, kr)
                link(dve.tensor_scalar(kk, kr, P(KKR + j), None, ALU.mult))
                dve.tensor_tensor(sq, kk, kk, ALU.mult).then_inc(q_["squares"], 1)
                dve.wait_ge(q_["tanhs"], j + 1)
                dve.tensor_scalar(a_, a_, 0.5, 0.5, ALU.mult, ALU.add)
                link(dve.tensor_scalar(ld, ld, -c1, -c1, ALU.mult, ALU.add))
                link(dve.tensor_tensor_scan(L, resets, ld, 0.0, ALU.mult, ALU.add))
                dve.tensor_copy(ec[:, j, 4:12], L[:, SEQ + LS - 1:N:LS])
                link(dve.tensor_copy(lmid[:, j, :], L[:, 63:SEQ:128]))
                link(dve.tensor_tensor(pr(L), pr(L), wide(lmid[:, j, :], 128), ALU.subtract))
                dve.tensor_copy(ec[:, j, 0:4], L[:, 127:SEQ:128])
                dve.tensor_tensor(tmp, L, ld, ALU.subtract).then_inc(q_["decay_args"], 1)
                shift(4 + 3 * j, vr)
                dve.wait_ge(q_["norms"], j + 1)
                link(dve.tensor_scalar(nrm, nrm, 1e-12, None, ALU.max))
                link(dve.reciprocal(nrm, nrm))
                link(dve.tensor_tensor(kk, kk, nrm, ALU.mult))
                dve.wait_ge(q_["decays"], j + 1)
                dve.tensor_tensor(arr[:, j, 0, :], kk, E1, ALU.mult)
                dve.tensor_tensor(arr[:, j, 1, :], r_, E2, ALU.mult)
                link(dve.tensor_tensor(tmp, kk, a_, ALU.mult))
                link(dve.scalar_tensor_tensor(out=nbeta[:, j, :], in0=tmp, scalar=-1.0, in1=E3, op0=ALU.mult, op1=ALU.mult))
                link(dve.tensor_scalar(tmp, a_, P(KAR + j), dprm[:, OMKA + j:OMKA + j + 1], ALU.mult, ALU.add))
                link(dve.tensor_tensor(kr2, kr, tmp, ALU.mult))
                dve.tensor_tensor(kap[:, j, :], kr2, E3, ALU.mult)
                dve.scalar_tensor_tensor(out=nrm, in0=r_, scalar=P(RKR + j), in1=kr2, op0=ALU.mult, op1=ALU.mult).then_inc(q_["rwkv_made"], 1)

            def conv(h, p_):
                n, k = 22 + 2 * h + p_, 14 + 2 * h + p_
                rw, c, dst = raw[k % 2], 4 * p_ + h, (kT if p_ else qT)[h % 2]
                dve.wait_ge(q_["slot_read"], n + 1)
                link(dve.tensor_scalar(zc[:, 0:600], rw[:, 0:600], P(CWR + c), P(CBR + c), ALU.mult, ALU.add))
                for t in range(1, CW):
                    ins = dve.scalar_tensor_tensor(out=zc[:, 0:600], in0=rw[:, t:600 + t], scalar=P(CWR + 8 * t + c), in1=zc[:, 0:600],
                                                   op0=ALU.mult, op1=ALU.add)
                    if t < CW - 1:
                        link(ins)
                ins.then_inc(q_["raw_used"], 1)
                dve.wait_ge(q_["silu_tanh"], 2 * h + p_ + 1)
                sc = 0.5 * (DHA ** -0.5 if p_ else 1.0)
                link(dve.tensor_scalar(th, th, sc, sc, ALU.mult, ALU.add))
                if h >= 2:
                    dve.wait_ge(q_["unit_projected"], h - 1)
                dve.tensor_tensor(dst[:, 0:SEQ], th[:, 0:SEQ], zc[:, 0:SEQ], ALU.mult)
                sv = [a[:, 515:603].rearrange("p (b t) -> p b t", b=NB)[:, :, 0:LS] for a in (th, zc)]
                dve.tensor_tensor(sa(dst), sv[0], sv[1], ALU.mult).then_inc(q_["qk_ready"], 1)
                dve.wait_ge(q_["qk_ready"], 2 * h + p_ + 1)

            def unit(h):
                if h:
                    dve.wait_ge(q_["unit_projected"], h)
                dve.wait_ge(q_["rows_spread"], h + 1)
                dve.tensor_tensor(qt[:, 0:SEQ], qT[h % 2][:, 0:SEQ], bank[4][:, :], ALU.mult)
                link(dve.tensor_tensor(qt[:, SEQ:N], qT[h % 2][:, SEQ:N], bank[5][:, 0:NS], ALU.mult))
                dve.wait_ge(q_["ones_set"], 2)
                o0 = arr_off(qpad)
                diag = arena[:, o0:o0 + NB * 72].rearrange("p (b t) -> p b t", t=72)[:, :, 0:LS]
                dve.tensor_copy(diag, sa(qt)).then_inc(q_["q_scaled"], 1)
                if h:
                    dve.wait_ge(q_["c0_loaded"], 16 * (h + 1))
                dve.tensor_copy(C0[:, :, 128], ncol.rearrange("p (b h) -> p b h", h=HA)[:, :, h])
                dve.tensor_tensor(vpad[0:NS], vext[0:NS, PT, h, :].unsqueeze(1).to_broadcast([NS, NB, 129]),
                                  seqmask[0:NS].unsqueeze(2).to_broadcast([NS, NB, 129]), ALU.mult).then_inc(q_["v_spread"], 1)
                dve.wait_ge(q_["weights"], h + 1)
                dve.tensor_tensor(sT[:, 0:PT, :], bank[4].rearrange("p (i t) -> p i t", i=PT), dm[:, 0:PT, :], ALU.mult)
                dve.tensor_tensor(sT[0:NS, PT, 0:NS], bank[5][0:NS, NS:2 * NS], dm[0:NS, PT, 0:NS], ALU.mult).then_inc(q_["weighted"], 1)
                for i in range(PT):
                    dve.wait_ge(q_["c_delta"], PT * h + i + 1)
                    dl = bank[7][:, 256:385]
                    if i == 0:
                        if h:
                            dve.wait_ge(q_["cs_stored"], 32 * h)
                        dve.tensor_copy(C, dl).then_inc(q_["c_state"], 1)
                    else:
                        dve.scalar_tensor_tensor(out=C, in0=C, scalar=woldb[:, h, i:i + 1], in1=dl, op0=ALU.mult, op1=ALU.add).then_inc(q_["c_state"], 1)
                    dve.wait_ge(q_["c_state"], PT * h + i + 1)
                dve.tensor_copy(nnew[:, NB, h:h + 1], C[:, 128:129])
                dve.wait_ge(q_["cs_delta"], h + 1)
                for b in range(NB):
                    src = (bank[5], bank[6], bank[7])[b // 3][:, 129 * (b % 3):129 * (b % 3) + 129]
                    ins = dve.scalar_tensor_tensor(out=C0[:, b, :], in0=C0[:, b, :], scalar=woldb[:, h, PT + b:PT + b + 1], in1=src, op0=ALU.mult, op1=ALU.add)
                ins.then_inc(q_["cs_new"], 1)
                dve.wait_ge(q_["cs_new"], h + 1)
                dve.tensor_copy(nnew[:, 0:NB, h], C0[:, :, 128]).then_inc(q_["n_new"], 1)
                dve.wait_ge(q_["num_read"], TILES * (h + 1))
                link(dve.scalar_tensor_tensor(out=den, in0=hh[:, :, 128], scalar=-1.0, in1=hh[:, :, 128], op0=ALU.mult, op1=ALU.max))
                link(dve.tensor_tensor(den, den, colg[:, 2, :, h], ALU.max))
                link(dve.reciprocal(rec, den))
                hv = hh[:, :, 0:128]
                link(dve.tensor_tensor(hv, hv, wide(rec, 128), ALU.mult))
                for i in range(TILES):
                    link(dve.bn_stats(out=st2[:, 0, :], in_=hh[:, i, 0:128]))
                    link(dve.bn_aggr(out=mv[:, i, :], in_=st2[:, 0, :]))
                dve.tensor_scalar(mv[:, :, 1], mv[:, :, 1], 1e-6, None, ALU.add).then_inc(q_["ha_moments"], 1)
                link(dve.tensor_tensor(hv, hv, wide(mv[:, :, 0], 128), ALU.subtract))
                dve.wait_ge(q_["ha_std"], h + 1)
                link(dve.reciprocal(rstd, rstd))
                link(dve.tensor_tensor(hv, hv, wide(rstd, 128), ALU.mult))
                link(dve.tensor_tensor(hv, hv, gn_a[:, 128 * h:128 * h + 128].unsqueeze(1).to_broadcast([128, TILES, 128]), ALU.mult))
                hgh = hg[:, :, 128 * h:128 * h + 128]
                dve.tensor_tensor(hgh, hgh, hv, ALU.mult).then_inc(q_["ha_done"], 1)

            dve.wait_ge(q_["post_projected"], NJ)
            link(dve.memset(hh, 1.0))
            for h in range(HA):
                conv(h, 0)
                conv(h, 1)
                if h == 1:
                    dve.wait_ge(q_["gn_loaded"], 48)
                    link(dve.tensor_scalar(hg[:, :, 0:DA], hg[:, :, 0:DA], 0.5, 0.5, ALU.mult, ALU.add))
                if h:
                    unit(h - 1)
            unit(HA - 1)


            dve.wait_ge(q_["outs_turned"], 1)
            for a, n in enumerate((126, 96, 96, 24)):
                dve.tensor_copy(outs[0:n, a, :], bank[5][0:n, 128 * a:128 * a + 128])
            dve.tensor_copy(outs[0:36, 4, :], bank[4][0:36, 0:128]).then_inc(q_["outs_ready"], 1)
            dve.wait_ge(q_["ec_ready"], 1)
            dve.tensor_tensor(pend, em, ec[:, :, 0:PT], ALU.mult)
            dve.memset(S, 0.0)
            link(dve.memset(Sh, 0.0))

            def recur(i, what):
                if what is None:
                    return
                n = rows(i)
                if what == "U":
                    dve.wait_ge(q_["u_projected"], i + 1)
                    dve.tensor_copy(Us[0:n], bank[7][0:n, :]).then_inc(q_["u_read"], 1)
                if what == "O" and i < PT:
                    dve.wait_ge(q_["s_projected"], i + 1)
                    link(dve.tensor_tensor(S, S, wide(pend[:, :, i], 128), ALU.mult))
                    pv = bank[7].rearrange("p (j v) -> p j v", j=NJ)
                    dve.tensor_tensor(S[0:64, :, 0:64], S[0:64, :, 0:64], pv[0:64, :, 0:64], ALU.add)
                    link(dve.tensor_tensor(S[64:128, :, 64:128], S[64:128, :, 64:128], pv[64:128, :, 64:128], ALU.add))
                    if i < PT - 1:
                        dve.tensor_tensor(Sh, S, wide(em[:, :, i + 1], 128), ALU.mult)
                    dve.nop().then_inc(q_["state"], 1)
                if what == "G":
                    dve.wait_ge(q_["o_read"], i + 1)
                    fv = hg[0:n, i, DA:D]
                    hv = fv.rearrange("p (h v) -> p h v", h=HB)
                    gv = gtk[0:n].rearrange("p (h v) -> p h v", h=HB)
                    link(dve.tensor_reduce(ssum[0:n], hv, AX.X, ALU.add))
                    link(dve.tensor_scalar(ssum[0:n], ssum[0:n], 1.0 / DHB, None, ALU.mult))
                    link(dve.tensor_tensor(hv, hv, wide(ssum[0:n], DHB), ALU.subtract))
                    link(dve.tensor_tensor(gv, hv, hv, ALU.mult))
                    link(dve.tensor_reduce(sqs[0:n], gv, AX.X, ALU.add))
                    dve.tensor_scalar(sqs[0:n], sqs[0:n], DHB * 64e-5, None, ALU.add).then_inc(q_["hb_moments"], 1)
                    link(dve.tensor_tensor(gv, vtok[0:n, i, :].rearrange("p (h v) -> p h v", h=HB), wide(bon[0:n, i, :], DHB), ALU.mult))
                    link(dve.tensor_tensor(gtk[0:n], gtk[0:n], lnx_b[0:n], ALU.add))
                    dve.wait_ge(q_["hb_std"], i + 1)
                    link(dve.reciprocal(sqs[0:n], sqs[0:n]))
                    link(dve.tensor_tensor(hv, hv, wide(sqs[0:n], DHB), ALU.mult))
                    link(dve.tensor_tensor(fv, fv, lnx_g[0:n], ALU.mult))
                    link(dve.tensor_tensor(fv, fv, gtk[0:n], ALU.add))
                    dve.wait_ge(q_["g_projected"], i + 1)
                    dve.tensor_tensor(fv, fv, bank[7][0:n, :], ALU.mult).then_inc(q_["hb_done"], 1)

            for i in range(TILES):
                n = rows(i)
                tri = tri_p if i < PT else tri_s
                if i >= 2:
                    dve.wait_ge(q_["o_projected"], i - 1)
                for s_ in range(4):
                    q, w = s_ // 2, s_ % 2
                    dve.wait_ge(q_["grams"], 4 * i + s_ + 1)
                    for odd in range(2):
                        src = bank[2 * (s_ % 3) + odd][0:n, :].rearrange("p (h v t) -> p h v t", h=2, v=2)[:, :, :, 0:n]
                        dst = G[i % 2][0:n, w, 4 * q + odd:4 * q + 4:2, :].rearrange("p h (v t) -> p h v t", v=2)[:, :, :, 0:n]
                        ins = dve.tensor_tensor(dst, src, tri[0:n].unsqueeze(1).to_broadcast([n, 2, 2, n]), ALU.mult)
                    ins.then_inc(q_["gram_read"], 1)
                for l in range(LV(i)):
                    for q in range(2):
                        k = ix(i, l, q)
                        Yq = Y[i % 2][0:n, 4 * q:4 * q + 4, 0:n]
                        if l == 0:
                            idn = ident[0:n, 0:n].unsqueeze(1).to_broadcast([n, 4, n])
                            dve.wait_ge(q_["mt_ready"], k + 1)
                            dve.tensor_tensor(Yq, MT[q][0:n, :, 0:n], idn, ALU.add)
                            dve.wait_ge(q_["w_read"], k + 1)
                            dve.tensor_tensor(X[q][0:n, :, 0:n], W[q][0:n, :, 0:n], idn, ALU.add).then_inc(q_["yx_read"], 1)
                        else:
                            dve.wait_ge(q_["yx_projected"], ix2(i, l, q) + 1)
                            pv = [bank[b_][0:n, :].rearrange("p (h t) -> p h t", h=4)[:, :, 0:n] for b_ in (2 + q, 4 + q)]
                            ins = dve.tensor_tensor(Yq, Yq, pv[0], ALU.add)
                            if l < LV(i) - 1:
                                ins = dve.tensor_tensor(X[q][0:n, :, 0:n], X[q][0:n, :, 0:n], pv[1], ALU.add)
                            ins.then_inc(q_["yx_read"], 1)
                    recur(i - 1, hooks(i, l))
            recur(PT - 1, "G")
            dve.wait_ge(q_["sst_zero"], 1)
            diag = [arena[:, arr_off(arpad[:, v]):arr_off(arpad[:, v]) + NB * 72].rearrange("p (b t) -> p b t", t=72)[:, :, 0:LS] for v in range(2)]
            for j in range(NJ):
                if j:
                    dve.wait_ge(q_["pads_used"], j)
                for v in range(2):
                    ins = dve.tensor_copy(diag[v], sa(arr[:, j, v, :]))
                ins.then_inc(q_["pads_made"], 1)
            dve.wait_ge(q_["ps_projected"], 1)
            for h2 in range(2):
                r = slice(64 * h2, 64 * h2 + 64)
                ins = dve.tensor_copy(pS[r], bank[5][r, 0:256].rearrange("p (j k) -> p j k", j=NJ))
            ins.then_inc(q_["ps_ready"], 1)
            recur(PT, "U")
            dve.tensor_tensor(SsT[:, :, :, :], SsT[:, :, :, :], ec[:, :, 4:12].unsqueeze(3).to_broadcast([128, NJ, NB, 128]), ALU.mult).then_inc(q_["sst_scaled"], 1)
            for h in range(HB):
                r = slice(64 * (h % 2), 64 * (h % 2) + 64)
                dve.wait_ge(q_["ss_projected"], h + 1)
                dve.tensor_copy(Sld[r, h // 2, :, :], bank[h % 4][r, :].rearrange("p (b k) -> p b k", b=NB)).then_inc(q_["ss_read"], 1)
            recur(PT, "G")

            def norm_rows(y, n, stat):
                for q in range(2):
                    ins = dve.bn_stats(out=st2[0:n, q, :], in_=y[:, 512 * q:512 * q + 512])
                link(ins)
                link(dve.bn_aggr(out=mv[0:n, 0, :], in_=st2[0:n]))
                dve.tensor_scalar(mv[0:n, 0, 1:2], mv[0:n, 0, 1:2], 1e-5, None, ALU.add).then_inc(q_["ln_moments"], 1)
                dve.wait_ge(q_["ln_std"], stat)
                link(dve.reciprocal(rstd[0:n, 0:1], rstd[0:n, 0:1]))
                link(dve.tensor_scalar(y, y, mv[0:n, 0, 0:1], rstd[0:n, 0:1], ALU.subtract, ALU.mult))

            dve.wait_ge(q_["x_back"], 16 * TILES)
            dve.wait_ge(q_["ln_loaded"], 16 * 6)
            for i in range(TILES):
                n = rows(i)
                y = xln[0:n, i, :]
                dve.wait_ge(q_["mix_projected"], i + 1)
                for q in range(2):
                    b_ = 2 * (i % 2) + q
                    yq = y[:, 512 * q:512 * q + 512]
                    ins = dve.scalar_tensor_tensor(out=yq, in0=yq, scalar=ALPHA, in1=bank[b_][0:n, :], op0=ALU.mult, op1=ALU.add)
                ins.then_inc(q_["mix_read"], 1)
                dve.wait_ge(q_["mix_read"], i + 1)
                norm_rows(y, n, i + 1)
                link(dve.tensor_tensor(y, y, l1g[0:n], ALU.mult))
                dve.tensor_tensor(y, y, l1b[0:n], ALU.add).then_inc(q_["ln1_done"], 1)
            dve.wait_ge(q_["ln1_done"], TILES)
            link(dve.memset(probs, 0.0))
            dve.wait_ge(q_["logits"], 1)
            lv = bank[4][:, 0:TILES * NE].rearrange("p (i e) -> p i e", i=TILES)
            dve.tensor_copy(probs[:, 0:PT, :], lv[:, 0:PT, :])
            link(dve.tensor_copy(probs[0:NS, PT, :], lv[0:NS, PT, :]))
            link(dve.tensor_reduce(one5, probs, AX.X, ALU.max))
            dve.tensor_tensor(probs, probs, wide(one5, NE), ALU.subtract).then_inc(q_["logits_shifted"], 1)
            dve.wait_ge(q_["probs_exp"], 1)
            link(dve.tensor_reduce(one5, probs, AX.X, ALU.add))
            link(dve.reciprocal(one5, one5))
            link(dve.tensor_tensor(probs, probs, wide(one5, NE), ALU.mult))
            link(dve.tensor_tensor(sl, probs, brr.unsqueeze(1).to_broadcast([128, TILES, NE]), ALU.add))

            def grp(ap):
                return ap.rearrange("p i (g e) -> p (i g) e", g=NG)

            def f1(ap):
                return ap.rearrange("p i g -> p (i g)")

            def first_of(dst, src, top, scratch):
                link(dve.tensor_tensor(grp(dst), grp(src), wide(f1(top), EG), ALU.is_ge))
                for k in range(1, EG):
                    link(dve.tensor_reduce(f1(scratch), grp(dst)[:, :, 0:k], AX.X, ALU.max))
                    link(dve.scalar_tensor_tensor(out=grp(dst)[:, :, k], in0=f1(scratch), scalar=0.0, in1=grp(dst)[:, :, k], op0=ALU.is_equal, op1=ALU.mult))

            link(dve.tensor_reduce(f1(gmax), grp(sl), AX.X, ALU.max))
            first_of(t80a, sl, gmax, gsum)
            link(dve.scalar_tensor_tensor(out=t80b, in0=t80a, scalar=NEG, in1=sl, op0=ALU.mult, op1=ALU.add))
            link(dve.tensor_reduce(f1(gsum), grp(t80b), AX.X, ALU.max))
            link(dve.tensor_tensor(gmax, gmax, gsum, ALU.add))
            link(dve.tensor_copy(f1(gtop), f1(gsum)))
            first_of(gate, t80b, gtop, gsum)
            link(dve.tensor_tensor(gate, gate, t80a, ALU.add))
            link(dve.tensor_reduce(one5, gmax, AX.X, ALU.max))
            link(dve.tensor_tensor(gtop, gmax, wide(one5, NG), ALU.is_ge))
            for k in range(1, NG):
                link(dve.tensor_reduce(one5, gtop[:, :, 0:k], AX.X, ALU.max))
                link(dve.scalar_tensor_tensor(out=gtop[:, :, k], in0=one5, scalar=0.0, in1=gtop[:, :, k], op0=ALU.is_equal, op1=ALU.mult))
            link(dve.tensor_tensor(grp(gate), grp(gate), wide(f1(gtop), EG), ALU.mult))
            link(dve.tensor_tensor(gate, gate, probs, ALU.mult))
            link(dve.tensor_reduce(one5, gate, AX.X, ALU.add))
            link(dve.reciprocal(one5, one5))
            link(dve.tensor_tensor(gate, gate, wide(one5, NE), ALU.mult))
            dve.wait_ge(q_["x1_turned"], TILES)
            for i in range(TILES):
                n = rows(i)
                ins = dve.tensor_scalar(xln[0:n, i, :], xln[0:n, i, :], ALPHA, None, ALU.mult)
            link(ins)
            for e_ in range(NE):
                for f in range(NF):
                    k = NF * e_ + f
                    dve.wait_ge(q_["hid_silu"], k + 1)
                    if f == 0 and e_:
                        dve.wait_ge(q_["down"], TILES * e_)
                    dve.tensor_tensor(hid[:, f, 0:SEQ], hs[:, 0:SEQ], bank[2][:, :], ALU.mult)
                    dve.tensor_tensor(hid[:, f, SEQ:N], hs[:, SEQ:N], bank[3][:, 0:NS], ALU.mult).then_inc(q_["hid_ready"], 1)
                for i in range(TILES):
                    n = rows(i)
                    k = TILES * e_ + i
                    dve.wait_ge(q_["down"], k + 1)
                    for q in range(2):
                        yq = xln[0:n, i, 512 * q:512 * q + 512]
                        ins = dve.scalar_tensor_tensor(out=yq, in0=bank[4 + 2 * (k % 2) + q][0:n, :], scalar=gate[0:n, i, e_:e_ + 1], in1=yq, op0=ALU.mult, op1=ALU.add)
                    ins.then_inc(q_["down_read"], 1)
            dve.wait_ge(q_["down_read"], TILES * NE)
            for i in range(TILES):
                n = rows(i)
                y = xln[0:n, i, :]
                norm_rows(y, n, TILES + i + 1)
                link(dve.tensor_tensor(y, y, l2g[0:n], ALU.mult))
                dve.tensor_tensor(y, y, l2b[0:n], ALU.add).then_inc(q_["y_ready"], 1)

        @block.tensor
        def _(pe):
            pe.wait_ge(q_["ident_ready"], 1)
            pe.wait_ge(q_["prm_loaded"], 128)
            pe.wait_ge(q_["hist_loaded"], 48)
            pe.transpose(bank[4][:, 0:NPRM], prow[0:NPRM, :], ident[0:NPRM, 0:NPRM])
            for t in range(14):
                pe.transpose(bank[4][:, 74 + 8 * t:82 + 8 * t], shrows[0:NB, t, :], ident[0:NB, 0:NB])
            for t in range(8):
                pe.transpose(bank[4][:, 186 + 24 * t:210 + 24 * t], cvrows[0:24, t, :], ident[0:24, 0:24])
            pe.transpose(bank[4][:, 378:410], nrows[0:32, :], ident[0:32, 0:32]).then_inc(q_["prm_turned"], 1)
            for i in range(TILES):
                n = rows(i)
                pe.wait_ge(q_["ln0_done"], i + 1)
                if i >= 2:
                    pe.wait_ge(q_["xt_ready"], i - 1)
                for k in range(KD):
                    ins = pe.transpose(bank[2 * (i % 2) + k // 4][:, 128 * (k % 4):128 * (k % 4) + n], x[0:n, i, 128 * k:128 * k + 128], ident[0:n, 0:n])
                ins.then_inc(q_["x_turned"], 1)
            pe.wait_ge(q_["xt_ready"], TILES)
            pe.wait_ge(q_["gate_loaded"], 64)
            for i in range(TILES):
                for k in range(KD):
                    ins = pe.matmul(bank[7][0:rows(i), 8 * i:8 * i + 8], xT[:, k, cols(i)], gw[:, k, :], start=k == 0, stop=k == KD - 1)
            ins.then_inc(q_["gates_projected"], 1)

            def slot(n):
                pe.wait_ge(w_loaded[n % NW], 16 * (n // NW + 1))
                if n >= 2:
                    pe.wait_ge(q_["slot_read"], n - 1)
                A, B = bank[2 * (n % 2)], bank[2 * (n % 2) + 1]
                w = wring[:, n % NW]
                if 14 <= n < 22:
                    for i in range(TILES):
                        dst = A[:, 128 * i:128 * i + 128] if i < PT else B[0:NS, 0:128]
                        for k in range(KD):
                            ins = pe.matmul(dst, xT[:, k, cols(i)], w[:, k, :], start=k == 0, stop=k == KD - 1)
                else:
                    for k in range(KD):
                        pe.matmul(A[:, :], w[:, k, :], xT[:, k, 0:SEQ], start=k == 0, stop=k == KD - 1)
                        ins = pe.matmul(B[:, 0:NS], w[:, k, :], xT[:, k, SEQ:N], start=k == 0, stop=k == KD - 1)
                ins.then_inc(q_["slot_projected"], 1)

            def both(A, B, lhs, rhs):
                pe.matmul(A, lhs, rhs[:, 0:SEQ], start=True, stop=True)
                return pe.matmul(B, lhs, rhs[:, SEQ:N], start=True, stop=True)

            slot(0)
            pe.wait_ge(q_["gate_tokens"], 1)
            pe.wait_ge(q_["cols_ready"], 1)
            for i in range(TILES):
                n = rows(i)
                li = bank[4][0:HA, 128 * i:128 * i + n] if i < PT else bank[5][0:HA, 0:NS]
                lf = bank[6][0:HA, 128 * i:128 * i + n] if i < PT else bank[5][0:HA, NS:2 * NS]
                pe.transpose(li, gtok[0:n, i, 0:HA], ident[0:n, 0:n])
                ins = pe.transpose(lf, gtok[0:n, i, HA:8], ident[0:n, 0:n])
            ins.then_inc(q_["gates_turned"], 1)
            slot(1)
            pe.wait_ge(q_["gate_rows"], 1)
            for a, src in enumerate((LI, wsr, emt)):
                for i in range(TILES):
                    pe.transpose(bank[5][0:rows(i), 20 * a + 4 * i:20 * a + 4 * i + 4], src[0:HA, cols(i)], ident[0:HA, 0:HA])
            for h in range(HA):
                ins = pe.matmul(bank[5][:, 64 + 12 * h:76 + 12 * h], sel[0:HA, h, :], wold[0:HA, :], start=True, stop=True)
            ins.then_inc(q_["cols_turned"], 1)
            pe.wait_ge(q_["gate_cols"], 1)

            def post(j):
                pe.wait_ge(q_["rwkv_made"], j + 1)
                for i in range(TILES):
                    pe.matmul(bank[7][0:rows(i), 2 * i:2 * i + 2], nrm[:, cols(i)], headsel, start=True, stop=True)
                for i in range(TILES):
                    dst = bank[6][:, 128 * i:128 * i + 128] if i < PT else bank[7][0:NS, 128:256]
                    ins = pe.transpose(dst, vr[:, cols(i)], ident)
                ins.then_inc(q_["post_projected"], 1)

            for j in range(NJ):
                slot(2 + 3 * j)
                if j:
                    post(j - 1)
                slot(3 + 3 * j)
                if j == 0:
                    pe.wait_ge(q_["lora_in"], 1)
                else:
                    pe.wait_ge(q_["norms"], j)
                    pe.wait_ge(q_["post_read"], j)
                both(bank[4][:, :], bank[5][:, 0:NS], w2a2[0:64, 128 * j:128 * j + 128], wlal[0:64])
                both(bank[6][:, :], bank[7][:, 256:256 + NS], w2a2[64:128, 128 * j:128 * j + 128], wlal[64:128]).then_inc(q_["lora_projected"], 1)
                slot(4 + 3 * j)
                pe.wait_ge(q_["squares"], j + 1)
                pe.wait_ge(q_["tanhs"], j + 1)
                both(bank[4][:, :], bank[5][:, 0:NS], blockones, sq).then_inc(q_["norms_projected"], 1)
            slot(14)
            post(NJ - 1)
            for n in range(15, 22):
                slot(n)

            def unit(h):
                if h == 0:
                    pe.wait_ge(q_["post_read"], NJ)
                else:
                    pe.wait_ge(q_["cs_new"], h)
                    pe.wait_ge(q_["num_read"], TILES * h)
                pe.wait_ge(q_["gate_rows"], 1)
                both(bank[4][:, :], bank[5][:, 0:NS], sel[0:HA, h, :], wint[0:HA]).then_inc(q_["rows_spread"], 1)
                pe.wait_ge(q_["qk_ready"], 2 * h + 2)
                for i in range(TILES):
                    dst = bank[6][:, 128 * i:128 * i + 128] if i < PT else bank[7][0:NS, 0:128]
                    ins = pe.transpose(dst, kT[h % 2][:, cols(i)], ident)
                ins.then_inc(q_["k_turned"], 1)
                pe.wait_ge(q_["q_scaled"], h + 1)
                pe.wait_ge(q_["k_tokens"], h + 1)
                for i in range(TILES):
                    n = rows(i)
                    kq = bank[4][:, 128 * i:128 * i + 128] if i < PT else bank[5][0:NS, NS:2 * NS]
                    dd = bank[6][:, 128 * i:128 * i + 128] if i < PT else bank[7][0:NS, 128:192]
                    pe.matmul(kq, kT[h % 2][:, cols(i)], qT[h % 2][:, cols(i)], start=True, stop=True)
                    pe.matmul(dd, sel[0:HA, h, 0:n], rbm[0:HA, cols(i)], start=True, stop=False)
                    ins = pe.matmul(dd, ident[0:n, 0:n], neg_p if i < PT else neg_s[0:NS], start=False, stop=True)
                ins.then_inc(q_["scores"], 1)
                pe.wait_ge(q_["weighted"], h + 1)
                for i in range(TILES):
                    n = rows(i)
                    dst = bank[4 + i % 2][0:n, 128:257]
                    if i >= 2:
                        pe.wait_ge(q_["num_read"], TILES * h + i - 1)
                    if i == 0:
                        pe.matmul(dst, sT[:, 0, :], vext[:, 0, h, :], start=True, stop=True).then_inc(q_["numerator"], 1)
                    elif i < PT:
                        pe.wait_ge(q_["c_state"], PT * h + i)
                        pe.matmul(dst, qt[:, cols(i)], C, start=True, stop=False)
                        pe.matmul(dst, sT[:, i, :], vext[:, i, h, :], start=False, stop=True).then_inc(q_["numerator"], 1)
                    else:
                        pe.wait_ge(q_["c0_loaded"], 16 * (h + 1))
                        pe.wait_ge(q_["v_spread"], h + 1)
                        for b in range(NB):
                            pe.matmul(dst, qpad[:, b, :], C0[:, b, :], start=b == 0, stop=False)
                        pe.matmul(dst, sT[0:NS, PT, 0:NS], vext[0:NS, PT, h, :], start=False, stop=True).then_inc(q_["numerator"], 1)
                    if i < PT:
                        if i:
                            pe.wait_ge(q_["c_state"], PT * h + i)
                        pe.matmul(bank[7][:, 256:385], kw[:, i, :], vext[:, i, h, :], start=True, stop=True).then_inc(q_["c_delta"], 1)
                pe.wait_ge(q_["c_state"], PT * (h + 1))
                pe.wait_ge(q_["num_read"], TILES * h + PT)
                for dst, b0, b1 in ((bank[5], 0, 3), (bank[6], 3, 6), (bank[7], 6, 8)):
                    ins = pe.matmul(dst[:, 0:129 * (b1 - b0)], kw[0:NS, PT, :], vpad[0:NS, b0:b1, :], start=True, stop=True)
                ins.then_inc(q_["cs_delta"], 1)
                pe.nop().then_inc(q_["unit_projected"], 1)

            for h in range(HA):
                slot(22 + 2 * h)
                slot(23 + 2 * h)
                if h:
                    unit(h - 1)
            unit(HA - 1)

            pe.wait_ge(q_["raw_collected"], 22)
            pe.wait_ge(q_["n_new"], HA)
            pe.wait_ge(q_["num_read"], TILES * HA)
            pe.transpose(bank[5][0:126, 0:128], shnew.rearrange("p b t -> p (b t)"), ident)
            cv = cvnew.rearrange("p b w c -> p (b w c)")
            pe.transpose(bank[5][0:96, 128:256], cv[:, 0:96], ident)
            pe.transpose(bank[5][0:96, 256:384], cv[:, 96:192], ident)
            pe.transpose(bank[5][0:24, 384:512], cv[:, 192:216], ident)
            pe.transpose(bank[4][0:36, 0:128], nnew.rearrange("p b h -> p (b h)"), ident).then_inc(q_["outs_turned"], 1)
            pe.wait_ge(q_["outs_ready"], 1)

            def recur(i, what):
                if what is None:
                    return
                n = rows(i)
                H = [slice(64 * h, 64 * h + 64) for h in range(HB)]
                Gi, Yi = G[i % 2], Y[i % 2]
                V = vtok[0:n, i, :]
                if what == "Z" and i < PT:
                    if i:
                        pe.wait_ge(q_["state"], i)
                        pe.wait_ge(q_["o_read"], i)
                    for j in range(NJ):
                        if i:
                            pe.matmul(bank[6][:, 128 * j:128 * j + 128], arr[:, j, 0, cols(i)], Sh[:, j, :], start=j == 0, stop=False, skip_group_check=True)
                        for h in (2 * j, 2 * j + 1):
                            ins = pe.matmul(bank[6][:, H[h]], Gi[:, 1, h, 0:128], V[:, H[h]], start=i + h == 0, stop=True, skip_group_check=True)
                    ins.then_inc(q_["z_projected"], 1)
                if what == "Z" and i == PT:
                    for j in range(NJ):
                        pe.wait_ge(q_["pads_made"], j + 1)
                        for v, dst in ((0, bank[6]), (1, bank[4])):
                            for b in range(NB):
                                ins = pe.matmul(dst[0:n, 128 * j:128 * j + 128], arpad[:, v, b, :], SsT[:, j, b, :], start=j + b == 0, stop=False, skip_group_check=True)
                        ins.then_inc(q_["pads_used"], 1)
                    for h in range(HB):
                        ins = pe.matmul(bank[6][0:n, H[h]], Gi[0:n, 1, h, 0:n], V[:, H[h]], start=False, stop=True, skip_group_check=True)
                    ins.then_inc(q_["z_projected"], 1)
                if what == "U":
                    pe.wait_ge(q_["z_read"], i + 1)
                    if i:
                        pe.wait_ge(q_["hb_done"], i)
                    for h in range(HB):
                        ins = pe.matmul(bank[7][0:n, H[h]], Yi[0:n, h, 0:n], Zs[0:n, H[h]], start=True, stop=True)
                    ins.then_inc(q_["u_projected"], 1)
                if what == "O":
                    pe.wait_ge(q_["u_read"], i + 1)
                    ob = bank[6 if i < PT else 4]
                    for j in range(NJ):
                        if 0 < i < PT:
                            pe.matmul(ob[:, 128 * j:128 * j + 128], arr[:, j, 1, cols(i)], Sh[:, j, :], start=j == 0, stop=False, skip_group_check=True)
                        for h in (2 * j, 2 * j + 1):
                            pe.matmul(ob[0:n, H[h]], Gi[0:n, 1, h, 128:128 + n], V[:, H[h]], start=i + h == 0, stop=False, skip_group_check=True)
                            ins = pe.matmul(ob[0:n, H[h]], Gi[0:n, 0, h, 128:128 + n], Us[0:n, H[h]], start=False, stop=True, skip_group_check=True)
                    ins.then_inc(q_["o_projected"], 1)
                    if i < PT:
                        for j in range(NJ):
                            c_ = slice(128 * j, 128 * j + 128)
                            pe.matmul(bank[7][:, c_], kpt[i % 2][:, 1, c_], V[:, c_], start=True, stop=False)
                            ins = pe.matmul(bank[7][:, c_], kpt[i % 2][:, 0, c_], Us[:, c_], start=False, stop=True)
                        ins.then_inc(q_["s_projected"], 1)
                if what == "G":
                    if i < PT:
                        pe.wait_ge(q_["state"], i + 1)
                    pe.matmul(bank[7][0:n, :], sgl[:, cols(i)], g2w, start=True, stop=True).then_inc(q_["g_projected"], 1)

            for i in range(TILES):
                n = rows(i)
                last = ix(i - 1, LV(i - 1) - 1, 1) + 1 if i else 0
                pe.wait_ge(q_["ktmp_made"], i + 1)
                if i:
                    pe.wait_ge(q_["yx_read"], last)
                    pe.wait_ge(q_["w_read"], last)
                for w in range(2):
                    for j in range(NJ):
                        ins = pe.transpose(bank[2 + w][0:n, 128 * j:128 * j + 128], ktmp[:, w, j, 0:n], ident)
                ins.then_inc(q_["kt_turned"], 1)
                for s_ in range(4):
                    q, w = s_ // 2, s_ % 2
                    if s_ == 1:
                        pe.wait_ge(q_["kt_read"], i + 1)
                    if s_ == 3:
                        pe.wait_ge(q_["gram_read"], 4 * i + 1)
                    for h in range(4 * q, 4 * q + 4):
                        r = slice(64 * (h % 2), 64 * (h % 2) + 64)
                        j = h // 2
                        dst = bank[2 * (s_ % 3) + h % 2][0:n, 256 * (j % 2):256 * (j % 2) + 256].rearrange("p (v t) -> p v t", v=2)[:, :, 0:n]
                        ins = pe.matmul(dst, (kap if w else nbeta)[r, j, cols(i)], arr[r, j, :, cols(i)], start=True, stop=True)
                    ins.then_inc(q_["grams"], 1)
                pe.wait_ge(q_["gram_read"], 4 * i + 4)
                for l in range(LV(i)):
                    for q in range(2):
                        k = ix(i, l, q)
                        pe.wait_ge(q_["mt_ready"], k + 1)
                        if l:
                            pe.wait_ge(q_["yx_read"], k - 1)
                        for h in range(4):
                            ins = pe.matmul(bank[q][0:n, 128 * h:128 * h + n], MT[q][0:n, h, 0:n], X[q][0:n, h, 0:n] if l else ident[0:n, 0:n], start=True, stop=True)
                        ins.then_inc(q_["w_projected"], 1)
                    for q in range(2):
                        if l:
                            pe.wait_ge(q_["w_read"], ix(i, l, q) + 1)
                            for h in range(4):
                                yh = Y[i % 2][0:n, 4 * q + h, 0:n]
                                ins = pe.matmul(bank[2 + q][0:n, 128 * h:128 * h + n], W[q][0:n, h, 0:n], yh, start=True, stop=True)
                                if l < LV(i) - 1:
                                    ins = pe.matmul(bank[4 + q][0:n, 128 * h:128 * h + n], yh, W[q][0:n, h, 0:n], start=True, stop=True)
                            ins.then_inc(q_["yx_projected"], 1)
                    recur(i - 1, hooks(i, l))
            recur(PT - 1, "G")
            pe.wait_ge(q_["sst_loaded"], 16 * HB)
            pe.wait_ge(q_["yx_read"], ix(PT, 2, 1) + 1)
            for j in range(NJ):
                if j >= 2:
                    pe.wait_ge(q_["st_read"], j - 1)
                for b in range(NB):
                    for h2 in range(2):
                        r = slice(64 * h2, 64 * h2 + 64)
                        ins = pe.matmul(bank[2 * (j % 2) + h2][r, 64 * b:64 * b + 64], Sld[r, j, b, :], ident[r, r], start=True, stop=True)
                ins.then_inc(q_["st_turned"], 1)
            for h in range(HB):
                r = slice(64 * (h % 2), 64 * (h % 2) + 64)
                ins = pe.matmul(bank[5][r, 64 * (h // 2):64 * (h // 2) + 64], S[:, h // 2, r], ident[:, r], start=True, stop=True)
            ins.then_inc(q_["ps_projected"], 1)
            pe.wait_ge(q_["st_read"], NJ)
            pe.wait_ge(q_["o_read"], PT)
            recur(PT, "Z")
            recur(PT, "U")
            recur(PT, "O")
            pe.wait_ge(q_["sst_scaled"], 1)
            for h in range(HB):
                r = slice(64 * (h % 2), 64 * (h % 2) + 64)
                j, H = h // 2, slice(64 * h, 64 * h + 64)
                pe.wait_ge(q_["kp_spread"], h + 1)
                if h >= 4:
                    pe.wait_ge(q_["ss_read"], h - 3)
                dst = bank[h % 4]
                for b in range(NB):
                    pe.matmul(dst[r, 64 * b:64 * b + 64], SsT[:, j, b, r], ident[:, r], start=b == 0, stop=False, skip_group_check=True)
                pe.matmul(dst[r, :], vtok[0:NS, PT, H], kppad[h % 2][0:NS, 1], start=False, stop=False, skip_group_check=True)
                ins = pe.matmul(dst[r, :], Us[0:NS, H], kppad[h % 2][0:NS, 0], start=False, stop=True, skip_group_check=True)
                ins.then_inc(q_["ss_projected"], 1)
            recur(PT, "G")

            for i in range(TILES):
                n = rows(i)
                if i == 0:
                    pe.wait_ge(q_["hb_done"], TILES)
                    pe.wait_ge(q_["o_read"], TILES)
                if i >= 2:
                    pe.wait_ge(q_["ht_ready"], i - 1)
                for k in range(KD):
                    ins = pe.transpose(bank[4 + 2 * (i % 2) + k // 4][:, 128 * (k % 4):128 * (k % 4) + n], hg[0:n, i, 128 * k:128 * k + 128], ident[0:n, 0:n])
                ins.then_inc(q_["h_turned"], 1)
            pe.wait_ge(q_["wout_loaded"], 16)
            for i in range(TILES):
                n = rows(i)
                pe.wait_ge(q_["ht_ready"], i + 1)
                if i >= 2:
                    pe.wait_ge(q_["mix_read"], i - 1)
                for q in range(2):
                    for k in range(KD):
                        ins = pe.matmul(bank[2 * (i % 2) + q][0:n, :], hT[:, k, cols(i)], wout[:, k, 512 * q:512 * q + 512], start=k == 0, stop=k == KD - 1)
                ins.then_inc(q_["mix_projected"], 1)
            for i in range(TILES):
                n = rows(i)
                pe.wait_ge(q_["ln1_done"], i + 1)
                if i >= 2:
                    pe.wait_ge(q_["x1_turned"], i - 1)
                else:
                    pe.wait_ge(q_["ht_ready"], TILES)
                for k in range(KD):
                    ins = pe.transpose(bank[4 + 2 * (i % 2) + k // 4][:, 128 * (k % 4):128 * (k % 4) + n], xln[0:n, i, 128 * k:128 * k + 128], ident[0:n, 0:n])
                ins.then_inc(q_["x1_in_psum"], 1)
            pe.wait_ge(q_["x1_turned"], TILES)
            for i in range(TILES):
                for k in range(KD):
                    ins = pe.matmul(bank[4][0:rows(i), NE * i:NE * i + NE], x1T[:, k, cols(i)], wrt[:, k, :], start=k == 0, stop=k == KD - 1)
            ins.then_inc(q_["logits"], 1)
            pe.wait_ge(q_["logits_shifted"], 1)
            for e_ in range(NE):
                wg, wu, wd = wexp[e_ % 2]
                pe.wait_ge(wexp_loaded[e_ % 2], 48 * (e_ // 2 + 1))
                for f in range(NF):
                    k_ = NF * e_ + f
                    if k_:
                        pe.wait_ge(q_["hid_ready"], k_)
                    for k in range(KD):
                        for w, A, B in ((wg, bank[0], bank[1]), (wu, bank[2], bank[3])):
                            pe.matmul(A[:, :], w[:, k, 128 * f:128 * f + 128], x1T[:, k, 0:SEQ], start=k == 0, stop=k == KD - 1)
                            ins = pe.matmul(B[:, 0:NS], w[:, k, 128 * f:128 * f + 128], x1T[:, k, SEQ:N], start=k == 0, stop=k == KD - 1)
                    ins.then_inc(q_["hidden"], 1)
                pe.wait_ge(q_["hid_ready"], NF * (e_ + 1))
                for i in range(TILES):
                    n = rows(i)
                    k_ = TILES * e_ + i
                    if k_ >= 2:
                        pe.wait_ge(q_["down_read"], k_ - 1)
                    for q in range(2):
                        for f in range(NF):
                            ins = pe.matmul(bank[4 + 2 * (k_ % 2) + q][0:n, :], hid[:, f, cols(i)], wd[:, f, 512 * q:512 * q + 512], start=f == 0, stop=f == NF - 1)
                    ins.then_inc(q_["down"], 1)


def flat(src, n):
    v = src[0] if len(src.shape) > 1 else src
    if len(v.shape) == 2:
        w = v.shape[1]
        return v.rearrange("a (b f) -> (a b) f", f=128) if w >= 128 else v.rearrange("(a b) c -> a (b c)", b=128 // w)
    return v.rearrange("(a f) -> a f", f=128)


def brow(v, n):
    return v.rearrange("(a n) -> a n", a=1).to_broadcast([128, n])


def arr_off(ap):
    return ap.offset


INS = ["x_prompt", "x_sample", "state_mlstm_C", "state_mlstm_n", "state_mlstm_m", "state_mlstm_conv", "state_rwkv_S",
       "state_rwkv_shift", "ln0_g", "ln0_b", "w_in", "conv_w", "conv_b", "b_i", "b_f", "gn_a_g", "mu_shift", "w0", "w2",
       "a0", "a2", "g2", "k_k", "k_a", "r_k", "lnx_g", "lnx_b", "w_out", "ln1_g", "ln1_b", "w_router", "b_router",
       "we_gate", "we_up", "we_down", "ln2_g", "ln2_b"]
OUTS = [("y_prompt", (1, SEQ, D)), ("y_sample", (NB, LS, D)),
        ("p_C", (1, 1, HA, DHA, DHA)), ("p_n", (1, 1, HA, DHA)), ("p_m", (1, 1, HA)),
        ("p_conv", (1, 1, CW - 1, 2 * DA)), ("p_S", (1, 1, HB, DHB, DHB)), ("p_shift", (1, 1, 14 * 128)),
        ("s_C", (1, NB, HA, DHA, DHA)), ("s_n", (1, NB, HA, DHA)), ("s_m", (1, NB, HA)),
        ("s_conv", (1, NB, CW - 1, 2 * DA)), ("s_S", (1, NB, HB, DHB, DHB)), ("s_shift", (1, NB, 14 * 128))]


def kernel(**inputs):
    import concourse.bacc as bacc
    from concourse.bass_utils import run_bass_kernel_spmd

    nc = bacc.Bacc("TRN2", target_bir_lowering=False, num_devices=1)
    arrays, dr = {}, {}
    for name in INS:
        arrays[name] = np.ascontiguousarray(inputs[name])
        dr[name] = nc.dram_tensor(name, arrays[name].shape, F32, kind="ExternalInput").ap()
    for name, shape in OUTS:
        dr[name] = nc.dram_tensor(name, shape, F32, kind="ExternalOutput").ap()
    for name, shape in SCRATCH.items():
        dr[name] = nc.dram_tensor(name, shape, F32, kind="Internal").ap()
    build(nc, dr)
    got = run_bass_kernel_spmd(nc, [arrays], core_ids=[0]).results[0]
    return tuple(got[name] for name, _ in OUTS)
```

```python
from contextlib import ExitStack
import math

import numpy as np
import concourse.bass as bass
import concourse.mybir as mybir
from concourse.alu_op_type import AluOpType as ALU

F32 = mybir.dt.float32
BF16 = mybir.dt.bfloat16
U32 = mybir.dt.uint32
ACT = mybir.ActivationFunctionType
AX = mybir.AxisListType

D, SEQ, NB, LS = 1024, 512, 8, 8
NS = NB * LS
N = SEQ + NS
TILES = SEQ // 128 + 1
PT = TILES - 1
KD = D // 128
DA, DB = 512, 512
HA, DHA = 4, 128
HB, DHB = 8, 64
NJ = DB // 128
DA_IN = 4 * DA + 2 * HA
NE, EG, NG, DE = 16, 4, 4, 512
ALPHA = 2 ** 0.25
SQRT_E = math.exp(-0.5)
NEG = -1e30
CW = 4
CAP = 128
SCRATCH = {"x_kept": (N, D), "x1_rows": (N, D), "y_slots": (NE * CAP, D)}


def rows(i):
    return 128 if i < PT else NS


def cols(i):
    return slice(128 * i, 128 * i + rows(i))


def build(nc, dr, stage=9):
    with ExitStack() as ctx:
        def sem(name):
            return ctx.enter_context(nc.semaphore(name))

        arena = ctx.enter_context(nc.sbuf_tensor("arena", [128, 53200], F32))
        bank = [ctx.enter_context(nc.psum_tensor(f"bank{i}", [128, 512], F32)) for i in range(8)]
        ends = {}

        class Region:
            def __init__(self, at, size):
                self.at, self.end = at, at + size

            def __call__(self, *dims):
                n = int(np.prod(dims))
                ap = arena[:, self.at:self.at + n]
                self.at += n
                assert self.at <= self.end, (self.at, self.end)
                if len(dims) == 2:
                    ap = ap.rearrange("p (a b) -> p a b", a=dims[0])
                if len(dims) == 3:
                    ap = ap.rearrange("p (a b c) -> p a b c", a=dims[0], b=dims[1])
                return ap

        KEEP, T1, T2 = 26800, 13300, 10800
        keep = Region(0, KEEP)
        ident = keep(128)
        blockones = keep(128)
        neg_p = keep(128)
        neg_s = keep(64)
        tri_p = keep(2, 128)
        tri_s = keep(2, 64)
        lvl = keep(7, 128)
        resets = keep(N)
        sel = keep(HA, 128)
        headsel = keep(2)
        seqmask = keep(NB)
        NPRM = 74
        prmc = keep(NPRM)
        shiftc = keep(14, NB)
        convc = keep(8, NB * 3)
        ncol = keep(NB * HA)
        dprm = keep(24)
        gn_a, lnx_g, lnx_b = keep(DA), keep(DB), keep(DB)
        hg = keep(TILES, D)
        arr = keep(NJ, 2, N)
        nbeta = keep(NJ, N)
        kap = keep(NJ, N)
        vtok = keep(TILES, DB)
        sgl = keep(N)
        g2w = keep(DB)
        bon = keep(TILES, HB)
        S = keep(NJ, 128)
        Sh = keep(NJ, 128)
        shnew = keep(NB + 1, 14)
        cvnew = keep(NB + 1, 3, 8)
        nnew = keep(NB + 1, HA)
        rbm = keep(N)
        wint = keep(N)
        woldb = keep(HA, 12)
        colg = keep(3, TILES, HA)
        em = keep(NJ, PT)
        ec = keep(NJ, 12)
        lmid = keep(NJ, PT)
        pend = keep(NJ, PT)
        mrow = keep(12)
        outs = keep(5, 128)
        mv = keep(TILES, 2)
        st6 = keep(2, 6)
        rstd = keep(TILES)
        prow = keep(128)
        ln_g = arena[:, arr_off(arr):arr_off(arr) + D]
        ln_b = arena[:, arr_off(arr) + D:arr_off(arr) + 2 * D]
        x = hg

        t1 = Region(KEEP, T1)
        raw = [t1(604) for _ in range(2)]
        t1_after_raw = t1.at
        wlal = t1(N)
        w2a2 = t1(DB)
        dt = t1(585)
        r_, kr, vr, ld, a_, L, E1, E2, E3, kk, tmp, sq, nrm, kr2 = (t1(N) for _ in range(14))
        g = Region(t1_after_raw + N + DB + 585, T1)
        shrows, cvrows, nrows = g(14, 128), g(8, 128), g(128)
        g = Region(t1_after_raw + N + DB + 585 + 14 * 128, T1)
        LI, LF, bb, mm, d0, d1, wsr, emt, ta_, tb_ = (g(N) for _ in range(10))
        m0r, mprev, blast, mlast, wold = g(8), g(12), g(12), g(12), g(12)
        gbias, gtok, gw = keep(8), keep(TILES, 8), g(8, 8)
        assert g.at <= KEEP + T1

        b = Region(t1_after_raw, T1 - 1208)
        zc, th = b(604), b(604)
        qT, kT = [b(N) for _ in range(2)], [b(N) for _ in range(2)]
        qt = b(N)
        kw, dm, sT = b(TILES, 128), b(TILES, 128), b(TILES, 128)
        C = b(129)
        C0 = b(NB, 129)
        qpad = b(NB, NS)
        vpad = b(NB, 129)
        hh = b(TILES, 129)
        den, rec = b(TILES), b(TILES)
        vext = b(TILES, HA, 129)
        c = Region(KEEP, T1)
        xwm = c.at
        X = [c(4, 128) for _ in range(2)]
        W = [c(4, 128) for _ in range(2)]
        MT = [c(4, 128) for _ in range(2)]
        p = Region(xwm, 3072)
        arpad = p(2, NB, NS)
        kppad = [p(2, NB, 64) for _ in range(2)]
        kpt = [c(2, DB) for _ in range(2)]
        ktmp = c(2, NJ, 128)
        Zs, Us = c(DB), c(DB)
        Sld = c(NJ, NB, 64)
        pS = c(NJ, 64)
        gtk = c(DB)
        ssum, sqs = c(HB), c(HB)
        t2 = Region(KEEP + T1, T2)
        xT = t2(KD, N)
        NW = 6
        wring = t2(NW, KD, 128)
        c = Region(KEEP + T1, T2)
        G = [c(2, HB, 256) for _ in range(2)]
        Y = [c(HB, 128) for _ in range(2)]
        SsT = Region(arr_off(G[1]), 4096)(NJ, NB, 128)
        o = Region(KEEP, T1)
        xln = o(TILES, D)
        l1g, l1b, l2g, l2b = o(D), o(D), o(D), o(D)
        wrt = o(KD, NE)
        wout = arena[:, arr_off(arr):arr_off(arr) + KD * D].rearrange("p (a b) -> p a b", a=KD)
        hT = Region(arr_off(arr) + KD * D, KD * N)(KD, N)
        x1T = Region(arr_off(hg), TILES * D)(KD, N)
        e = Region(o.at, KEEP + T1 - o.at)
        probs, sl, gate, s01, inb = (e(TILES, NE) for _ in range(5))
        gmax, gsum, gtop = e(TILES, NG), e(TILES, NG), e(TILES, NG)
        t80a, t80b, brr = e(TILES, NE), e(TILES, NE), e(NE)
        one5, slotA, slotB, gA, gB = (e(TILES) for _ in range(5))
        slotAu, slotBu = (e(TILES).bitcast(U32) for _ in range(2))
        idxf, idxu, flagf, flagu = e(NE), e(NE).bitcast(U32), e(1), e(1).bitcast(U32)
        slot0 = keep(NE)
        places = keep(CAP)
        ones = keep(128)
        tokid = keep(TILES).bitcast(BF16).rearrange("p (i c) -> p i c", c=2)
        onehot = [e(NE * CAP // 2).bitcast(BF16).rearrange("p (e c) -> p e c", e=NE) for _ in range(1)]
        e = Region(arr_off(l1g), 2 * D)
        ysb = [e(D) for _ in range(2)]
        e = Region(arr_off(hg), TILES * D)
        xs = [e(D) for _ in range(2)]
        xsT = [e(KD, CAP) for _ in range(2)]
        NF = DE // 128
        hsl, hid = e(2, CAP), e(NF, CAP)
        wexp = []
        for at in (KEEP + T1, arr_off(arr)):
            w = Region(at, 12288)
            wexp.append((w(KD, DE), w(KD, DE), w(NF, D)))
        e = Region(arr_off(arr), 12288)
        ya = [(e(D), e(D)) for _ in range(2)]
        e = Region(KEEP + T1, 12288)
        dx, dxT = e(TILES, D), e(KD, N)
        dhs, dgc = e(N), e(TILES)
        e = Region(arr_off(hg), TILES * D)
        dhid = e(NF, N)
        dw = wexp[1]

        class Sems(dict):
            def __missing__(self, name):
                self[name] = ctx.enter_context(nc.semaphore(name))
                return self[name]

        q_ = Sems()
        x_loaded = [q_[f"x_loaded{i}"] for i in range(TILES)]
        w_loaded = [q_[f"w_loaded{i}"] for i in range(NW)]
        wgu_loaded, wd_loaded = w_loaded[0:2], w_loaded[2:4]
        xs_loaded = [q_[f"rows_gathered{i}"] for i in range(2)]
        ya_loaded = xs_loaded
        block = ctx.enter_context(nc.Block())

        def wcol(n):
            if n < 2:
                return DA_IN + 3 * DB + 128 * n
            if n < 14:
                return DA_IN + DB * ((n - 2) % 3) + 128 * ((n - 2) // 3)
            if n < 22:
                return 2 * DA + 128 * (n - 14)
            return DA * ((n - 22) % 2) + 128 * ((n - 22) // 2)

        def shift_tile(n):
            return 12 + n if n < 2 else 4 * ((n - 2) % 3) + (n - 2) // 3

        SLOTS = 30
        W0 = 16 * (SLOTS // NW)

        def LV(i):
            return 7 if i < PT else 3

        def ix(i, l, q):
            return 14 * i + 2 * l + q

        def ix2(i, l, q):
            return 12 * i + 2 * (l - 1) + q

        def hooks(i, l):
            return ("Z", "U", "O", "G")[l - (1 if i < PT else 0)] if i and 0 <= l - (1 if i < PT else 0) < 4 else None
        MU, CWR, CBR, KKR, KAR, W0R, A0R, RKR = 0, 14, 46, 54, 58, 62, 66, 70
        HW0, HA0, OMKA = 0, 4, 8
        UNITS = PT + 1

        def P(n):
            return prmc[:, n:n + 1]

        def pr(ap):
            return ap[:, 0:SEQ].rearrange("p (c t) -> p c t", c=PT)

        def sa(ap):
            return ap[:, SEQ:N].rearrange("p (b t) -> p b t", b=NB)

        def wide(ap, n):
            return ap.unsqueeze(2).to_broadcast([ap.shape[0], ap.shape[1], n])

        @block.sync
        def _(sp):
            for k, (name, at) in enumerate((("mu_shift", MU), ("conv_w", CWR), ("conv_b", CBR), ("k_k", KKR),
                                            ("k_a", KAR), ("w0", W0R), ("a0", A0R), ("r_k", RKR))):
                src = dr[name]
                n = int(np.prod(src.shape)) // 128
                sp.dma_start(prow[at:at + n, :], flat(src, n)).then_inc(q_["prm_loaded"], 16)
            for i in range(TILES):
                src = dr["x_prompt"][0, 128 * i:128 * i + 128, :] if i < PT else dr["x_sample"].rearrange("b t d -> (b t) d")
                sp.dma_start(x[0:rows(i), i, :], src).then_inc(x_loaded[i], 16)
                if i == 0:
                    for ap, name in ((ln_g, "ln0_g"), (ln_b, "ln0_b")):
                        sp.dma_start(ap, brow(dr[name], D)).then_inc(q_["ln0_loaded"], 16)
            sp.dma_start(shrows[0:NB, :, :], dr["state_rwkv_shift"][0].rearrange("b (a f) -> b a f", f=128)).then_inc(q_["hist_loaded"], 16)
            sp.dma_start(cvrows[0:24, :, :], dr["state_mlstm_conv"][0].rearrange("b w (a f) -> (b w) a f", f=128)).then_inc(q_["hist_loaded"], 16)
            sp.dma_start(nrows[0:NB * HA, :], dr["state_mlstm_n"][0].rearrange("b h d -> (b h) d")).then_inc(q_["hist_loaded"], 16)
            sp.dma_start(gw, dr["w_in"][0, :, 4 * DA:DA_IN].rearrange("(k p) c -> p k c", p=128)).then_inc(q_["gate_loaded"], 16)
            sp.dma_start(gbias[:, 0:HA], brow(dr["b_i"][0], HA)).then_inc(q_["gate_loaded"], 16)
            sp.dma_start(gbias[:, HA:8], brow(dr["b_f"][0], HA)).then_inc(q_["gate_loaded"], 16)
            sp.dma_start(m0r[0:HA, :], dr["state_mlstm_m"][0].rearrange("b h -> h b"), allow_slow_non_contiguous=True).then_inc(q_["gate_loaded"], 16)
            for n in range(SLOTS):
                if n >= NW:
                    sp.wait_ge(q_["slot_projected"], n - NW + 1)
                c = wcol(n)
                sp.dma_start(wring[:, n % NW, :, :], dr["w_in"][0, :, c:c + 128].rearrange("(k p) c -> p k c", p=128)).then_inc(w_loaded[n % NW], 16)
                if n == 5:
                    sp.wait_ge(q_["ln0_done"], TILES)
                    for i in range(TILES):
                        sp.dma_start(dr["x_kept"][128 * i:128 * i + rows(i), :], x[0:rows(i), i, :]).then_inc(q_["x_kept"], 16)
                if n == 1:
                    sp.dma_start(w2a2[0:64, :], dr["w2"][0]).then_inc(q_["gn_loaded"], 16)
                    sp.dma_start(w2a2[64:128, :], dr["a2"][0]).then_inc(q_["gn_loaded"], 16)
                    sp.dma_start(g2w, dr["g2"][0]).then_inc(q_["gn_loaded"], 16)
                    for ap, name, w in ((gn_a, "gn_a_g", DA), (lnx_g, "lnx_g", DB), (lnx_b, "lnx_b", DB)):
                        sp.dma_start(ap, brow(dr[name][0], w)).then_inc(q_["gn_loaded"], 16)

            stored = 0

            def store(dst, src, **kw):
                nonlocal stored
                stored += 1
                sp.dma_start(dst, src, **kw).then_inc(q_["stored"], 16)

            sp.wait_ge(q_["outs_ready"], 1)
            store(dr["s_shift"][0].rearrange("b (t f) -> (b t) f", f=128), outs[0:112, 0, :])
            store(dr["p_shift"][0].rearrange("b (t f) -> (b t) f", f=128), outs[112:126, 0, :])
            sc = dr["s_conv"][0].rearrange("b w (c f) -> (b w c) f", f=128)
            store(sc[0:96], outs[0:96, 1, :])
            store(sc[96:192], outs[0:96, 2, :])
            store(dr["p_conv"][0, 0].rearrange("w (c f) -> (w c) f", f=128), outs[0:24, 3, :])
            store(dr["s_n"][0].rearrange("b h d -> (b h) d"), outs[0:32, 4, :])
            store(dr["p_n"][0, 0], outs[32:36, 4, :])
            store(dr["p_m"][0].rearrange("b h -> h b"), mrow[0:HA, 3:4], allow_slow_non_contiguous=True)
            store(dr["s_m"][0].rearrange("b h -> h b"), mrow[0:HA, 4:12], allow_slow_non_contiguous=True)
            sp.wait_ge(q_["ktmp_made"], 1)
            sp.wait_ge(q_["unit_projected"], HA)
            sp.wait_ge(q_["ha_done"], HA)
            for h in range(HB):
                sp.dma_start(Sld[64 * (h % 2):64 * (h % 2) + 64, h // 2, :, :], dr["state_rwkv_S"][0, :, h].rearrange("b v k -> v b k")).then_inc(q_["sst_loaded"], 16)
            sp.wait_ge(q_["pads_made"], NJ)
            sp.wait_ge(q_["grams"], 4 * TILES)
            sp.wait_ge(q_["ktmp_made"], TILES)
            sp.dma_start(wout, dr["w_out"][0].rearrange("(k p) c -> p k c", p=128)).then_inc(q_["wout_loaded"], 16)
            sp.wait_ge(q_["ps_ready"], 1)
            store(dr["p_S"][0, 0].rearrange("(j h) v k -> (h v) j k", h=2), pS)
            for h in range(HB):
                sp.wait_ge(q_["ss_read"], h + 1)
                store(dr["s_S"][0, :, h].rearrange("b v k -> v b k"), Sld[64 * (h % 2):64 * (h % 2) + 64, h // 2, :, :])
            sp.wait_ge(q_["stored"], 16 * stored)
            sp.wait_ge(q_["hb_done"], TILES)
            sp.wait_ge(q_["x_kept"], 16 * TILES)
            for i in range(TILES):
                sp.dma_start(xln[0:rows(i), i, :], dr["x_kept"][128 * i:128 * i + rows(i), :]).then_inc(q_["x_back"], 16)
            for ap, src, w in ((l1g, dr["ln1_g"][0], D), (l1b, dr["ln1_b"][0], D), (l2g, dr["ln2_g"][0], D), (l2b, dr["ln2_b"][0], D), (brr, dr["b_router"], NE)):
                sp.dma_start(ap, brow(src, w)).then_inc(q_["x_back"], 16)
            sp.dma_start(wrt, dr["w_router"].rearrange("(k p) c -> p k c", p=128)).then_inc(q_["x_back"], 16)
            for i in range(TILES):
                sp.wait_ge(q_["ln1_done"], i + 1)
                sp.dma_start(dr["x1_rows"][128 * i:128 * i + rows(i), :], xln[0:rows(i), i, :]).then_inc(q_["x1_stored"], 16)
            sp.wait_ge(q_["mix_projected"], TILES)
            def expert_w(e_, p_):
                wg, wu, wd = wexp[p_]
                for w, name in ((wg, "we_gate"), (wu, "we_up")):
                    sp.dma_start(w, dr[name][0, bass.ds(e_, 1)].rearrange("a (k p) c -> p (a k) c", p=128)).then_inc(wgu_loaded[p_], 16)
                return lambda: sp.dma_start(wd, dr["we_down"][0, bass.ds(e_, 1)].rearrange("a (k p) c -> p (a k) c", p=128)).then_inc(wd_loaded[p_], 16)

            expert_w(0, 0)()
            expert_w(1, 1)()
            with sp.Fori(0, NE // 2 - 1) as it:
                for p_ in range(2):
                    sp.wait_ge(q_["hidden"], 4 * it + 2 * p_ + 2)
                    down = expert_w(2 * it + 2 + p_, p_)
                    sp.wait_ge(q_["down"], 2 * it + p_ + 1)
                    down()
            sp.wait_ge(q_["combined"], TILES)
            over = sp.value_load(flagu[0:1, 0:1], min_val=0, max_val=1)
            with sp.If(over):
                sp.wait_ge(q_["down"], NE)
                for i in range(TILES):
                    sp.dma_start(dx[0:rows(i), i, :], dr["x1_rows"][128 * i:128 * i + rows(i), :]).then_inc(q_["all_x"], 16)
                with sp.Fori(0, NE) as it:
                    sp.wait_ge(q_["all_down"], TILES * it)
                    for w, name in zip(dw, ("we_gate", "we_up", "we_down")):
                        sp.dma_start(w, dr[name][0, bass.ds(it, 1)].rearrange("a (k p) c -> p (a k) c", p=128)).then_inc(q_["all_w"], 16)
            for i in range(TILES):
                sp.wait_ge(q_["y_ready"], i + 1)
                dst = dr["y_prompt"][0, 128 * i:128 * i + 128, :] if i < PT else dr["y_sample"].rearrange("b t d -> (b t) d")
                store(dst, xln[0:rows(i), i, :])
            sp.wait_ge(q_["stored"], 16 * stored)
            sp.wait_ge(q_["cs_stored"], 32 * HA)

        @block.gpsimd
        def _(pool):
            step = [0]

            def link(ins):
                step[0] += 1
                ins.then_inc(q_["pool_step"], 1)
                pool.wait_ge(q_["pool_step"], step[0])

            def keep_where(ap, pattern, base, cm, op=ALU.is_ge, fill=0.0):
                link(pool.affine_select(out=ap, in_=ap, pattern=pattern, compare_op=op, fill=fill, base=base,
                                        channel_multiplier=cm))

            link(pool.memset(ident, 0.0))
            keep_where(ident, [[-1, 128]], 0, 1, ALU.not_equal, 1.0)
            pool.nop().then_inc(q_["ident_ready"], 1)
            for ap in (raw[0], raw[1]):
                link(pool.memset(ap, 0.0))
            link(pool.memset(resets, 1.0))
            link(pool.memset(resets[:, 0:SEQ:128], 0.0))
            link(pool.memset(resets[:, SEQ:N:LS], 0.0))
            link(pool.memset(sel[0:HA], 0.0))
            keep_where(sel[0:HA], [[-1, HA], [0, 128]], 0, 1, ALU.not_equal, 1.0)
            bo = blockones.rearrange("p (a b) -> p a b", a=2)
            link(pool.memset(blockones, 1.0))
            keep_where(bo, [[-64, 2], [0, 64]], 0, 1)
            keep_where(bo, [[64, 2], [0, 64]], 63, -1)
            link(pool.memset(headsel, 1.0))
            keep_where(headsel, [[-64, 2]], 0, 1)
            keep_where(headsel, [[64, 2]], 63, -1)
            link(pool.memset(seqmask, 1.0))
            keep_where(seqmask, [[-LS, NB]], 0, 1)
            keep_where(seqmask, [[LS, NB]], LS - 1, -1)
            link(pool.memset(neg_p, 0.0))
            keep_where(neg_p, [[1, 128]], 0, -1, fill=NEG)
            link(pool.memset(neg_s, 0.0))
            keep_where(neg_s, [[1, NS]], 0, -1, fill=NEG)
            keep_where(neg_s.rearrange("p (b t) -> p b t", b=NB), [[-LS, NB], [0, LS]], 0, 1, fill=NEG)
            keep_where(neg_s.rearrange("p (b t) -> p b t", b=NB), [[LS, NB], [0, LS]], LS - 1, -1, fill=NEG)
            link(pool.memset(tri_p, 1.0))
            link(pool.memset(tri_s, 1.0))
            for tri, n in ((tri_p, 128), (tri_s, NS)):
                keep_where(tri[:, 0, :], [[1, n]], 0, -1, ALU.is_gt)
                keep_where(tri[:, 1, :], [[1, n]], 0, -1)
            for v in range(2):
                ts = tri_s[:, v, :].rearrange("p (b t) -> p b t", b=NB)
                keep_where(ts, [[-LS, NB], [0, LS]], 0, 1)
                keep_where(ts, [[LS, NB], [0, LS]], LS - 1, -1)
            link(pool.memset(lvl, 0.0))
            for l in range(7):
                m = 2 ** l
                up = lvl[:, l, :].rearrange("p (a c b) -> p a c b", c=2, b=m)[:, :, 1, :]
                link(pool.memset(up, 1.0))
                keep_where(up, [[-2 * m, 64 // m], [0, m]], 0, 1)
                keep_where(up, [[2 * m, 64 // m], [0, m]], m - 1, -1)
            link(pool.memset(ones, 1.0))
            link(pool.iota(slot0, [[CAP, NE]], base=1, channel_multiplier=0, allow_small_or_imprecise_dtypes=True))
            link(pool.iota(places, [[1, CAP]], base=0, channel_multiplier=0, allow_small_or_imprecise_dtypes=True))
            link(pool.iota(tokid[:, :, 0], [[0, TILES]], base=0, channel_multiplier=1, allow_small_or_imprecise_dtypes=True))
            link(pool.iota(tokid[:, :, 1], [[1, TILES]], base=0, channel_multiplier=0, allow_small_or_imprecise_dtypes=True))
            pool.nop().then_inc(q_["masks_ready"], 1)

            def collect(n, k):
                pool.wait_ge(q_["slot_read"], n + 1)
                rw = raw[k % 2]
                if n < 14:
                    t = shift_tile(n)
                    pool.tensor_copy(shnew[:, NB, t:t + 1], rw[:, SEQ:SEQ + 1])
                    pool.tensor_copy(shnew[:, 0:NB, t], rw[:, 513:585].rearrange("p (b t) -> p b t", b=NB)[:, :, LS]).then_inc(q_["raw_collected"], 1)
                else:
                    c = 4 * ((n - 22) % 2) + (n - 22) // 2
                    pool.tensor_copy(cvnew[:, NB, :, c], rw[:, SEQ:SEQ + 3])
                    pool.tensor_copy(cvnew[:, 0:NB, :, c], rw[:, 515:603].rearrange("p (b t) -> p b t", b=NB)[:, :, LS:LS + 3]).then_inc(q_["raw_collected"], 1)

            def mlstm_io(h):
                pool.wait_ge(q_["cs_new"], h + 1)
                pool.dma_start(dr["s_C"][0, :, h].rearrange("b d e -> d b e"), C0[:, :, 0:128]).then_inc(q_["cs_stored"], 16)
                pool.wait_ge(q_["c_state"], PT * (h + 1))
                pool.dma_start(dr["p_C"][0, 0, h], C[:, 0:128]).then_inc(q_["cs_stored"], 16)
                if h < HA - 1:
                    pool.wait_ge(q_["cs_stored"], 32 * (h + 1))
                    pool.dma_start(C0[:, :, 0:128], dr["state_mlstm_C"][0, :, h + 1].rearrange("b d e -> d b e")).then_inc(q_["c0_loaded"], 16)

            for n in range(14):
                collect(n, n)
            pool.wait_ge(q_["rwkv_made"], NJ)
            pool.wait_ge(q_["post_projected"], NJ)
            pool.dma_start(C0[:, :, 0:128], dr["state_mlstm_C"][0, :, 0].rearrange("b d e -> d b e")).then_inc(q_["c0_loaded"], 16)
            pool.memset(vext[:, :, :, 128:129], 1.0).then_inc(q_["ones_set"], 1)
            pool.memset(qpad, 0.0).then_inc(q_["ones_set"], 1)
            collect(22, 14)
            collect(23, 15)
            for h in range(HA):
                if h < HA - 1:
                    collect(24 + 2 * h, 16 + 2 * h)
                    collect(25 + 2 * h, 17 + 2 * h)
                mlstm_io(h)


            pool.wait_ge(q_["ec_ready"], 1)
            pool.wait_ge(q_["unit_projected"], HA)
            pool.wait_ge(q_["ha_done"], HA)
            pool.wait_ge(q_["cs_stored"], 32 * HA)
            for i in range(TILES):
                n = rows(i)
                if i:
                    pool.wait_ge(q_["kt_turned"], i)
                for w, src in enumerate((nbeta, kap)):
                    if i < PT:
                        ins = pool.tensor_tensor(ktmp[:, w, :, :], src[:, :, cols(i)], wide(ec[:, :, i], 128), ALU.mult)
                    else:
                        for j in range(NJ):
                            ins = pool.tensor_tensor(ktmp[:, w, j, 0:NS].rearrange("p (b t) -> p b t", b=NB), sa(src[:, j, :]), wide(ec[:, j, 4:12], LS), ALU.mult)
                ins.then_inc(q_["ktmp_made"], 1)
                for l in range(LV(i)):
                    for q in range(2):
                        k = ix(i, l, q)
                        if l == 0:
                            pool.wait_ge(q_["gram_read"], 4 * i + 2 * q + 1)
                        if k >= 2:
                            pool.wait_ge(q_["w_projected"], k - 1)
                        if l == 1:
                            pool.wait_ge(q_["yx_read"], k - 1)
                        pool.tensor_tensor(MT[q][0:n, :, 0:n], G[i % 2][0:n, 0, 4 * q:4 * q + 4, 0:n],
                                           lvl[0:n, l, 0:n].unsqueeze(1).to_broadcast([n, 4, n]), ALU.mult).then_inc(q_["mt_ready"], 1)
            pool.wait_ge(q_["o_projected"], PT)
            link(pool.memset(SsT, 0.0))
            pool.wait_ge(q_["yx_read"], ix(PT, 2, 1) + 1)
            pool.wait_ge(q_["w_projected"], ix(PT, 2, 1) + 1)
            pool.wait_ge(q_["yx_projected"], ix2(PT, 2, 1) + 1)
            link(pool.memset(arpad, 0.0))
            pool.nop().then_inc(q_["sst_zero"], 1)
            for h in range(HB):
                if h == 0:
                    pool.wait_ge(q_["kt_read"], TILES)
                if h >= 2:
                    pool.wait_ge(q_["ss_projected"], h - 1)
                for w in range(2):
                    ins = pool.tensor_tensor(kppad[h % 2][0:NS, w], kpt[PT % 2][0:NS, w, 64 * h:64 * h + 64].unsqueeze(1).to_broadcast([NS, NB, 64]),
                                             seqmask[0:NS].unsqueeze(2).to_broadcast([NS, NB, 64]), ALU.mult)
                ins.then_inc(q_["kp_spread"], 1)


            pool.wait_ge(q_["routing"], 3)
            pool.wait_ge(q_["x1_stored"], 16 * TILES)
            for e_ in range(NE + 1):
                if e_ >= 2:
                    pool.wait_ge(q_["xs_turned"], e_ - 1)
                else:
                    pool.wait_ge(q_["routed"], 1)
                pool.indirect_dma_start(out=xs[e_ % 2], out_offset=None, in_=dr["x1_rows"], in_offset=bass.IndirectOffsetOnAxis(ap=idxu[:, e_ % NE:e_ % NE + 1], axis=0)).then_inc(xs_loaded[e_ % 2], 16)
            pool.wait_ge(q_["y_stored"], 16 * NE)
            pool.wait_ge(q_["slots_ready"], 1)
            for i in range(TILES):
                n = rows(i)
                if i >= 2:
                    pool.wait_ge(q_["combined"], i - 1)
                for dst, ix_ in zip(ya[i % 2], (slotAu, slotBu)):
                    pool.indirect_dma_start(out=dst[0:n], out_offset=None, in_=dr["y_slots"], in_offset=bass.IndirectOffsetOnAxis(ap=ix_[0:n, i:i + 1], axis=0)).then_inc(ya_loaded[i % 2], 16)

        @block.scalar
        def _(act):
            step = [0]

            def link(ins):
                step[0] += 1
                ins.then_inc(q_["act_step"], 1)
                act.wait_ge(q_["act_step"], step[0])

            act.wait_ge(q_["x_moments"], 1)
            act.activation(rstd, mv[:, :, 1], ACT.Sqrt).then_inc(q_["x_std"], 1)
            for i in range(TILES):
                act.wait_ge(q_["x_turned"], i + 1)
                for q in range(2):
                    v = bank[2 * (i % 2) + q].rearrange("p (a b) -> p a b", a=4)[:, :, 0:rows(i)]
                    ins = act.copy(xT[:, 4 * q:4 * q + 4, cols(i)], v)
                ins.then_inc(q_["xt_ready"], 1)

            def to_raw(n, k):
                act.wait_ge(q_["slot_projected"], n + 1)
                if k >= 2:
                    act.wait_ge(q_["raw_used"], k - 1)
                    act.wait_ge(q_["raw_collected"], k - 1)
                elif k == 0:
                    act.wait_ge(q_["masks_ready"], 1)
                    act.wait_ge(q_["cols_ready"], 1)
                rw, A, B = raw[k % 2], bank[2 * (n % 2)], bank[2 * (n % 2) + 1]
                if n < 14:
                    sv = rw[:, 513:585].rearrange("p (b t) -> p b t", b=NB)
                    act.copy(sv[:, :, 0], shiftc[:, shift_tile(n), :])
                    act.copy(rw[:, 1:513], A[:, :])
                    act.copy(sv[:, :, 1:9], B[:, 0:NS].rearrange("p (b t) -> p b t", b=NB)).then_inc(q_["slot_read"], 1)
                else:
                    sv = rw[:, 515:603].rearrange("p (b t) -> p b t", b=NB)
                    c = 4 * ((n - 22) % 2) + (n - 22) // 2
                    if k < 16:
                        act.copy(rw[:, 0:3], resets[:, 0:SEQ:128][:, 0:3])
                    act.copy(sv[:, :, 0:3], convc[:, c, :].rearrange("p (b w) -> p b w", b=NB))
                    act.copy(rw[:, 3:515], A[:, :])
                    act.copy(sv[:, :, 3:11], B[:, 0:NS].rearrange("p (b t) -> p b t", b=NB)).then_inc(q_["slot_read"], 1)

            to_raw(0, 0)
            act.wait_ge(q_["gate_steps"], 3)
            act.activation(ta_[0:HA, :], ta_[0:HA, :], ACT.Exp).then_inc(q_["gate_exps"], 1)
            act.wait_ge(q_["gate_steps"], 4)
            act.activation(tb_[0:HA, :], ta_[0:HA, :], ACT.Ln).then_inc(q_["gate_exps"], 1)
            to_raw(1, 1)
            act.wait_ge(q_["gate_steps"], 5)
            act.activation(wint[0:HA, :], wint[0:HA, :], ACT.Exp)
            act.activation(wsr[0:HA, :], wsr[0:HA, :], ACT.Exp)
            act.activation(emt[0:HA, :], mm[0:HA, :], ACT.Exp, scale=-1.0)
            act.activation(wold[0:HA, :], wold[0:HA, :], ACT.Exp).then_inc(q_["gate_exps"], 1)
            act.wait_ge(q_["gates_on_pe"], 4)
            for a in range(3):
                act.copy(colg[:, a, 0:PT, :], bank[5][:, 20 * a:20 * a + 16].rearrange("p (i h) -> p i h", h=HA))
                act.copy(colg[0:NS, a, PT, :], bank[5][0:NS, 20 * a + 16:20 * a + 20])
            act.copy(woldb, bank[5][:, 64:112].rearrange("p (h c) -> p h c", h=HA)).then_inc(q_["gate_exps"], 1)
            act.wait_ge(q_["shifted"], 2)
            act.activation(wlal[0:64, :], wlal[0:64, :], ACT.Tanh)
            act.activation(sgl, sgl, ACT.Tanh, scale=0.5).then_inc(q_["lora_in"], 1)

            def exps(j):
                act.wait_ge(q_["decay_args"], j + 1)
                act.activation(E1, tmp, ACT.Exp)
                act.activation(E2, L, ACT.Exp)
                act.activation(E3, L, ACT.Exp, scale=-1.0)
                act.activation(em[:, j, :], lmid[:, j, :], ACT.Exp).then_inc(q_["decays"], 1)

            def post(j):
                act.wait_ge(q_["post_projected"], j + 1)
                act.copy(bon[:, 0:PT, 2 * j:2 * j + 2], bank[7][:, 0:8].rearrange("p (i h) -> p i h", h=2))
                act.copy(bon[0:NS, PT, 2 * j:2 * j + 2], bank[7][0:NS, 8:10])
                act.copy(vtok[:, 0:PT, 128 * j:128 * j + 128], bank[6].rearrange("p (i f) -> p i f", i=PT))
                act.copy(vtok[0:NS, PT, 128 * j:128 * j + 128], bank[7][0:NS, 128:256]).then_inc(q_["post_read"], 1)

            for j in range(NJ):
                to_raw(2 + 3 * j, 2 + 3 * j)
                to_raw(3 + 3 * j, 3 + 3 * j)
                if j:
                    post(j - 1)
                act.wait_ge(q_["lora_projected"], j + 1)
                if j:
                    act.wait_ge(q_["rwkv_made"], j)
                for dst, A, B, hb in ((ld, bank[4], bank[5][:, 0:NS], HW0), (a_, bank[6], bank[7][:, 256:256 + NS], HA0)):
                    act.activation(dst[:, 0:SEQ], A[:, :], ACT.Tanh, bias=dprm[:, hb + j:hb + j + 1], scale=0.5)
                    ins = act.activation(dst[:, SEQ:N], B, ACT.Tanh, bias=dprm[:, hb + j:hb + j + 1], scale=0.5)
                ins.then_inc(q_["tanhs"], 1)
                to_raw(4 + 3 * j, 4 + 3 * j)
                exps(j)
                act.wait_ge(q_["norms_projected"], j + 1)
                act.activation(nrm[:, 0:SEQ], bank[4][:, :], ACT.Sqrt)
                act.activation(nrm[:, SEQ:N], bank[5][:, 0:NS], ACT.Sqrt).then_inc(q_["norms"], 1)
            act.wait_ge(q_["rwkv_made"], NJ)
            for n in range(14, 22):
                act.wait_ge(q_["slot_projected"], n + 1)
                h = (n - 14) % 4
                A, B = bank[2 * (n % 2)].rearrange("p (i f) -> p i f", i=PT), bank[2 * (n % 2) + 1][0:NS, 0:128]
                if n < 18:
                    act.copy(vext[:, 0:PT, h, 0:128], A)
                    act.copy(vext[0:NS, PT, h, 0:128], B).then_inc(q_["slot_read"], 1)
                else:
                    act.activation(hg[:, 0:PT, 128 * h:128 * h + 128], A, ACT.Tanh, scale=0.5)
                    act.activation(hg[0:NS, PT, 128 * h:128 * h + 128], B, ACT.Tanh, scale=0.5).then_inc(q_["slot_read"], 1)
                if n == 14:
                    post(NJ - 1)

            def silu_tanh(k):
                act.wait_ge(q_["raw_used"], 15 + k)
                act.activation(th, zc, ACT.Tanh, scale=0.5).then_inc(q_["silu_tanh"], 1)

            def unit(h):
                act.wait_ge(q_["k_turned"], h + 1)
                if h:
                    act.wait_ge(q_["unit_projected"], h)
                for i in range(TILES):
                    n = rows(i)
                    src = bank[6][:, 128 * i:128 * i + 128] if i < PT else bank[7][0:NS, 0:128]
                    ins = act.activation(kw[0:n, i, :], src, ACT.Copy, scale=colg[0:n, 1, i, h:h + 1])
                ins.then_inc(q_["k_tokens"], 1)
                act.wait_ge(q_["scores"], h + 1)
                for i in range(TILES):
                    n = rows(i)
                    src = bank[6][:, 128 * i:128 * i + 128] if i < PT else bank[7][0:NS, 128:192]
                    ins = act.activation(dm[0:n, i, 0:n], src, ACT.Exp, bias=colg[0:n, 0, i, h:h + 1])
                ins.then_inc(q_["weights"], 1)
                for i in range(TILES):
                    act.wait_ge(q_["numerator"], TILES * h + i + 1)
                    if h and i == 0:
                        act.wait_ge(q_["ha_done"], h)
                    act.copy(hh[0:rows(i), i, :], bank[4 + i % 2][0:rows(i), 128:257]).then_inc(q_["num_read"], 1)
                act.wait_ge(q_["ha_moments"], h + 1)
                act.activation(rstd, mv[:, :, 1], ACT.Sqrt).then_inc(q_["ha_std"], 1)

            for h in range(HA):
                for p_ in range(2):
                    n, k = 22 + 2 * h + p_, 14 + 2 * h + p_
                    to_raw(n, k)
                    silu_tanh(2 * h + p_)
                if h:
                    unit(h - 1)
            unit(HA - 1)


            act.wait_ge(q_["rwkv_made"], NJ)
            act.activation(ec, ec, ACT.Exp).then_inc(q_["ec_ready"], 1)

            def recur(i, what):
                if what is None:
                    return
                n = rows(i)
                if what == "Z":
                    act.wait_ge(q_["z_projected"], i + 1)
                    act.copy(Zs[0:n], bank[6][0:n, :]).then_inc(q_["z_read"], 1)
                if what == "O":
                    act.wait_ge(q_["o_projected"], i + 1)
                    act.copy(hg[0:n, i, DA:D], bank[6 if i < PT else 4][0:n, :]).then_inc(q_["o_read"], 1)
                if what == "G":
                    act.wait_ge(q_["hb_moments"], i + 1)
                    act.activation(sqs[0:n], sqs[0:n], ACT.Sqrt, scale=1.0 / DHB).then_inc(q_["hb_std"], 1)

            for i in range(TILES):
                act.wait_ge(q_["kt_turned"], i + 1)
                n = rows(i)
                if i >= 2:
                    act.wait_ge(q_["s_projected"], i - 1)
                for w in range(2):
                    ins = act.copy(kpt[i % 2][0:n, w, :], bank[2 + w][0:n, :])
                ins.then_inc(q_["kt_read"], 1)
                for l in range(LV(i)):
                    for q in range(2):
                        act.wait_ge(q_["w_projected"], ix(i, l, q) + 1)
                        act.copy(W[q][0:n, :, 0:n], bank[q][0:n, :].rearrange("p (h t) -> p h t", h=4)[:, :, 0:n]).then_inc(q_["w_read"], 1)
                    recur(i - 1, hooks(i, l))
            recur(PT - 1, "G")
            for j in range(NJ):
                act.wait_ge(q_["st_turned"], j + 1)
                act.wait_ge(q_["sst_zero"], 1)
                act.copy(SsT[0:64, j, :, 0:64], bank[2 * (j % 2)][0:64, :].rearrange("p (b v) -> p b v", b=NB))
                act.copy(SsT[64:128, j, :, 64:128], bank[2 * (j % 2) + 1][64:128, :].rearrange("p (b v) -> p b v", b=NB)).then_inc(q_["st_read"], 1)
            recur(PT, "Z")
            recur(PT, "O")
            recur(PT, "G")


            for i in range(TILES):
                n = rows(i)
                act.wait_ge(q_["h_turned"], i + 1)
                if i == 0:
                    act.wait_ge(q_["ss_projected"], HB)
                for q in range(2):
                    v = bank[4 + 2 * (i % 2) + q].rearrange("p (a b) -> p a b", a=4)[:, :, 0:n]
                    ins = act.copy(hT[:, 4 * q:4 * q + 4, cols(i)], v)
                ins.then_inc(q_["ht_ready"], 1)

            def row_std(stat, n):
                act.wait_ge(q_["ln_moments"], stat)
                act.activation(rstd[0:n, 0:1], mv[0:n, 0, 1:2], ACT.Sqrt).then_inc(q_["ln_std"], 1)

            for i in range(TILES):
                row_std(i + 1, rows(i))
            for i in range(TILES):
                n = rows(i)
                act.wait_ge(q_["x1_in_psum"], i + 1)
                for q in range(2):
                    v = bank[4 + 2 * (i % 2) + q].rearrange("p (a b) -> p a b", a=4)[:, :, 0:n]
                    ins = act.copy(x1T[:, 4 * q:4 * q + 4, cols(i)], v)
                ins.then_inc(q_["x1_turned"], 1)
            act.wait_ge(q_["routing"], 1)
            act.activation(probs, probs, ACT.Exp).then_inc(q_["probs_exp"], 1)
            with act.Fori(0, NE // 2) as it:
                for p_ in range(2):
                    act.wait_ge(q_["xs_turned"], 2 * it + p_ + 1)
                    for q in range(2):
                        ins = act.copy(xsT[p_][:, 4 * q:4 * q + 4, :], bank[6 + q].rearrange("p (k c) -> p k c", k=4))
                    ins.then_inc(q_["xst_ready"], 1)
                    for hf in range(2):
                        act.wait_ge(q_["hidden"], 4 * it + 2 * p_ + hf + 1)
                        act.wait_ge(q_["hid_ready"], 4 * it + 2 * p_ + hf)
                        act.activation(hsl, bank[2 * p_ + hf][:, 0:256].rearrange("p (f c) -> p f c", f=2), ACT.Silu).then_inc(q_["hid_silu"], 1)
                    act.wait_ge(q_["down"], 2 * it + p_ + 1)
                    act.wait_ge(q_["y_stored"], 32 * it + 16 * p_)
                    act.copy(ysb[0][:, 0:512], bank[4][:, :])
                    act.copy(ysb[0][:, 512:1024], bank[5][:, :]).then_inc(q_["y_slots_ready"], 1)
                    act.wait_ge(q_["y_slots_ready"], 2 * it + p_ + 1)
                    act.dma_start(dr["y_slots"].rearrange("(e c) d -> e c d", c=CAP)[bass.ds(2 * it + p_, 1)].rearrange("a c d -> (a c) d"), ysb[0]).then_inc(q_["y_stored"], 16)
            act.wait_ge(q_["combined"], TILES)
            over = act.value_load(flagu[0:1, 0:1], min_val=0, max_val=1)
            with act.If(over):
                for i in range(TILES):
                    n = rows(i)
                    act.wait_ge(q_["all_turned"], i + 1)
                    for q in range(2):
                        v = bank[6 + q].rearrange("p (a b) -> p a b", a=4)[:, :, 0:n]
                        ins = act.copy(dxT[:, 4 * q:4 * q + 4, cols(i)], v)
                    ins.then_inc(q_["all_xt"], 1)
                with act.Fori(0, NE) as it:
                    for f in range(NF):
                        act.wait_ge(q_["all_hidden"], NF * it + f + 1)
                        act.wait_ge(q_["all_hid"], NF * it + f)
                        act.activation(dhs[:, 0:SEQ], bank[0][:, :], ACT.Silu)
                        act.activation(dhs[:, SEQ:N], bank[1][:, 0:NS], ACT.Silu).then_inc(q_["all_silu"], 1)
            for i in range(TILES):
                row_std(TILES + i + 1, rows(i))
        @block.vector
        def _(dve):
            step = [0]

            def link(ins):
                step[0] += 1
                ins.then_inc(q_["dve_step"], 1)
                dve.wait_ge(q_["dve_step"], step[0])

            link(dve.memset(mv, 1.0))
            link(dve.memset(colg, 1.0))
            dve.memset(hg[64:128, PT, :], 0.0)
            st2 = st6
            for i in range(TILES):
                dve.wait_ge(x_loaded[i], 16)
                n = rows(i)
                for q in range(2):
                    ins = dve.bn_stats(out=st2[0:n, q, :], in_=x[0:n, i, 512 * q:512 * q + 512])
                link(ins)
                link(dve.bn_aggr(out=mv[0:n, i, :], in_=st2[0:n]))
            link(dve.tensor_scalar(mv[:, :, 1], mv[:, :, 1], 1e-5, None, ALU.add))
            dve.nop().then_inc(q_["x_moments"], 1)
            dve.wait_ge(q_["x_std"], 1)
            link(dve.reciprocal(rstd, rstd))
            dve.wait_ge(q_["ln0_loaded"], 32)
            for i in range(TILES):
                n = rows(i)
                xi = x[0:n, i, :]
                link(dve.tensor_scalar(xi, xi, mv[0:n, i, 0:1], rstd[0:n, i:i + 1], ALU.subtract, ALU.mult))
                link(dve.tensor_tensor(xi, xi, ln_g[0:n], ALU.mult))
                dve.tensor_tensor(xi, xi, ln_b[0:n], ALU.add).then_inc(q_["ln0_done"], 1)
            dve.wait_ge(q_["gates_on_pe"], 1)
            dve.tensor_copy(prmc, bank[4][:, 0:NPRM])
            dve.tensor_copy(shiftc, bank[4][:, 74:186].rearrange("p (a b) -> p a b", a=14))
            dve.tensor_copy(convc, bank[4][:, 186:378].rearrange("p (a b) -> p a b", a=8))
            dve.tensor_copy(ncol, bank[4][:, 378:410]).then_inc(q_["cols_ready"], 1)
            dve.wait_ge(q_["cols_ready"], 1)
            dve.tensor_scalar(dprm[:, HW0:HW0 + 4], prmc[:, W0R:W0R + 4], 0.5, None, ALU.mult)
            dve.tensor_scalar(dprm[:, HA0:HA0 + 4], prmc[:, A0R:A0R + 4], 0.5, None, ALU.mult)
            link(dve.tensor_scalar(dprm[:, OMKA:OMKA + 4], prmc[:, KAR:KAR + 4], -1.0, 1.0, ALU.mult, ALU.add))

            def shift(n, dst):
                dve.wait_ge(q_["slot_read"], n + 1)
                rw, m = raw[n % 2], P(MU + shift_tile(n))
                rs = rw[:, 513:585].rearrange("p (b t) -> p b t", b=NB)
                link(dve.tensor_tensor(dt[:, 0:584], rw[:, 0:584], rw[:, 1:585], ALU.subtract))
                ds = dt[:, 513:585].rearrange("p (b t) -> p b t", b=NB)
                dve.scalar_tensor_tensor(out=dst[:, 0:SEQ], in0=dt[:, 0:SEQ], scalar=m, in1=rw[:, 1:513], op0=ALU.mult, op1=ALU.add)
                dve.scalar_tensor_tensor(out=sa(dst), in0=ds[:, :, 0:LS], scalar=m, in1=rs[:, :, 1:9], op0=ALU.mult, op1=ALU.add).then_inc(q_["raw_used"], 1)
                dve.wait_ge(q_["raw_used"], n + 1)

            def gate_rows():
                R = slice(0, HA)
                dve.wait_ge(q_["gates_on_pe"], 2)
                dve.wait_ge(q_["gate_loaded"], 64)
                gv = bank[7][:, 0:40].rearrange("p (i c) -> p i c", i=TILES)
                dve.tensor_tensor(gtok[:, 0:PT, :], gv[:, 0:PT, :], gbias.unsqueeze(1).to_broadcast([128, PT, 8]), ALU.add)
                dve.tensor_tensor(gtok[0:NS, PT, :], gv[0:NS, PT, :], gbias[0:NS], ALU.add).then_inc(q_["gate_steps"], 1)
                dve.wait_ge(q_["gates_on_pe"], 3)
                dve.tensor_copy(LI[R, 0:SEQ], bank[4][R, :])
                dve.tensor_copy(LI[R, SEQ:N], bank[5][R, 0:NS])
                dve.tensor_copy(LF[R, 0:SEQ], bank[6][R, :])
                dve.tensor_copy(LF[R, SEQ:N], bank[5][R, NS:2 * NS]).then_inc(q_["gate_steps"], 1)
                dve.wait_ge(q_["gate_steps"], 2)
                dve.scalar_tensor_tensor(out=ta_[R], in0=LF[R], scalar=-1.0, in1=LF[R], op0=ALU.mult, op1=ALU.min).then_inc(q_["gate_steps"], 1)
                dve.wait_ge(q_["gate_exps"], 1)
                dve.tensor_scalar(ta_[R], ta_[R], 1.0, None, ALU.add).then_inc(q_["gate_steps"], 1)
                dve.wait_ge(q_["gate_exps"], 2)
                link(dve.scalar_tensor_tensor(out=LF[R], in0=LF[R], scalar=0.0, in1=tb_[R], op0=ALU.min, op1=ALU.subtract))
                dve.wait_ge(q_["masks_ready"], 1)
                dve.tensor_tensor_scan(bb[R], resets[R], LF[R], 0.0, ALU.mult, ALU.add)
                dve.tensor_copy(d0[R], LF[R])
                dve.tensor_copy(d1[R], LI[R])
                link(dve.tensor_tensor(mprev[R, 4:12], LF[R, SEQ:N:LS], m0r[R], ALU.add))
                link(dve.tensor_tensor(d1[R, SEQ:N:LS], mprev[R, 4:12], LI[R, SEQ:N:LS], ALU.max))
                link(dve.memset(d0[R, SEQ:N:LS], NEG))
                link(dve.tensor_tensor_scan(mm[R], d0[R], d1[R], 0.0, ALU.add, ALU.max))
                dve.memset(mprev[R, 0:1], 0.0)
                dve.tensor_copy(mprev[R, 1:4], mm[R, 127:384:128])
                dve.tensor_copy(mprev[R, 4:12], m0r[R])
                for dst, src in ((blast, bb), (mlast, mm)):
                    dve.tensor_copy(dst[R, 0:4], src[R, 127:SEQ:128])
                    ins = dve.tensor_copy(dst[R, 4:12], src[R, SEQ + LS - 1:N:LS])
                link(ins)
                dve.tensor_copy(mrow[R], mlast[R])
                link(dve.tensor_tensor(blast[R], blast[R], mlast[R], ALU.subtract))
                dve.tensor_tensor(wold[R], blast[R], mprev[R], ALU.add)
                link(dve.tensor_tensor(rbm[R], bb[R], mm[R], ALU.subtract))
                dve.tensor_tensor(pr(wint[R]), pr(rbm[R]), wide(mprev[R, 0:4], 128), ALU.add)
                dve.tensor_tensor(sa(wint[R]), sa(rbm[R]), wide(mprev[R, 4:12], LS), ALU.add)
                link(dve.tensor_tensor(LI[R], LI[R], bb[R], ALU.subtract))
                dve.tensor_tensor(pr(wsr[R]), pr(LI[R]), wide(blast[R, 0:4], 128), ALU.add)
                dve.tensor_tensor(sa(wsr[R]), sa(LI[R]), wide(blast[R, 4:12], LS), ALU.add).then_inc(q_["gate_steps"], 1)

            gate_rows()
            dve.wait_ge(q_["gn_loaded"], 96)
            dve.wait_ge(q_["gates_on_pe"], 4)
            shift(0, wlal)
            shift(1, sgl)
            dve.nop().then_inc(q_["shifted"], 2)
            dve.wait_ge(q_["lora_in"], 1)
            dve.tensor_scalar(sgl, sgl, 0.5, 0.5, ALU.mult, ALU.add)

            c1 = 0.5 * SQRT_E
            for j in range(NJ):
                if j:
                    dve.wait_ge(q_["post_projected"], j)
                shift(2 + 3 * j, r_)
                shift(3 + 3 * j, kr)
                link(dve.tensor_scalar(kk, kr, P(KKR + j), None, ALU.mult))
                dve.tensor_tensor(sq, kk, kk, ALU.mult).then_inc(q_["squares"], 1)
                dve.wait_ge(q_["tanhs"], j + 1)
                dve.tensor_scalar(a_, a_, 0.5, 0.5, ALU.mult, ALU.add)
                link(dve.tensor_scalar(ld, ld, -c1, -c1, ALU.mult, ALU.add))
                link(dve.tensor_tensor_scan(L, resets, ld, 0.0, ALU.mult, ALU.add))
                dve.tensor_copy(ec[:, j, 4:12], L[:, SEQ + LS - 1:N:LS])
                link(dve.tensor_copy(lmid[:, j, :], L[:, 63:SEQ:128]))
                link(dve.tensor_tensor(pr(L), pr(L), wide(lmid[:, j, :], 128), ALU.subtract))
                dve.tensor_copy(ec[:, j, 0:4], L[:, 127:SEQ:128])
                dve.tensor_tensor(tmp, L, ld, ALU.subtract).then_inc(q_["decay_args"], 1)
                shift(4 + 3 * j, vr)
                dve.wait_ge(q_["norms"], j + 1)
                link(dve.tensor_scalar(nrm, nrm, 1e-12, None, ALU.max))
                link(dve.reciprocal(nrm, nrm))
                link(dve.tensor_tensor(kk, kk, nrm, ALU.mult))
                dve.wait_ge(q_["decays"], j + 1)
                dve.tensor_tensor(arr[:, j, 0, :], kk, E1, ALU.mult)
                dve.tensor_tensor(arr[:, j, 1, :], r_, E2, ALU.mult)
                link(dve.tensor_tensor(tmp, kk, a_, ALU.mult))
                link(dve.scalar_tensor_tensor(out=nbeta[:, j, :], in0=tmp, scalar=-1.0, in1=E3, op0=ALU.mult, op1=ALU.mult))
                link(dve.tensor_scalar(tmp, a_, P(KAR + j), dprm[:, OMKA + j:OMKA + j + 1], ALU.mult, ALU.add))
                link(dve.tensor_tensor(kr2, kr, tmp, ALU.mult))
                dve.tensor_tensor(kap[:, j, :], kr2, E3, ALU.mult)
                dve.scalar_tensor_tensor(out=nrm, in0=r_, scalar=P(RKR + j), in1=kr2, op0=ALU.mult, op1=ALU.mult).then_inc(q_["rwkv_made"], 1)

            def conv(h, p_):
                n, k = 22 + 2 * h + p_, 14 + 2 * h + p_
                rw, c, dst = raw[k % 2], 4 * p_ + h, (kT if p_ else qT)[h % 2]
                dve.wait_ge(q_["slot_read"], n + 1)
                link(dve.tensor_scalar(zc[:, 0:600], rw[:, 0:600], P(CWR + c), P(CBR + c), ALU.mult, ALU.add))
                for t in range(1, CW):
                    ins = dve.scalar_tensor_tensor(out=zc[:, 0:600], in0=rw[:, t:600 + t], scalar=P(CWR + 8 * t + c), in1=zc[:, 0:600],
                                                   op0=ALU.mult, op1=ALU.add)
                    if t < CW - 1:
                        link(ins)
                ins.then_inc(q_["raw_used"], 1)
                dve.wait_ge(q_["silu_tanh"], 2 * h + p_ + 1)
                sc = 0.5 * (DHA ** -0.5 if p_ else 1.0)
                link(dve.tensor_scalar(th, th, sc, sc, ALU.mult, ALU.add))
                if h >= 2:
                    dve.wait_ge(q_["unit_projected"], h - 1)
                dve.tensor_tensor(dst[:, 0:SEQ], th[:, 0:SEQ], zc[:, 0:SEQ], ALU.mult)
                sv = [a[:, 515:603].rearrange("p (b t) -> p b t", b=NB)[:, :, 0:LS] for a in (th, zc)]
                dve.tensor_tensor(sa(dst), sv[0], sv[1], ALU.mult).then_inc(q_["qk_ready"], 1)
                dve.wait_ge(q_["qk_ready"], 2 * h + p_ + 1)

            def unit(h):
                if h:
                    dve.wait_ge(q_["unit_projected"], h)
                dve.wait_ge(q_["rows_spread"], h + 1)
                dve.tensor_tensor(qt[:, 0:SEQ], qT[h % 2][:, 0:SEQ], bank[4][:, :], ALU.mult)
                link(dve.tensor_tensor(qt[:, SEQ:N], qT[h % 2][:, SEQ:N], bank[5][:, 0:NS], ALU.mult))
                dve.wait_ge(q_["ones_set"], 2)
                o0 = arr_off(qpad)
                diag = arena[:, o0:o0 + NB * 72].rearrange("p (b t) -> p b t", t=72)[:, :, 0:LS]
                dve.tensor_copy(diag, sa(qt)).then_inc(q_["q_scaled"], 1)
                if h:
                    dve.wait_ge(q_["c0_loaded"], 16 * (h + 1))
                dve.tensor_copy(C0[:, :, 128], ncol.rearrange("p (b h) -> p b h", h=HA)[:, :, h])
                dve.tensor_tensor(vpad[0:NS], vext[0:NS, PT, h, :].unsqueeze(1).to_broadcast([NS, NB, 129]),
                                  seqmask[0:NS].unsqueeze(2).to_broadcast([NS, NB, 129]), ALU.mult).then_inc(q_["v_spread"], 1)
                dve.wait_ge(q_["weights"], h + 1)
                dve.tensor_tensor(sT[:, 0:PT, :], bank[4].rearrange("p (i t) -> p i t", i=PT), dm[:, 0:PT, :], ALU.mult)
                dve.tensor_tensor(sT[0:NS, PT, 0:NS], bank[5][0:NS, NS:2 * NS], dm[0:NS, PT, 0:NS], ALU.mult).then_inc(q_["weighted"], 1)
                for i in range(PT):
                    dve.wait_ge(q_["c_delta"], PT * h + i + 1)
                    dl = bank[7][:, 256:385]
                    if i == 0:
                        if h:
                            dve.wait_ge(q_["cs_stored"], 32 * h)
                        dve.tensor_copy(C, dl).then_inc(q_["c_state"], 1)
                    else:
                        dve.scalar_tensor_tensor(out=C, in0=C, scalar=woldb[:, h, i:i + 1], in1=dl, op0=ALU.mult, op1=ALU.add).then_inc(q_["c_state"], 1)
                    dve.wait_ge(q_["c_state"], PT * h + i + 1)
                dve.tensor_copy(nnew[:, NB, h:h + 1], C[:, 128:129])
                dve.wait_ge(q_["cs_delta"], h + 1)
                for b in range(NB):
                    src = (bank[5], bank[6], bank[7])[b // 3][:, 129 * (b % 3):129 * (b % 3) + 129]
                    ins = dve.scalar_tensor_tensor(out=C0[:, b, :], in0=C0[:, b, :], scalar=woldb[:, h, PT + b:PT + b + 1], in1=src, op0=ALU.mult, op1=ALU.add)
                ins.then_inc(q_["cs_new"], 1)
                dve.wait_ge(q_["cs_new"], h + 1)
                dve.tensor_copy(nnew[:, 0:NB, h], C0[:, :, 128]).then_inc(q_["n_new"], 1)
                dve.wait_ge(q_["num_read"], TILES * (h + 1))
                link(dve.scalar_tensor_tensor(out=den, in0=hh[:, :, 128], scalar=-1.0, in1=hh[:, :, 128], op0=ALU.mult, op1=ALU.max))
                link(dve.tensor_tensor(den, den, colg[:, 2, :, h], ALU.max))
                link(dve.reciprocal(rec, den))
                hv = hh[:, :, 0:128]
                link(dve.tensor_tensor(hv, hv, wide(rec, 128), ALU.mult))
                for i in range(TILES):
                    link(dve.bn_stats(out=st2[:, 0, :], in_=hh[:, i, 0:128]))
                    link(dve.bn_aggr(out=mv[:, i, :], in_=st2[:, 0, :]))
                dve.tensor_scalar(mv[:, :, 1], mv[:, :, 1], 1e-6, None, ALU.add).then_inc(q_["ha_moments"], 1)
                link(dve.tensor_tensor(hv, hv, wide(mv[:, :, 0], 128), ALU.subtract))
                dve.wait_ge(q_["ha_std"], h + 1)
                link(dve.reciprocal(rstd, rstd))
                link(dve.tensor_tensor(hv, hv, wide(rstd, 128), ALU.mult))
                link(dve.tensor_tensor(hv, hv, gn_a[:, 128 * h:128 * h + 128].unsqueeze(1).to_broadcast([128, TILES, 128]), ALU.mult))
                hgh = hg[:, :, 128 * h:128 * h + 128]
                dve.tensor_tensor(hgh, hgh, hv, ALU.mult).then_inc(q_["ha_done"], 1)

            dve.wait_ge(q_["post_projected"], NJ)
            link(dve.memset(hh, 1.0))
            for h in range(HA):
                conv(h, 0)
                conv(h, 1)
                if h == 1:
                    dve.wait_ge(q_["gn_loaded"], 96)
                    link(dve.tensor_scalar(hg[:, :, 0:DA], hg[:, :, 0:DA], 0.5, 0.5, ALU.mult, ALU.add))
                if h:
                    unit(h - 1)
            unit(HA - 1)


            dve.wait_ge(q_["outs_turned"], 1)
            for a, n in enumerate((126, 96, 96, 24)):
                dve.tensor_copy(outs[0:n, a, :], bank[5][0:n, 128 * a:128 * a + 128])
            dve.tensor_copy(outs[0:36, 4, :], bank[4][0:36, 0:128]).then_inc(q_["outs_ready"], 1)
            dve.wait_ge(q_["ec_ready"], 1)
            dve.tensor_tensor(pend, em, ec[:, :, 0:PT], ALU.mult)
            dve.memset(S, 0.0)
            link(dve.memset(Sh, 0.0))

            def recur(i, what):
                if what is None:
                    return
                n = rows(i)
                if what == "U":
                    dve.wait_ge(q_["u_projected"], i + 1)
                    dve.tensor_copy(Us[0:n], bank[7][0:n, :]).then_inc(q_["u_read"], 1)
                if what == "O" and i < PT:
                    dve.wait_ge(q_["s_projected"], i + 1)
                    link(dve.tensor_tensor(S, S, wide(pend[:, :, i], 128), ALU.mult))
                    pv = bank[7].rearrange("p (j v) -> p j v", j=NJ)
                    dve.tensor_tensor(S[0:64, :, 0:64], S[0:64, :, 0:64], pv[0:64, :, 0:64], ALU.add)
                    link(dve.tensor_tensor(S[64:128, :, 64:128], S[64:128, :, 64:128], pv[64:128, :, 64:128], ALU.add))
                    if i < PT - 1:
                        dve.tensor_tensor(Sh, S, wide(em[:, :, i + 1], 128), ALU.mult)
                    dve.nop().then_inc(q_["state"], 1)
                if what == "G":
                    dve.wait_ge(q_["o_read"], i + 1)
                    fv = hg[0:n, i, DA:D]
                    hv = fv.rearrange("p (h v) -> p h v", h=HB)
                    gv = gtk[0:n].rearrange("p (h v) -> p h v", h=HB)
                    link(dve.tensor_reduce(ssum[0:n], hv, AX.X, ALU.add))
                    link(dve.tensor_scalar(ssum[0:n], ssum[0:n], 1.0 / DHB, None, ALU.mult))
                    link(dve.tensor_tensor(hv, hv, wide(ssum[0:n], DHB), ALU.subtract))
                    link(dve.tensor_tensor(gv, hv, hv, ALU.mult))
                    link(dve.tensor_reduce(sqs[0:n], gv, AX.X, ALU.add))
                    dve.tensor_scalar(sqs[0:n], sqs[0:n], DHB * 64e-5, None, ALU.add).then_inc(q_["hb_moments"], 1)
                    link(dve.tensor_tensor(gv, vtok[0:n, i, :].rearrange("p (h v) -> p h v", h=HB), wide(bon[0:n, i, :], DHB), ALU.mult))
                    link(dve.tensor_tensor(gtk[0:n], gtk[0:n], lnx_b[0:n], ALU.add))
                    dve.wait_ge(q_["hb_std"], i + 1)
                    link(dve.reciprocal(sqs[0:n], sqs[0:n]))
                    link(dve.tensor_tensor(hv, hv, wide(sqs[0:n], DHB), ALU.mult))
                    link(dve.tensor_tensor(fv, fv, lnx_g[0:n], ALU.mult))
                    link(dve.tensor_tensor(fv, fv, gtk[0:n], ALU.add))
                    dve.wait_ge(q_["g_projected"], i + 1)
                    dve.tensor_tensor(fv, fv, bank[7][0:n, :], ALU.mult).then_inc(q_["hb_done"], 1)

            for i in range(TILES):
                n = rows(i)
                tri = tri_p if i < PT else tri_s
                if i >= 2:
                    dve.wait_ge(q_["o_projected"], i - 1)
                for s_ in range(4):
                    q, w = s_ // 2, s_ % 2
                    dve.wait_ge(q_["grams"], 4 * i + s_ + 1)
                    for odd in range(2):
                        src = bank[2 * (s_ % 3) + odd][0:n, :].rearrange("p (h v t) -> p h v t", h=2, v=2)[:, :, :, 0:n]
                        dst = G[i % 2][0:n, w, 4 * q + odd:4 * q + 4:2, :].rearrange("p h (v t) -> p h v t", v=2)[:, :, :, 0:n]
                        ins = dve.tensor_tensor(dst, src, tri[0:n].unsqueeze(1).to_broadcast([n, 2, 2, n]), ALU.mult)
                    ins.then_inc(q_["gram_read"], 1)
                for l in range(LV(i)):
                    for q in range(2):
                        k = ix(i, l, q)
                        Yq = Y[i % 2][0:n, 4 * q:4 * q + 4, 0:n]
                        if l == 0:
                            idn = ident[0:n, 0:n].unsqueeze(1).to_broadcast([n, 4, n])
                            dve.wait_ge(q_["mt_ready"], k + 1)
                            dve.tensor_tensor(Yq, MT[q][0:n, :, 0:n], idn, ALU.add)
                            dve.wait_ge(q_["w_read"], k + 1)
                            dve.tensor_tensor(X[q][0:n, :, 0:n], W[q][0:n, :, 0:n], idn, ALU.add).then_inc(q_["yx_read"], 1)
                        else:
                            dve.wait_ge(q_["yx_projected"], ix2(i, l, q) + 1)
                            pv = [bank[b_][0:n, :].rearrange("p (h t) -> p h t", h=4)[:, :, 0:n] for b_ in (2 + q, 4 + q)]
                            ins = dve.tensor_tensor(Yq, Yq, pv[0], ALU.add)
                            if l < LV(i) - 1:
                                ins = dve.tensor_tensor(X[q][0:n, :, 0:n], X[q][0:n, :, 0:n], pv[1], ALU.add)
                            ins.then_inc(q_["yx_read"], 1)
                    recur(i - 1, hooks(i, l))
            recur(PT - 1, "G")
            dve.wait_ge(q_["sst_zero"], 1)
            diag = [arena[:, arr_off(arpad[:, v]):arr_off(arpad[:, v]) + NB * 72].rearrange("p (b t) -> p b t", t=72)[:, :, 0:LS] for v in range(2)]
            for j in range(NJ):
                if j:
                    dve.wait_ge(q_["pads_used"], j)
                for v in range(2):
                    ins = dve.tensor_copy(diag[v], sa(arr[:, j, v, :]))
                ins.then_inc(q_["pads_made"], 1)
            dve.wait_ge(q_["ps_projected"], 1)
            for h2 in range(2):
                r = slice(64 * h2, 64 * h2 + 64)
                ins = dve.tensor_copy(pS[r], bank[5][r, 0:256].rearrange("p (j k) -> p j k", j=NJ))
            ins.then_inc(q_["ps_ready"], 1)
            recur(PT, "U")
            dve.tensor_tensor(SsT[:, :, :, :], SsT[:, :, :, :], ec[:, :, 4:12].unsqueeze(3).to_broadcast([128, NJ, NB, 128]), ALU.mult).then_inc(q_["sst_scaled"], 1)
            for h in range(HB):
                r = slice(64 * (h % 2), 64 * (h % 2) + 64)
                dve.wait_ge(q_["ss_projected"], h + 1)
                dve.tensor_copy(Sld[r, h // 2, :, :], bank[h % 4][r, :].rearrange("p (b k) -> p b k", b=NB)).then_inc(q_["ss_read"], 1)
            recur(PT, "G")

            def norm_rows(y, n, stat):
                for q in range(2):
                    ins = dve.bn_stats(out=st2[0:n, q, :], in_=y[:, 512 * q:512 * q + 512])
                link(ins)
                link(dve.bn_aggr(out=mv[0:n, 0, :], in_=st2[0:n]))
                dve.tensor_scalar(mv[0:n, 0, 1:2], mv[0:n, 0, 1:2], 1e-5, None, ALU.add).then_inc(q_["ln_moments"], 1)
                dve.wait_ge(q_["ln_std"], stat)
                link(dve.reciprocal(rstd[0:n, 0:1], rstd[0:n, 0:1]))
                link(dve.tensor_scalar(y, y, mv[0:n, 0, 0:1], rstd[0:n, 0:1], ALU.subtract, ALU.mult))

            dve.wait_ge(q_["x_back"], 16 * (TILES + 6))
            for i in range(TILES):
                n = rows(i)
                y = xln[0:n, i, :]
                dve.wait_ge(q_["mix_projected"], i + 1)
                for q in range(2):
                    b_ = 2 * (i % 2) + q
                    yq = y[:, 512 * q:512 * q + 512]
                    ins = dve.scalar_tensor_tensor(out=yq, in0=yq, scalar=ALPHA, in1=bank[b_][0:n, :], op0=ALU.mult, op1=ALU.add)
                ins.then_inc(q_["mix_read"], 1)
                dve.wait_ge(q_["mix_read"], i + 1)
                norm_rows(y, n, i + 1)
                link(dve.tensor_tensor(y, y, l1g[0:n], ALU.mult))
                dve.tensor_tensor(y, y, l1b[0:n], ALU.add).then_inc(q_["ln1_done"], 1)
            dve.wait_ge(q_["ln1_done"], TILES)
            link(dve.memset(probs, 0.0))
            dve.wait_ge(q_["routed"], 1)
            lv = bank[4][:, 0:TILES * NE].rearrange("p (i e) -> p i e", i=TILES)
            dve.tensor_copy(probs[:, 0:PT, :], lv[:, 0:PT, :])
            link(dve.tensor_copy(probs[0:NS, PT, :], lv[0:NS, PT, :]))
            link(dve.tensor_reduce(one5, probs, AX.X, ALU.max))
            dve.tensor_tensor(probs, probs, wide(one5, NE), ALU.subtract).then_inc(q_["routing"], 1)
            dve.wait_ge(q_["probs_exp"], 1)
            link(dve.tensor_reduce(one5, probs, AX.X, ALU.add))
            link(dve.reciprocal(one5, one5))
            link(dve.tensor_tensor(probs, probs, wide(one5, NE), ALU.mult))
            link(dve.tensor_tensor(sl, probs, brr.unsqueeze(1).to_broadcast([128, TILES, NE]), ALU.add))

            def grp(ap):
                return ap.rearrange("p i (g e) -> p (i g) e", g=NG)

            def f1(ap):
                return ap.rearrange("p i g -> p (i g)")

            def first_of(dst, src, top, scratch):
                link(dve.tensor_tensor(grp(dst), grp(src), wide(f1(top), EG), ALU.is_ge))
                for k in range(1, EG):
                    link(dve.tensor_reduce(f1(scratch), grp(dst)[:, :, 0:k], AX.X, ALU.max))
                    link(dve.scalar_tensor_tensor(out=grp(dst)[:, :, k], in0=f1(scratch), scalar=0.0, in1=grp(dst)[:, :, k], op0=ALU.is_equal, op1=ALU.mult))

            link(dve.tensor_reduce(f1(gmax), grp(sl), AX.X, ALU.max))
            first_of(t80a, sl, gmax, gsum)
            link(dve.scalar_tensor_tensor(out=t80b, in0=t80a, scalar=NEG, in1=sl, op0=ALU.mult, op1=ALU.add))
            link(dve.tensor_reduce(f1(gsum), grp(t80b), AX.X, ALU.max))
            link(dve.tensor_tensor(gmax, gmax, gsum, ALU.add))
            link(dve.tensor_copy(f1(gtop), f1(gsum)))
            first_of(gate, t80b, gtop, gsum)
            link(dve.tensor_tensor(gate, gate, t80a, ALU.add))
            link(dve.tensor_reduce(one5, gmax, AX.X, ALU.max))
            link(dve.tensor_tensor(gtop, gmax, wide(one5, NG), ALU.is_ge))
            for k in range(1, NG):
                link(dve.tensor_reduce(one5, gtop[:, :, 0:k], AX.X, ALU.max))
                link(dve.scalar_tensor_tensor(out=gtop[:, :, k], in0=one5, scalar=0.0, in1=gtop[:, :, k], op0=ALU.is_equal, op1=ALU.mult))
            link(dve.tensor_tensor(grp(gate), grp(gate), wide(f1(gtop), EG), ALU.mult))
            link(dve.memset(gate[64:128, PT, :], 0.0))
            dve.tensor_copy(s01, gate).then_inc(q_["routing"], 1)
            link(dve.tensor_tensor(gate, gate, probs, ALU.mult))
            link(dve.tensor_reduce(one5, gate, AX.X, ALU.add))
            link(dve.tensor_scalar(one5, one5, 1e-37, None, ALU.max))
            link(dve.reciprocal(one5, one5))
            link(dve.tensor_tensor(gate, gate, wide(one5, NE), ALU.mult))
            dve.wait_ge(q_["routed"], 2)
            rk = bank[5][:, 0:TILES * NE].rearrange("p (i e) -> p i e", i=TILES)
            link(dve.tensor_reduce(flagf, bank[5][:, TILES * NE:TILES * NE + NE], AX.X, ALU.max))
            dve.tensor_scalar(flagu, flagf, CAP + 0.5, None, ALU.is_gt)
            link(dve.scalar_tensor_tensor(out=inb, in0=rk, scalar=CAP - 0.5, in1=s01, op0=ALU.is_lt, op1=ALU.mult))
            link(dve.tensor_tensor(t80a, rk, slot0.unsqueeze(1).to_broadcast([128, TILES, NE]), ALU.add))
            link(dve.tensor_tensor(sl, t80a, inb, ALU.mult))
            link(dve.scalar_tensor_tensor(out=t80b, in0=rk, scalar=1.0, in1=inb, op0=ALU.add, op1=ALU.mult))
            link(dve.tensor_scalar(t80b, t80b, -1.0, None, ALU.add))
            for i in range(TILES):
                if i:
                    dve.wait_ge(q_["onehot_used"], i)
                dve.tensor_tensor(onehot[0], places.unsqueeze(1).to_broadcast([128, NE, CAP]), t80b[:, i, :].unsqueeze(2).to_broadcast([128, NE, CAP]), ALU.is_equal).then_inc(q_["onehot"], 1)
            dve.wait_ge(q_["onehot_used"], TILES)
            iv = bank[6][:, 0:2 * NE].rearrange("p (e c) -> p e c", c=2)
            link(dve.tensor_scalar(idxf, iv[:, :, 1], 128.0, None, ALU.mult))
            dve.tensor_tensor(idxu, idxf, iv[:, :, 0], ALU.add).then_inc(q_["routing"], 1)
            link(dve.tensor_reduce(slotA, sl, AX.X, ALU.max))
            link(dve.tensor_reduce(slotB, sl, AX.X, ALU.add))
            link(dve.tensor_tensor(slotB, slotB, slotA, ALU.subtract))
            link(dve.tensor_tensor(t80a, sl, wide(slotA, NE), ALU.is_equal))
            link(dve.tensor_tensor(t80a, t80a, inb, ALU.mult))
            link(dve.tensor_tensor(t80b, inb, t80a, ALU.subtract))
            link(dve.tensor_tensor(t80a, t80a, gate, ALU.mult))
            link(dve.tensor_tensor(t80b, t80b, gate, ALU.mult))
            link(dve.tensor_reduce(gA, t80a, AX.X, ALU.add))
            link(dve.tensor_reduce(gB, t80b, AX.X, ALU.add))
            dve.tensor_scalar(slotAu, slotA, -1.0, 0.0, ALU.add, ALU.max)
            dve.tensor_scalar(slotBu, slotB, -1.0, 0.0, ALU.add, ALU.max).then_inc(q_["slots_ready"], 1)
            link(dve.tensor_tensor(s01, s01, inb, ALU.subtract))
            link(dve.tensor_tensor(s01, s01, gate, ALU.mult))
            dve.wait_ge(q_["x1_turned"], TILES)
            dve.wait_ge(q_["x1_stored"], 16 * TILES)
            for i in range(TILES):
                n = rows(i)
                ins = dve.tensor_scalar(xln[0:n, i, :], xln[0:n, i, :], ALPHA, None, ALU.mult)
            link(ins)
            with dve.Fori(0, NE // 2) as it:
                for p_ in range(2):
                    for hf in range(2):
                        dve.wait_ge(q_["hid_silu"], 4 * it + 2 * p_ + hf + 1)
                        dve.wait_ge(q_["down"], 2 * it + p_)
                        dve.tensor_tensor(hid[:, 2 * hf:2 * hf + 2, :], hsl, bank[2 * p_ + hf][:, 256:512].rearrange("p (f c) -> p f c", f=2), ALU.mult).then_inc(q_["hid_ready"], 1)
            for i in range(TILES):
                n = rows(i)
                dve.wait_ge(ya_loaded[i % 2], 16 * (NE // 2 + 1 - i % 2) + 32 * (i // 2 + 1))
                y = xln[0:n, i, :]
                link(dve.scalar_tensor_tensor(out=y, in0=ya[i % 2][0][0:n], scalar=gA[0:n, i:i + 1], in1=y, op0=ALU.mult, op1=ALU.add))
                dve.scalar_tensor_tensor(out=y, in0=ya[i % 2][1][0:n], scalar=gB[0:n, i:i + 1], in1=y, op0=ALU.mult, op1=ALU.add).then_inc(q_["combined"], 1)
            dve.wait_ge(q_["combined"], TILES)
            over = dve.value_load(flagu[0:1, 0:1], min_val=0, max_val=1)
            with dve.If(over):
                with dve.Fori(0, NE) as it:
                    dve.wait_ge(q_["all_read"], TILES * it)
                    dve.tensor_copy(dgc.unsqueeze(2), s01[:, :, bass.ds(it, 1)]).then_inc(q_["all_gate"], 1)
                    dve.wait_ge(q_["all_gate"], it + 1)
                    for f in range(NF):
                        dve.wait_ge(q_["all_silu"], NF * it + f + 1)
                        dve.tensor_tensor(dhid[:, f, 0:SEQ], dhs[:, 0:SEQ], bank[2][:, :], ALU.mult)
                        dve.tensor_tensor(dhid[:, f, SEQ:N], dhs[:, SEQ:N], bank[3][:, 0:NS], ALU.mult).then_inc(q_["all_hid"], 1)
                    for i in range(TILES):
                        n = rows(i)
                        dve.wait_ge(q_["all_down"], TILES * it + i + 1)
                        for q in range(2):
                            yq = xln[0:n, i, 512 * q:512 * q + 512]
                            ins = dve.scalar_tensor_tensor(out=yq, in0=bank[4 + q][0:n, :], scalar=dgc[0:n, i:i + 1], in1=yq, op0=ALU.mult, op1=ALU.add)
                        ins.then_inc(q_["all_read"], 1)
                dve.wait_ge(q_["all_read"], TILES * NE)
            for i in range(TILES):
                n = rows(i)
                y = xln[0:n, i, :]
                norm_rows(y, n, TILES + i + 1)
                link(dve.tensor_tensor(y, y, l2g[0:n], ALU.mult))
                dve.tensor_tensor(y, y, l2b[0:n], ALU.add).then_inc(q_["y_ready"], 1)

        @block.tensor
        def _(pe):
            pe.wait_ge(q_["ident_ready"], 1)
            pe.wait_ge(q_["prm_loaded"], 128)
            pe.wait_ge(q_["hist_loaded"], 48)
            pe.transpose(bank[4][:, 0:NPRM], prow[0:NPRM, :], ident[0:NPRM, 0:NPRM])
            for t in range(14):
                pe.transpose(bank[4][:, 74 + 8 * t:82 + 8 * t], shrows[0:NB, t, :], ident[0:NB, 0:NB])
            for t in range(8):
                pe.transpose(bank[4][:, 186 + 24 * t:210 + 24 * t], cvrows[0:24, t, :], ident[0:24, 0:24])
            pe.transpose(bank[4][:, 378:410], nrows[0:32, :], ident[0:32, 0:32]).then_inc(q_["gates_on_pe"], 1)
            for i in range(TILES):
                n = rows(i)
                pe.wait_ge(q_["ln0_done"], i + 1)
                if i >= 2:
                    pe.wait_ge(q_["xt_ready"], i - 1)
                for k in range(KD):
                    ins = pe.transpose(bank[2 * (i % 2) + k // 4][:, 128 * (k % 4):128 * (k % 4) + n], x[0:n, i, 128 * k:128 * k + 128], ident[0:n, 0:n])
                ins.then_inc(q_["x_turned"], 1)
            pe.wait_ge(q_["xt_ready"], TILES)
            pe.wait_ge(q_["gate_loaded"], 64)
            for i in range(TILES):
                for k in range(KD):
                    ins = pe.matmul(bank[7][0:rows(i), 8 * i:8 * i + 8], xT[:, k, cols(i)], gw[:, k, :], start=k == 0, stop=k == KD - 1)
            ins.then_inc(q_["gates_on_pe"], 1)

            def slot(n):
                pe.wait_ge(w_loaded[n % NW], 16 * (n // NW + 1))
                if n >= 2:
                    pe.wait_ge(q_["slot_read"], n - 1)
                A, B = bank[2 * (n % 2)], bank[2 * (n % 2) + 1]
                w = wring[:, n % NW]
                if 14 <= n < 22:
                    for i in range(TILES):
                        dst = A[:, 128 * i:128 * i + 128] if i < PT else B[0:NS, 0:128]
                        for k in range(KD):
                            ins = pe.matmul(dst, xT[:, k, cols(i)], w[:, k, :], start=k == 0, stop=k == KD - 1)
                else:
                    for k in range(KD):
                        pe.matmul(A[:, :], w[:, k, :], xT[:, k, 0:SEQ], start=k == 0, stop=k == KD - 1)
                        ins = pe.matmul(B[:, 0:NS], w[:, k, :], xT[:, k, SEQ:N], start=k == 0, stop=k == KD - 1)
                ins.then_inc(q_["slot_projected"], 1)

            def both(A, B, lhs, rhs):
                pe.matmul(A, lhs, rhs[:, 0:SEQ], start=True, stop=True)
                return pe.matmul(B, lhs, rhs[:, SEQ:N], start=True, stop=True)

            slot(0)
            pe.wait_ge(q_["gate_steps"], 1)
            pe.wait_ge(q_["cols_ready"], 1)
            for i in range(TILES):
                n = rows(i)
                li = bank[4][0:HA, 128 * i:128 * i + n] if i < PT else bank[5][0:HA, 0:NS]
                lf = bank[6][0:HA, 128 * i:128 * i + n] if i < PT else bank[5][0:HA, NS:2 * NS]
                pe.transpose(li, gtok[0:n, i, 0:HA], ident[0:n, 0:n])
                ins = pe.transpose(lf, gtok[0:n, i, HA:8], ident[0:n, 0:n])
            ins.then_inc(q_["gates_on_pe"], 1)
            slot(1)
            pe.wait_ge(q_["gate_exps"], 3)
            for a, src in enumerate((LI, wsr, emt)):
                for i in range(TILES):
                    pe.transpose(bank[5][0:rows(i), 20 * a + 4 * i:20 * a + 4 * i + 4], src[0:HA, cols(i)], ident[0:HA, 0:HA])
            for h in range(HA):
                ins = pe.matmul(bank[5][:, 64 + 12 * h:76 + 12 * h], sel[0:HA, h, :], wold[0:HA, :], start=True, stop=True)
            ins.then_inc(q_["gates_on_pe"], 1)
            pe.wait_ge(q_["gate_exps"], 4)

            def post(j):
                pe.wait_ge(q_["rwkv_made"], j + 1)
                for i in range(TILES):
                    pe.matmul(bank[7][0:rows(i), 2 * i:2 * i + 2], nrm[:, cols(i)], headsel, start=True, stop=True)
                for i in range(TILES):
                    dst = bank[6][:, 128 * i:128 * i + 128] if i < PT else bank[7][0:NS, 128:256]
                    ins = pe.transpose(dst, vr[:, cols(i)], ident)
                ins.then_inc(q_["post_projected"], 1)

            for j in range(NJ):
                slot(2 + 3 * j)
                if j:
                    post(j - 1)
                slot(3 + 3 * j)
                if j == 0:
                    pe.wait_ge(q_["lora_in"], 1)
                else:
                    pe.wait_ge(q_["norms"], j)
                    pe.wait_ge(q_["post_read"], j)
                both(bank[4][:, :], bank[5][:, 0:NS], w2a2[0:64, 128 * j:128 * j + 128], wlal[0:64])
                both(bank[6][:, :], bank[7][:, 256:256 + NS], w2a2[64:128, 128 * j:128 * j + 128], wlal[64:128]).then_inc(q_["lora_projected"], 1)
                slot(4 + 3 * j)
                pe.wait_ge(q_["squares"], j + 1)
                pe.wait_ge(q_["tanhs"], j + 1)
                both(bank[4][:, :], bank[5][:, 0:NS], blockones, sq).then_inc(q_["norms_projected"], 1)
            slot(14)
            post(NJ - 1)
            for n in range(15, 22):
                slot(n)

            def unit(h):
                if h == 0:
                    pe.wait_ge(q_["post_read"], NJ)
                else:
                    pe.wait_ge(q_["cs_new"], h)
                    pe.wait_ge(q_["num_read"], TILES * h)
                pe.wait_ge(q_["gate_exps"], 3)
                both(bank[4][:, :], bank[5][:, 0:NS], sel[0:HA, h, :], wint[0:HA]).then_inc(q_["rows_spread"], 1)
                pe.wait_ge(q_["qk_ready"], 2 * h + 2)
                for i in range(TILES):
                    dst = bank[6][:, 128 * i:128 * i + 128] if i < PT else bank[7][0:NS, 0:128]
                    ins = pe.transpose(dst, kT[h % 2][:, cols(i)], ident)
                ins.then_inc(q_["k_turned"], 1)
                pe.wait_ge(q_["q_scaled"], h + 1)
                pe.wait_ge(q_["k_tokens"], h + 1)
                for i in range(TILES):
                    n = rows(i)
                    kq = bank[4][:, 128 * i:128 * i + 128] if i < PT else bank[5][0:NS, NS:2 * NS]
                    dd = bank[6][:, 128 * i:128 * i + 128] if i < PT else bank[7][0:NS, 128:192]
                    pe.matmul(kq, kT[h % 2][:, cols(i)], qT[h % 2][:, cols(i)], start=True, stop=True)
                    pe.matmul(dd, sel[0:HA, h, 0:n], rbm[0:HA, cols(i)], start=True, stop=False)
                    ins = pe.matmul(dd, ident[0:n, 0:n], neg_p if i < PT else neg_s[0:NS], start=False, stop=True)
                ins.then_inc(q_["scores"], 1)
                pe.wait_ge(q_["weighted"], h + 1)
                for i in range(TILES):
                    n = rows(i)
                    dst = bank[4 + i % 2][0:n, 128:257]
                    if i >= 2:
                        pe.wait_ge(q_["num_read"], TILES * h + i - 1)
                    if i == 0:
                        pe.matmul(dst, sT[:, 0, :], vext[:, 0, h, :], start=True, stop=True).then_inc(q_["numerator"], 1)
                    elif i < PT:
                        pe.wait_ge(q_["c_state"], PT * h + i)
                        pe.matmul(dst, qt[:, cols(i)], C, start=True, stop=False)
                        pe.matmul(dst, sT[:, i, :], vext[:, i, h, :], start=False, stop=True).then_inc(q_["numerator"], 1)
                    else:
                        pe.wait_ge(q_["c0_loaded"], 16 * (h + 1))
                        pe.wait_ge(q_["v_spread"], h + 1)
                        for b in range(NB):
                            pe.matmul(dst, qpad[:, b, :], C0[:, b, :], start=b == 0, stop=False)
                        pe.matmul(dst, sT[0:NS, PT, 0:NS], vext[0:NS, PT, h, :], start=False, stop=True).then_inc(q_["numerator"], 1)
                    if i < PT:
                        if i:
                            pe.wait_ge(q_["c_state"], PT * h + i)
                        pe.matmul(bank[7][:, 256:385], kw[:, i, :], vext[:, i, h, :], start=True, stop=True).then_inc(q_["c_delta"], 1)
                pe.wait_ge(q_["c_state"], PT * (h + 1))
                pe.wait_ge(q_["num_read"], TILES * h + PT)
                for dst, b0, b1 in ((bank[5], 0, 3), (bank[6], 3, 6), (bank[7], 6, 8)):
                    ins = pe.matmul(dst[:, 0:129 * (b1 - b0)], kw[0:NS, PT, :], vpad[0:NS, b0:b1, :], start=True, stop=True)
                ins.then_inc(q_["cs_delta"], 1)
                pe.nop().then_inc(q_["unit_projected"], 1)

            for h in range(HA):
                slot(22 + 2 * h)
                slot(23 + 2 * h)
                if h:
                    unit(h - 1)
            unit(HA - 1)

            pe.wait_ge(q_["raw_collected"], 22)
            pe.wait_ge(q_["n_new"], HA)
            pe.wait_ge(q_["num_read"], TILES * HA)
            pe.transpose(bank[5][0:126, 0:128], shnew.rearrange("p b t -> p (b t)"), ident)
            cv = cvnew.rearrange("p b w c -> p (b w c)")
            pe.transpose(bank[5][0:96, 128:256], cv[:, 0:96], ident)
            pe.transpose(bank[5][0:96, 256:384], cv[:, 96:192], ident)
            pe.transpose(bank[5][0:24, 384:512], cv[:, 192:216], ident)
            pe.transpose(bank[4][0:36, 0:128], nnew.rearrange("p b h -> p (b h)"), ident).then_inc(q_["outs_turned"], 1)
            pe.wait_ge(q_["outs_ready"], 1)

            def recur(i, what):
                if what is None:
                    return
                n = rows(i)
                H = [slice(64 * h, 64 * h + 64) for h in range(HB)]
                Gi, Yi = G[i % 2], Y[i % 2]
                V = vtok[0:n, i, :]
                if what == "Z" and i < PT:
                    if i:
                        pe.wait_ge(q_["state"], i)
                        pe.wait_ge(q_["o_read"], i)
                    for j in range(NJ):
                        if i:
                            pe.matmul(bank[6][:, 128 * j:128 * j + 128], arr[:, j, 0, cols(i)], Sh[:, j, :], start=j == 0, stop=False, skip_group_check=True)
                        for h in (2 * j, 2 * j + 1):
                            ins = pe.matmul(bank[6][:, H[h]], Gi[:, 1, h, 0:128], V[:, H[h]], start=i + h == 0, stop=True, skip_group_check=True)
                    ins.then_inc(q_["z_projected"], 1)
                if what == "Z" and i == PT:
                    for j in range(NJ):
                        pe.wait_ge(q_["pads_made"], j + 1)
                        for v, dst in ((0, bank[6]), (1, bank[4])):
                            for b in range(NB):
                                ins = pe.matmul(dst[0:n, 128 * j:128 * j + 128], arpad[:, v, b, :], SsT[:, j, b, :], start=j + b == 0, stop=False, skip_group_check=True)
                        ins.then_inc(q_["pads_used"], 1)
                    for h in range(HB):
                        ins = pe.matmul(bank[6][0:n, H[h]], Gi[0:n, 1, h, 0:n], V[:, H[h]], start=False, stop=True, skip_group_check=True)
                    ins.then_inc(q_["z_projected"], 1)
                if what == "U":
                    pe.wait_ge(q_["z_read"], i + 1)
                    if i:
                        pe.wait_ge(q_["hb_done"], i)
                    for h in range(HB):
                        ins = pe.matmul(bank[7][0:n, H[h]], Yi[0:n, h, 0:n], Zs[0:n, H[h]], start=True, stop=True)
                    ins.then_inc(q_["u_projected"], 1)
                if what == "O":
                    pe.wait_ge(q_["u_read"], i + 1)
                    ob = bank[6 if i < PT else 4]
                    for j in range(NJ):
                        if 0 < i < PT:
                            pe.matmul(ob[:, 128 * j:128 * j + 128], arr[:, j, 1, cols(i)], Sh[:, j, :], start=j == 0, stop=False, skip_group_check=True)
                        for h in (2 * j, 2 * j + 1):
                            pe.matmul(ob[0:n, H[h]], Gi[0:n, 1, h, 128:128 + n], V[:, H[h]], start=i + h == 0, stop=False, skip_group_check=True)
                            ins = pe.matmul(ob[0:n, H[h]], Gi[0:n, 0, h, 128:128 + n], Us[0:n, H[h]], start=False, stop=True, skip_group_check=True)
                    ins.then_inc(q_["o_projected"], 1)
                    if i < PT:
                        for j in range(NJ):
                            c_ = slice(128 * j, 128 * j + 128)
                            pe.matmul(bank[7][:, c_], kpt[i % 2][:, 1, c_], V[:, c_], start=True, stop=False)
                            ins = pe.matmul(bank[7][:, c_], kpt[i % 2][:, 0, c_], Us[:, c_], start=False, stop=True)
                        ins.then_inc(q_["s_projected"], 1)
                if what == "G":
                    if i < PT:
                        pe.wait_ge(q_["state"], i + 1)
                    pe.matmul(bank[7][0:n, :], sgl[:, cols(i)], g2w, start=True, stop=True).then_inc(q_["g_projected"], 1)

            for i in range(TILES):
                n = rows(i)
                last = ix(i - 1, LV(i - 1) - 1, 1) + 1 if i else 0
                pe.wait_ge(q_["ktmp_made"], i + 1)
                if i:
                    pe.wait_ge(q_["yx_read"], last)
                    pe.wait_ge(q_["w_read"], last)
                for w in range(2):
                    for j in range(NJ):
                        ins = pe.transpose(bank[2 + w][0:n, 128 * j:128 * j + 128], ktmp[:, w, j, 0:n], ident)
                ins.then_inc(q_["kt_turned"], 1)
                for s_ in range(4):
                    q, w = s_ // 2, s_ % 2
                    if s_ == 1:
                        pe.wait_ge(q_["kt_read"], i + 1)
                    if s_ == 3:
                        pe.wait_ge(q_["gram_read"], 4 * i + 1)
                    for h in range(4 * q, 4 * q + 4):
                        r = slice(64 * (h % 2), 64 * (h % 2) + 64)
                        j = h // 2
                        dst = bank[2 * (s_ % 3) + h % 2][0:n, 256 * (j % 2):256 * (j % 2) + 256].rearrange("p (v t) -> p v t", v=2)[:, :, 0:n]
                        ins = pe.matmul(dst, (kap if w else nbeta)[r, j, cols(i)], arr[r, j, :, cols(i)], start=True, stop=True)
                    ins.then_inc(q_["grams"], 1)
                pe.wait_ge(q_["gram_read"], 4 * i + 4)
                for l in range(LV(i)):
                    for q in range(2):
                        k = ix(i, l, q)
                        pe.wait_ge(q_["mt_ready"], k + 1)
                        if l:
                            pe.wait_ge(q_["yx_read"], k - 1)
                        for h in range(4):
                            ins = pe.matmul(bank[q][0:n, 128 * h:128 * h + n], MT[q][0:n, h, 0:n], X[q][0:n, h, 0:n] if l else ident[0:n, 0:n], start=True, stop=True)
                        ins.then_inc(q_["w_projected"], 1)
                    for q in range(2):
                        if l:
                            pe.wait_ge(q_["w_read"], ix(i, l, q) + 1)
                            for h in range(4):
                                yh = Y[i % 2][0:n, 4 * q + h, 0:n]
                                ins = pe.matmul(bank[2 + q][0:n, 128 * h:128 * h + n], W[q][0:n, h, 0:n], yh, start=True, stop=True)
                                if l < LV(i) - 1:
                                    ins = pe.matmul(bank[4 + q][0:n, 128 * h:128 * h + n], yh, W[q][0:n, h, 0:n], start=True, stop=True)
                            ins.then_inc(q_["yx_projected"], 1)
                    recur(i - 1, hooks(i, l))
            recur(PT - 1, "G")
            pe.wait_ge(q_["sst_loaded"], 16 * HB)
            pe.wait_ge(q_["yx_read"], ix(PT, 2, 1) + 1)
            for j in range(NJ):
                if j >= 2:
                    pe.wait_ge(q_["st_read"], j - 1)
                for b in range(NB):
                    for h2 in range(2):
                        r = slice(64 * h2, 64 * h2 + 64)
                        ins = pe.matmul(bank[2 * (j % 2) + h2][r, 64 * b:64 * b + 64], Sld[r, j, b, :], ident[r, r], start=True, stop=True)
                ins.then_inc(q_["st_turned"], 1)
            for h in range(HB):
                r = slice(64 * (h % 2), 64 * (h % 2) + 64)
                ins = pe.matmul(bank[5][r, 64 * (h // 2):64 * (h // 2) + 64], S[:, h // 2, r], ident[:, r], start=True, stop=True)
            ins.then_inc(q_["ps_projected"], 1)
            pe.wait_ge(q_["st_read"], NJ)
            pe.wait_ge(q_["o_read"], PT)
            recur(PT, "Z")
            recur(PT, "U")
            recur(PT, "O")
            pe.wait_ge(q_["sst_scaled"], 1)
            for h in range(HB):
                r = slice(64 * (h % 2), 64 * (h % 2) + 64)
                j, H = h // 2, slice(64 * h, 64 * h + 64)
                pe.wait_ge(q_["kp_spread"], h + 1)
                if h >= 4:
                    pe.wait_ge(q_["ss_read"], h - 3)
                dst = bank[h % 4]
                for b in range(NB):
                    pe.matmul(dst[r, 64 * b:64 * b + 64], SsT[:, j, b, r], ident[:, r], start=b == 0, stop=False, skip_group_check=True)
                pe.matmul(dst[r, :], vtok[0:NS, PT, H], kppad[h % 2][0:NS, 1], start=False, stop=False, skip_group_check=True)
                ins = pe.matmul(dst[r, :], Us[0:NS, H], kppad[h % 2][0:NS, 0], start=False, stop=True, skip_group_check=True)
                ins.then_inc(q_["ss_projected"], 1)
            recur(PT, "G")

            for i in range(TILES):
                n = rows(i)
                if i == 0:
                    pe.wait_ge(q_["hb_done"], TILES)
                    pe.wait_ge(q_["o_read"], TILES)
                if i >= 2:
                    pe.wait_ge(q_["ht_ready"], i - 1)
                for k in range(KD):
                    ins = pe.transpose(bank[4 + 2 * (i % 2) + k // 4][:, 128 * (k % 4):128 * (k % 4) + n], hg[0:n, i, 128 * k:128 * k + 128], ident[0:n, 0:n])
                ins.then_inc(q_["h_turned"], 1)
            pe.wait_ge(q_["wout_loaded"], 16)
            for i in range(TILES):
                n = rows(i)
                pe.wait_ge(q_["ht_ready"], i + 1)
                if i >= 2:
                    pe.wait_ge(q_["mix_read"], i - 1)
                for q in range(2):
                    for k in range(KD):
                        ins = pe.matmul(bank[2 * (i % 2) + q][0:n, :], hT[:, k, cols(i)], wout[:, k, 512 * q:512 * q + 512], start=k == 0, stop=k == KD - 1)
                ins.then_inc(q_["mix_projected"], 1)
            for i in range(TILES):
                n = rows(i)
                pe.wait_ge(q_["ln1_done"], i + 1)
                if i >= 2:
                    pe.wait_ge(q_["x1_turned"], i - 1)
                else:
                    pe.wait_ge(q_["ht_ready"], TILES)
                for k in range(KD):
                    ins = pe.transpose(bank[4 + 2 * (i % 2) + k // 4][:, 128 * (k % 4):128 * (k % 4) + n], xln[0:n, i, 128 * k:128 * k + 128], ident[0:n, 0:n])
                ins.then_inc(q_["x1_in_psum"], 1)
            pe.wait_ge(q_["x1_turned"], TILES)
            for i in range(TILES):
                for k in range(KD):
                    ins = pe.matmul(bank[4][0:rows(i), NE * i:NE * i + NE], x1T[:, k, cols(i)], wrt[:, k, :], start=k == 0, stop=k == KD - 1)
            ins.then_inc(q_["routed"], 1)
            pe.wait_ge(q_["routing"], 2)
            for i in range(TILES):
                for i2 in range(i + 1):
                    pe.matmul(bank[5][:, NE * i:NE * i + NE], ones if i2 < i else tri_p[:, 0, :], s01[:, i2, :], start=i2 == 0, stop=i2 == i)
            for i in range(TILES):
                ins = pe.matmul(bank[5][:, NE * TILES:NE * TILES + NE], ones, s01[:, i, :], start=i == 0, stop=i == PT)
            ins.then_inc(q_["routed"], 1)
            for i in range(TILES):
                pe.wait_ge(q_["onehot"], i + 1)
                for e_ in range(NE):
                    ins = pe.matmul(bank[6][0:CAP, 2 * e_:2 * e_ + 2], onehot[0][:, e_, :], tokid[:, i, :], start=i + e_ == 0, stop=i == PT, skip_group_check=True)
                ins.then_inc(q_["onehot_used"], 1)
            pe.wait_ge(q_["routing"], 3)

            def turn(e_, p_):
                pe.wait_ge(xs_loaded[p_], 8 * (e_ - p_) + 16)
                for k in range(KD):
                    ins = pe.transpose(bank[6 + k // 4][:, 128 * (k % 4):128 * (k % 4) + CAP], xs[p_][:, 128 * k:128 * k + 128], ident)
                ins.then_inc(q_["xs_turned"], 1)

            turn(0, 0)
            with pe.Fori(0, NE // 2) as it:
                for p_ in range(2):
                    wg, wu, wd = wexp[p_]
                    pe.wait_ge(wgu_loaded[p_], 32 * it + W0 + 32)
                    pe.wait_ge(q_["xst_ready"], 2 * it + p_ + 1)
                    for hf in range(2):
                        dst = bank[2 * p_ + hf]
                        for g_, w in enumerate((wg, wu)):
                            for f2 in range(2):
                                f = 2 * hf + f2
                                for k in range(KD):
                                    ins = pe.matmul(dst[:, 256 * g_ + 128 * f2:256 * g_ + 128 * f2 + CAP], w[:, k, 128 * f:128 * f + 128], xsT[p_][:, k, :], start=k == 0, stop=k == KD - 1)
                        ins.then_inc(q_["hidden"], 1)
                    if p_ == 0:
                        turn(2 * it + 1, 1)
                    else:
                        turn(2 * it + 2, 0)
                    pe.wait_ge(wd_loaded[p_], 16 * it + W0 + 16)
                    pe.wait_ge(q_["y_slots_ready"], 2 * it + p_)
                    for f in range(NF):
                        if f % 2 == 0:
                            pe.wait_ge(q_["hid_ready"], 4 * it + 2 * p_ + f // 2 + 1)
                        for q in range(2):
                            ins = pe.matmul(bank[4 + q][0:CAP, :], hid[:, f, :], wd[:, f, 512 * q:512 * q + 512], start=f == 0, stop=f == NF - 1)
                    ins.then_inc(q_["down"], 1)
            over = pe.value_load(flagu[0:1, 0:1], min_val=0, max_val=1)
            with pe.If(over):
                for i in range(TILES):
                    n = rows(i)
                    pe.wait_ge(q_["all_x"], 16 * TILES)
                    if i:
                        pe.wait_ge(q_["all_xt"], i)
                    for k in range(KD):
                        ins = pe.transpose(bank[6 + k // 4][:, 128 * (k % 4):128 * (k % 4) + n], dx[0:n, i, 128 * k:128 * k + 128], ident[0:n, 0:n])
                    ins.then_inc(q_["all_turned"], 1)
                pe.wait_ge(q_["all_xt"], TILES)
                with pe.Fori(0, NE) as it:
                    wg, wu, wd = dw
                    pe.wait_ge(q_["all_w"], 48 * it + 48)
                    for f in range(NF):
                        pe.wait_ge(q_["all_hid"], NF * it + f)
                        for k in range(KD):
                            for w, A, B in ((wg, bank[0], bank[1]), (wu, bank[2], bank[3])):
                                pe.matmul(A[:, :], w[:, k, 128 * f:128 * f + 128], dxT[:, k, 0:SEQ], start=k == 0, stop=k == KD - 1)
                                ins = pe.matmul(B[:, 0:NS], w[:, k, 128 * f:128 * f + 128], dxT[:, k, SEQ:N], start=k == 0, stop=k == KD - 1)
                        ins.then_inc(q_["all_hidden"], 1)
                    pe.wait_ge(q_["all_hid"], NF * it + NF)
                    for i in range(TILES):
                        n = rows(i)
                        pe.wait_ge(q_["all_read"], TILES * it + i)
                        for q in range(2):
                            for f in range(NF):
                                ins = pe.matmul(bank[4 + q][0:n, :], dhid[:, f, cols(i)], wd[:, f, 512 * q:512 * q + 512], start=f == 0, stop=f == NF - 1)
                        ins.then_inc(q_["all_down"], 1)


def flat(src, n):
    v = src[0] if len(src.shape) > 1 else src
    if len(v.shape) == 2:
        w = v.shape[1]
        return v.rearrange("a (b f) -> (a b) f", f=128) if w >= 128 else v.rearrange("(a b) c -> a (b c)", b=128 // w)
    return v.rearrange("(a f) -> a f", f=128)


def brow(v, n):
    return v.rearrange("(a n) -> a n", a=1).to_broadcast([128, n])


def arr_off(ap):
    return ap.offset


INS = ["x_prompt", "x_sample", "state_mlstm_C", "state_mlstm_n", "state_mlstm_m", "state_mlstm_conv", "state_rwkv_S",
       "state_rwkv_shift", "ln0_g", "ln0_b", "w_in", "conv_w", "conv_b", "b_i", "b_f", "gn_a_g", "mu_shift", "w0", "w2",
       "a0", "a2", "g2", "k_k", "k_a", "r_k", "lnx_g", "lnx_b", "w_out", "ln1_g", "ln1_b", "w_router", "b_router",
       "we_gate", "we_up", "we_down", "ln2_g", "ln2_b"]
OUTS = [("y_prompt", (1, SEQ, D)), ("y_sample", (NB, LS, D)),
        ("p_C", (1, 1, HA, DHA, DHA)), ("p_n", (1, 1, HA, DHA)), ("p_m", (1, 1, HA)),
        ("p_conv", (1, 1, CW - 1, 2 * DA)), ("p_S", (1, 1, HB, DHB, DHB)), ("p_shift", (1, 1, 14 * 128)),
        ("s_C", (1, NB, HA, DHA, DHA)), ("s_n", (1, NB, HA, DHA)), ("s_m", (1, NB, HA)),
        ("s_conv", (1, NB, CW - 1, 2 * DA)), ("s_S", (1, NB, HB, DHB, DHB)), ("s_shift", (1, NB, 14 * 128))]


def kernel(**inputs):
    import concourse.bacc as bacc
    from concourse.bass_utils import run_bass_kernel_spmd

    nc = bacc.Bacc("TRN2", target_bir_lowering=False, num_devices=1)
    arrays, dr = {}, {}
    for name in INS:
        arrays[name] = np.ascontiguousarray(inputs[name])
        dr[name] = nc.dram_tensor(name, arrays[name].shape, F32, kind="ExternalInput").ap()
    for name, shape in OUTS:
        dr[name] = nc.dram_tensor(name, shape, F32, kind="ExternalOutput").ap()
    for name, shape in SCRATCH.items():
        dr[name] = nc.dram_tensor(name, shape, F32, kind="Internal").ap()
    build(nc, dr)
    got = run_bass_kernel_spmd(nc, [arrays], core_ids=[0]).results[0]
    return tuple(got[name] for name, _ in OUTS)
```

```python
from contextlib import ExitStack
import math

import numpy as np
import concourse.bass as bass
import concourse.mybir as mybir
from concourse.alu_op_type import AluOpType as ALU

F32 = mybir.dt.float32
BF16 = mybir.dt.bfloat16
U32 = mybir.dt.uint32
ACT = mybir.ActivationFunctionType
AX = mybir.AxisListType

D, SEQ, NB, LS = 1024, 512, 8, 8
NS = NB * LS
N = SEQ + NS
TILES = SEQ // 128 + 1
PT = TILES - 1
KD = D // 128
DA, DB = 512, 512
HA, DHA = 4, 128
HB, DHB = 8, 64
NJ = DB // 128
DA_IN = 4 * DA + 2 * HA
NE, EG, NG, DE = 16, 4, 4, 512
ALPHA = 2 ** 0.25
SQRT_E = math.exp(-0.5)
NEG = -1e30
CW = 4
CAP = 128
SCRATCH = {"x_kept": (N, D), "x1_rows": (N, D), "y_slots": (NE * CAP, D)}


def rows(i):
    return 128 if i < PT else NS


def cols(i):
    return slice(128 * i, 128 * i + rows(i))


def build(nc, dr, stage=9):
    with ExitStack() as ctx:
        def sem(name):
            return ctx.enter_context(nc.semaphore(name))

        arena = ctx.enter_context(nc.sbuf_tensor("arena", [128, 53200], F32))
        bank = [ctx.enter_context(nc.psum_tensor(f"bank{i}", [128, 512], F32)) for i in range(8)]
        ends = {}

        class Region:
            def __init__(self, at, size):
                self.at, self.end = at, at + size

            def __call__(self, *dims):
                n = int(np.prod(dims))
                ap = arena[:, self.at:self.at + n]
                self.at += n
                assert self.at <= self.end, (self.at, self.end)
                if len(dims) == 2:
                    ap = ap.rearrange("p (a b) -> p a b", a=dims[0])
                if len(dims) == 3:
                    ap = ap.rearrange("p (a b c) -> p a b c", a=dims[0], b=dims[1])
                return ap

        KEEP, T1, T2 = 26800, 13300, 10800
        keep = Region(0, KEEP)
        ident = keep(128)
        blockones = keep(128)
        neg_p = keep(128)
        neg_s = keep(64)
        tri_p = keep(2, 128)
        tri_s = keep(2, 64)
        lvl = keep(7, 128)
        resets = keep(N)
        sel = keep(HA, 128)
        headsel = keep(2)
        seqmask = keep(NB)
        NPRM = 74
        prmc = keep(NPRM)
        shiftc = keep(14, NB)
        convc = keep(8, NB * 3)
        ncol = keep(NB * HA)
        dprm = keep(24)
        gn_a, lnx_g, lnx_b = keep(DA), keep(DB), keep(DB)
        hg = keep(TILES, D)
        arr = keep(NJ, 2, N)
        nbeta = keep(NJ, N)
        kap = keep(NJ, N)
        vtok = keep(TILES, DB)
        sgl = keep(N)
        g2w = keep(DB)
        bon = keep(TILES, HB)
        S = keep(NJ, 128)
        Sh = keep(NJ, 128)
        shnew = keep(NB + 1, 14)
        cvnew = keep(NB + 1, 3, 8)
        nnew = keep(NB + 1, HA)
        rbm = keep(N)
        wint = keep(N)
        woldb = keep(HA, 12)
        colg = keep(3, TILES, HA)
        em = keep(NJ, PT)
        ec = keep(NJ, 12)
        lmid = keep(NJ, PT)
        pend = keep(NJ, PT)
        mrow = keep(12)
        outs = keep(5, 128)
        mv = keep(TILES, 2)
        st6 = keep(2, 6)
        rstd = keep(TILES)
        prow = keep(128)
        ln_g = arena[:, arr_off(arr):arr_off(arr) + D]
        ln_b = arena[:, arr_off(arr) + D:arr_off(arr) + 2 * D]
        x = hg

        t1 = Region(KEEP, T1)
        raw = [t1(604) for _ in range(2)]
        t1_after_raw = t1.at
        wlal = t1(N)
        w2a2 = t1(DB)
        dt = t1(585)
        r_, kr, vr, ld, a_, L, E1, E2, E3, kk, tmp, sq, nrm, kr2 = (t1(N) for _ in range(14))
        g = Region(t1_after_raw + N + DB + 585, T1)
        shrows, cvrows, nrows = g(14, 128), g(8, 128), g(128)
        g = Region(t1_after_raw + N + DB + 585 + 14 * 128, T1)
        LI, LF, bb, mm, d0, d1, wsr, emt, ta_, tb_ = (g(N) for _ in range(10))
        m0r, mprev, blast, mlast, wold = g(8), g(12), g(12), g(12), g(12)
        gbias, gw = keep(2), g(KD, 64)
        assert g.at <= KEEP + T1

        b = Region(t1_after_raw, T1 - 1208)
        zc, th = b(604), b(604)
        qT, kT = [b(N) for _ in range(2)], [b(N) for _ in range(2)]
        qt = b(N)
        kw, dm, sT = b(TILES, 128), b(TILES, 128), b(TILES, 128)
        C = b(PT, 129)
        C0 = b(NB, 129)
        qpad = b(NB, NS)
        vpad = b(NB, 129)
        hh = b(TILES, 129)
        den, rec = b(TILES), b(TILES)
        c = Region(KEEP, T1)
        xwm = c.at
        X = [c(4, 128) for _ in range(2)]
        W = [c(4, 128) for _ in range(2)]
        MT = [c(4, 128) for _ in range(2)]
        kppad = [Region(xwm + 1024 * w, 1024)(2, NB, 64) for w in range(2)]
        zt = Region(xwm + 2048, 512)(NJ, 2, NS)
        kpt = [c(2, DB) for _ in range(2)]
        ktmp = c(2, NJ, 128)
        Zs, Us = c(DB), c(DB)
        Sld = c(NJ, NB, 64)
        pS = c(NJ, 64)
        gtk = c(DB)
        ssum, sqs = c(HB), c(HB)
        t2 = Region(KEEP + T1, T2)
        xT = t2(KD, N)
        NW = 5
        wring = t2(NW, KD, 128)
        vext = arena[:, 53200 - TILES * HA * 129:].rearrange("p (i h c) -> p i h c", i=TILES, h=HA)
        assert t2.at <= 53200 - TILES * HA * 129
        c = Region(KEEP + T1, T2)
        G = [c(2, HB, 256) for _ in range(2)]
        Y = [c(HB, 128) for _ in range(2)]
        SsT = Region(arr_off(G[1]), 4096)(NJ, NB, 128)
        o = Region(KEEP, T1)
        xln = o(TILES, D)
        l1g, l1b, l2g, l2b = o(D), o(D), o(D), o(D)
        wrt = o(KD, NE)
        wout = arena[:, arr_off(arr):arr_off(arr) + KD * D].rearrange("p (a b) -> p a b", a=KD)
        hT = [Region(at, 4 * N)(4, N) for at in (KEEP + T1, 53200 - 4 * N)]
        x1T = Region(arr_off(hg), TILES * D)(KD, N)
        e = Region(o.at, KEEP + T1 - o.at)
        probs, sl, gate, s01, inb = (e(TILES, NE) for _ in range(5))
        gmax, gsum, gtop = e(TILES, NG), e(TILES, NG), e(TILES, NG)
        t80a, t80b, brr = e(TILES, NE), e(TILES, NE), e(NE)
        one5, slotA, slotB, gA, gB = (e(TILES) for _ in range(5))
        slotAu, slotBu = (e(TILES).bitcast(U32) for _ in range(2))
        idxf, idxu, flagf, flagu = e(NE), e(NE).bitcast(U32), e(1), e(1).bitcast(U32)
        slot0 = keep(NE)
        places = keep(CAP // 2).bitcast(BF16)
        ones = keep(128)
        downcount = keep(EG)
        tokid = keep(TILES).bitcast(BF16).rearrange("p (i c) -> p i c", c=2)
        ranks = e(TILES * NE // 2).bitcast(BF16).rearrange("p (i e) -> p i e", i=TILES)
        onehot = [w(NE * CAP // 2).bitcast(BF16).rearrange("p (e c) -> p e c", e=NE) for w in (e, Region(arr_off(l1g), D), Region(arr_off(l1b), D))]
        e = Region(arr_off(l1g), 2 * D)
        ysb = [e(D) for _ in range(2)]
        e = Region(arr_off(hg), TILES * D)
        xs = [e(D) for _ in range(2)]
        xsT = [e(KD, CAP) for _ in range(2)]
        NF = DE // 128
        hsl, hid = e(2, CAP), e(NF, CAP)
        wexp = []
        for at in (KEEP + T1, arr_off(arr)):
            w = Region(at, 12288)
            wexp.append((w(KD, DE), w(KD, DE), w(NF, D)))
        e = Region(arr_off(arr), 12288)
        ya = [(e(D), e(D)) for _ in range(TILES)]
        e = Region(KEEP + T1, 12288)
        dx, dxT = e(TILES, D), e(KD, N)
        dhs, dgc = e(N), e(TILES)
        e = Region(arr_off(hg), TILES * D)
        dhid = e(NF, N)
        dw = wexp[1]

        class Sems(dict):
            def __missing__(self, name):
                self[name] = ctx.enter_context(nc.semaphore(name))
                return self[name]

        q_ = Sems()
        x_loaded = [q_[f"x_loaded{i}"] for i in range(TILES)]
        w_loaded = [q_[f"w_loaded{i}"] for i in range(NW)]
        wgu_loaded, wd_loaded = w_loaded[0:2], w_loaded[2:4]
        ya_loaded = [q_[f"rows_gathered{i}"] for i in range(TILES)]
        xs_loaded = ya_loaded[0:2]
        block = ctx.enter_context(nc.Block())

        R_, K_, MV, V_, MO = range(5)

        def slot_of(j, what):
            return 2 + 5 * j + what

        def wcol(n):
            j, what = divmod(n - 2, 5)
            if n < 2:
                return DA_IN + 3 * DB + 128 * n
            if n < 22 and what in (MV, MO):
                return (2 + what // MO) * DA + 128 * j
            if n < 22:
                return DA_IN + DB * (R_, K_, V_).index(what) + 128 * j
            return DA * ((n - 22) % 2) + 128 * ((n - 22) // 2)

        def raw_of(n):
            j, what = divmod(n - 2, 5)
            return n if n < 2 else 2 + 3 * j + (R_, K_, V_).index(what) if n < 22 else n - 8

        def shift_tile(n):
            j, what = divmod(n - 2, 5)
            return 12 + n if n < 2 else 4 * (R_, K_, V_).index(what) + j

        SLOTS = 30
        W0 = 16 * (SLOTS // NW)

        def LV(i):
            return 7 if i < PT else 3

        def ix(i, l, q):
            return 14 * i + 2 * l + q

        def ix2(i, l, q):
            return 12 * i + 2 * (l - 1) + q

        def spread(eng, h, w):
            return eng.tensor_tensor(kppad[h % 2][0:NS, w], kpt[PT % 2][0:NS, w, 64 * h:64 * h + 64].unsqueeze(1).to_broadcast([NS, NB, 64]),
                                     seqmask[0:NS].unsqueeze(2).to_broadcast([NS, NB, 64]), ALU.mult)

        def block_of(n, l):
            return (slice(64, 128), slice(0, 64)) if l == 6 else (slice(0, n), slice(0, n))

        def hooks(i, l):
            return ((None, "Z", "U", "O", "G", None, None) if i < PT else ("Z", "U", "O"))[l] if i else None
        MU, CWR, CBR, KKR, KAR, W0R, A0R, RKR = 0, 14, 46, 54, 58, 62, 66, 70
        HW0, HA0, OMKA = 0, 4, 8
        UNITS = PT + 1

        def P(n):
            return prmc[:, n:n + 1]

        def pr(ap):
            return ap[:, 0:SEQ].rearrange("p (c t) -> p c t", c=PT)

        def sa(ap):
            return ap[:, SEQ:N].rearrange("p (b t) -> p b t", b=NB)

        def wide(ap, n):
            return ap.unsqueeze(2).to_broadcast([ap.shape[0], ap.shape[1], n])

        @block.sync
        def _(sp):
            for i in range(TILES):
                src = dr["x_prompt"][0, 128 * i:128 * i + 128, :] if i < PT else dr["x_sample"].rearrange("b t d -> (b t) d")
                sp.dma_start(x[0:rows(i), i, :], src).then_inc(x_loaded[i], 16)
                if i == 0:
                    for ap, name in ((ln_g, "ln0_g"), (ln_b, "ln0_b")):
                        sp.dma_start(ap, brow(dr[name], D)).then_inc(q_["ln0_loaded"], 16)
            for n in range(SLOTS):
                if n >= NW:
                    sp.wait_ge(q_["slot_projected"], n - NW + 1)
                c = wcol(n)
                sp.dma_start(wring[:, n % NW, :, :], dr["w_in"][0, :, c:c + 128].rearrange("(k p) c -> p k c", p=128)).then_inc(w_loaded[n % NW], 16)
                if n == 5:
                    sp.wait_ge(q_["ln0_done"], TILES)
                    for i in range(TILES):
                        sp.dma_start(dr["x_kept"][128 * i:128 * i + rows(i), :], x[0:rows(i), i, :]).then_inc(q_["x_kept"], 16)
                if n == 1:
                    sp.dma_start(w2a2[0:64, :], dr["w2"][0]).then_inc(q_["gn_loaded"], 16)
                    sp.dma_start(w2a2[64:128, :], dr["a2"][0]).then_inc(q_["gn_loaded"], 16)
                    sp.dma_start(g2w, dr["g2"][0]).then_inc(q_["gn_loaded"], 16)
                    for ap, name, w in ((gn_a, "gn_a_g", DA), (lnx_g, "lnx_g", DB), (lnx_b, "lnx_b", DB)):
                        sp.dma_start(ap, brow(dr[name][0], w)).then_inc(q_["gn_loaded"], 16)

            stored = 0

            def store(dst, src, **kw):
                nonlocal stored
                stored += 1
                sp.dma_start(dst, src, **kw).then_inc(q_["stored"], 16)

            sp.wait_ge(q_["outs_ready"], 1)
            store(dr["s_shift"][0].rearrange("b (t f) -> (b t) f", f=128), outs[0:112, 0, :])
            store(dr["p_shift"][0].rearrange("b (t f) -> (b t) f", f=128), outs[112:126, 0, :])
            sc = dr["s_conv"][0].rearrange("b w (c f) -> (b w c) f", f=128)
            store(sc[0:96], outs[0:96, 1, :])
            store(sc[96:192], outs[0:96, 2, :])
            store(dr["p_conv"][0, 0].rearrange("w (c f) -> (w c) f", f=128), outs[0:24, 3, :])
            store(dr["s_n"][0].rearrange("b h d -> (b h) d"), outs[0:32, 4, :])
            store(dr["p_n"][0, 0], outs[32:36, 4, :])
            store(dr["p_m"][0].rearrange("b h -> h b"), mrow[0:HA, 3:4], allow_slow_non_contiguous=True)
            store(dr["s_m"][0].rearrange("b h -> h b"), mrow[0:HA, 4:12], allow_slow_non_contiguous=True)
            sp.wait_ge(q_["cs_stored"], 32 * HA)
            sp.wait_ge(q_["unit_projected"], HA)
            sp.wait_ge(q_["ha_done"], HA)
            for h in range(HB):
                sp.dma_start(Sld[64 * (h % 2):64 * (h % 2) + 64, h // 2, :, :], dr["state_rwkv_S"][0, :, h].rearrange("b v k -> v b k")).then_inc(q_["sst_loaded"], 16)
            sp.wait_ge(q_["zt_projected"], 1)
            sp.wait_ge(q_["grams"], 4 * TILES)
            sp.wait_ge(q_["ktmp_made"], TILES)
            sp.dma_start(wout, dr["w_out"][0].rearrange("(k p) c -> p k c", p=128)).then_inc(q_["wout_loaded"], 16)
            sp.wait_ge(q_["ps_ready"], 1)
            store(dr["p_S"][0, 0].rearrange("(j h) v k -> (h v) j k", h=2), pS)
            for h in range(HB):
                sp.wait_ge(q_["ss_read"], h + 1)
                store(dr["s_S"][0, :, h].rearrange("b v k -> v b k"), Sld[64 * (h % 2):64 * (h % 2) + 64, h // 2, :, :])
            sp.wait_ge(q_["stored"], 16 * stored)
            sp.wait_ge(q_["hb_done"], TILES)
            sp.wait_ge(q_["x_kept"], 16 * TILES)
            for i in range(TILES):
                sp.dma_start(xln[0:rows(i), i, :], dr["x_kept"][128 * i:128 * i + rows(i), :]).then_inc(q_["x_back"], 16)
            for ap, src, w in ((l1g, dr["ln1_g"][0], D), (l1b, dr["ln1_b"][0], D), (l2g, dr["ln2_g"][0], D), (l2b, dr["ln2_b"][0], D), (brr, dr["b_router"], NE)):
                sp.dma_start(ap, brow(src, w)).then_inc(q_["x_back"], 16)
            sp.dma_start(wrt, dr["w_router"].rearrange("(k p) c -> p k c", p=128)).then_inc(q_["x_back"], 16)
            for i in range(TILES):
                sp.wait_ge(q_["ln1_done"], i + 1)
                sp.dma_start(dr["x1_rows"][128 * i:128 * i + rows(i), :], xln[0:rows(i), i, :]).then_inc(q_["x1_stored"], 16)
            sp.wait_ge(q_["mix_projected"], TILES)
            def expert_w(e_, p_):
                wg, wu, wd = wexp[p_]
                for w, name in ((wg, "we_gate"), (wu, "we_up")):
                    sp.dma_start(w, dr[name][0, bass.ds(e_, 1)].rearrange("a (k p) c -> p (a k) c", p=128)).then_inc(wgu_loaded[p_], 16)
                return lambda: sp.dma_start(wd, dr["we_down"][0, bass.ds(e_, 1)].rearrange("a (k p) c -> p (a k) c", p=128)).then_inc(wd_loaded[p_], 16)

            expert_w(0, 0)()
            expert_w(1, 1)()
            with sp.Fori(0, NE // 2 - 1) as it:
                for p_ in range(2):
                    sp.wait_ge(q_["hidden"], 4 * it + 2 * p_ + 2)
                    down = expert_w(2 * it + 2 + p_, p_)
                    sp.wait_ge(q_["down"], 2 * it + p_ + 2)
                    down()
            sp.wait_ge(q_["slots_ready"], 1)
            over = sp.value_load(flagu[0:1, 0:1], min_val=0, max_val=1)
            with sp.If(over):
                sp.wait_ge(q_["combined"], TILES)
                sp.wait_ge(q_["down"], NE + 1)
                for i in range(TILES):
                    sp.dma_start(dx[0:rows(i), i, :], dr["x1_rows"][128 * i:128 * i + rows(i), :]).then_inc(q_["all_x"], 16)
                with sp.Fori(0, NE) as it:
                    sp.wait_ge(q_["all_down"], TILES * it + 1)
                    for w, name in zip(dw, ("we_gate", "we_up", "we_down")):
                        sp.dma_start(w, dr[name][0, bass.ds(it, 1)].rearrange("a (k p) c -> p (a k) c", p=128)).then_inc(q_["all_w"], 16)
            for i in range(TILES):
                sp.wait_ge(q_["y_ready"], i + 1)
                dst = dr["y_prompt"][0, 128 * i:128 * i + 128, :] if i < PT else dr["y_sample"].rearrange("b t d -> (b t) d")
                store(dst, xln[0:rows(i), i, :])
            sp.wait_ge(q_["stored"], 16 * stored)
            sp.wait_ge(q_["cs_stored"], 32 * HA)

        @block.gpsimd
        def _(pool):
            step = [0]

            def link(ins):
                step[0] += 1
                ins.then_inc(q_["pool_step"], 1)
                pool.wait_ge(q_["pool_step"], step[0])

            def keep_where(ap, pattern, base, cm, op=ALU.is_ge, fill=0.0):
                link(pool.affine_select(out=ap, in_=ap, pattern=pattern, compare_op=op, fill=fill, base=base,
                                        channel_multiplier=cm))

            link(pool.memset(ident, 0.0))
            keep_where(ident, [[-1, 128]], 0, 1, ALU.not_equal, 1.0)
            pool.nop().then_inc(q_["ident_ready"], 1)
            for ap in (raw[0], raw[1]):
                link(pool.memset(ap, 0.0))
            link(pool.memset(resets, 1.0))
            link(pool.memset(resets[:, 0:SEQ:128], 0.0))
            link(pool.memset(resets[:, SEQ:N:LS], 0.0))
            link(pool.memset(sel[0:HA], 0.0))
            keep_where(sel[0:HA], [[-1, HA], [0, 128]], 0, 1, ALU.not_equal, 1.0)
            bo = blockones.rearrange("p (a b) -> p a b", a=2)
            link(pool.memset(blockones, 1.0))
            keep_where(bo, [[-64, 2], [0, 64]], 0, 1)
            keep_where(bo, [[64, 2], [0, 64]], 63, -1)
            link(pool.memset(headsel, 1.0))
            keep_where(headsel, [[-64, 2]], 0, 1)
            keep_where(headsel, [[64, 2]], 63, -1)
            link(pool.memset(seqmask, 1.0))
            keep_where(seqmask, [[-LS, NB]], 0, 1)
            keep_where(seqmask, [[LS, NB]], LS - 1, -1)
            link(pool.memset(neg_p, 0.0))
            keep_where(neg_p, [[1, 128]], 0, -1, fill=NEG)
            link(pool.memset(neg_s, 0.0))
            keep_where(neg_s, [[1, NS]], 0, -1, fill=NEG)
            keep_where(neg_s.rearrange("p (b t) -> p b t", b=NB), [[-LS, NB], [0, LS]], 0, 1, fill=NEG)
            keep_where(neg_s.rearrange("p (b t) -> p b t", b=NB), [[LS, NB], [0, LS]], LS - 1, -1, fill=NEG)
            link(pool.memset(tri_p, 1.0))
            link(pool.memset(tri_s, 1.0))
            for tri, n in ((tri_p, 128), (tri_s, NS)):
                keep_where(tri[:, 0, :], [[1, n]], 0, -1, ALU.is_gt)
                keep_where(tri[:, 1, :], [[1, n]], 0, -1)
            for v in range(2):
                ts = tri_s[:, v, :].rearrange("p (b t) -> p b t", b=NB)
                keep_where(ts, [[-LS, NB], [0, LS]], 0, 1)
                keep_where(ts, [[LS, NB], [0, LS]], LS - 1, -1)
            link(pool.memset(lvl, 0.0))
            for l in range(7):
                m = 2 ** l
                up = lvl[:, l, :].rearrange("p (a c b) -> p a c b", c=2, b=m)[:, :, 1, :]
                link(pool.memset(up, 1.0))
                keep_where(up, [[-2 * m, 64 // m], [0, m]], 0, 1)
                keep_where(up, [[2 * m, 64 // m], [0, m]], m - 1, -1)
            link(pool.memset(ones, 1.0))
            link(pool.iota(downcount, [[-1, EG]], base=EG, channel_multiplier=0, allow_small_or_imprecise_dtypes=True))
            link(pool.iota(slot0, [[CAP, NE]], base=1, channel_multiplier=0, allow_small_or_imprecise_dtypes=True))
            link(pool.iota(places, [[1, CAP]], base=0, channel_multiplier=0, allow_small_or_imprecise_dtypes=True))
            link(pool.iota(tokid[:, :, 0], [[0, TILES]], base=0, channel_multiplier=1, allow_small_or_imprecise_dtypes=True))
            link(pool.iota(tokid[:, :, 1], [[1, TILES]], base=0, channel_multiplier=0, allow_small_or_imprecise_dtypes=True))
            pool.nop().then_inc(q_["masks_ready"], 1)

            def collect(n):
                k = raw_of(n)
                pool.wait_ge(q_["slot_read"], n + 1)
                rw = raw[k % 2]
                if n < 22:
                    t = shift_tile(n)
                    pool.tensor_copy(shnew[:, NB, t:t + 1], rw[:, SEQ:SEQ + 1])
                    pool.tensor_copy(shnew[:, 0:NB, t], rw[:, 513:585].rearrange("p (b t) -> p b t", b=NB)[:, :, LS]).then_inc(q_["raw_collected"], 1)
                else:
                    c = 4 * ((n - 22) % 2) + (n - 22) // 2
                    pool.tensor_copy(cvnew[:, NB, :, c], rw[:, SEQ:SEQ + 3])
                    pool.tensor_copy(cvnew[:, 0:NB, :, c], rw[:, 515:603].rearrange("p (b t) -> p b t", b=NB)[:, :, LS:LS + 3]).then_inc(q_["raw_collected"], 1)

            def mlstm_io(h):
                pool.wait_ge(q_["cs_new"], h + 1)
                pool.dma_start(dr["s_C"][0, :, h].rearrange("b d e -> d b e"), C0[:, :, 0:128]).then_inc(q_["cs_stored"], 16)
                pool.wait_ge(q_["c_state"], PT * (h + 1))
                pool.dma_start(dr["p_C"][0, 0, h], C[:, PT - 1, 0:128]).then_inc(q_["cs_stored"], 16)
                if h < HA - 1:
                    pool.wait_ge(q_["cs_stored"], 32 * (h + 1))
                    pool.dma_start(C0[:, :, 0:128], dr["state_mlstm_C"][0, :, h + 1].rearrange("b d e -> d b e")).then_inc(q_["c0_loaded"], 16)

            pool.memset(vext[:, :, :, 128:129], 1.0).then_inc(q_["ones_set"], 1)
            collect(0)
            collect(1)
            for j in range(NJ):
                for what in (R_, K_, V_):
                    collect(slot_of(j, what))
            pool.wait_ge(q_["rwkv_made"], NJ)
            pool.wait_ge(q_["post_projected"], NJ)
            pool.dma_start(C0[:, :, 0:128], dr["state_mlstm_C"][0, :, 0].rearrange("b d e -> d b e")).then_inc(q_["c0_loaded"], 16)
            pool.memset(qpad, 0.0).then_inc(q_["ones_set"], 1)
            for n in range(22, 26):
                collect(n)
            for h in range(HA):
                if h < HA - 2:
                    collect(26 + 2 * h)
                    collect(27 + 2 * h)
                mlstm_io(h)


            pool.wait_ge(q_["ec_ready"], 1)
            pool.wait_ge(q_["unit_projected"], HA)
            for i in range(TILES):
                n = rows(i)
                if i:
                    pool.wait_ge(q_["kt_turned"], i)
                for w, src in enumerate((nbeta, kap)):
                    if i < PT:
                        ins = pool.tensor_tensor(ktmp[:, w, :, :], src[:, :, cols(i)], wide(ec[:, :, i], 128), ALU.mult)
                    else:
                        for j in range(NJ):
                            ins = pool.tensor_tensor(ktmp[:, w, j, 0:NS].rearrange("p (b t) -> p b t", b=NB), sa(src[:, j, :]), wide(ec[:, j, 4:12], LS), ALU.mult)
                ins.then_inc(q_["ktmp_made"], 1)
                for l in range(LV(i)):
                    for q in range(2):
                        k = ix(i, l, q)
                        if l == 0:
                            pool.wait_ge(q_["gram_read"], 4 * i + 2 * q + 1)
                        if k >= 2:
                            pool.wait_ge(q_["w_projected"], k - 1)
                        if l == 1:
                            pool.wait_ge(q_["yx_read"], k - 1)
                        pool.tensor_tensor(MT[q][0:n, :, 0:n], G[i % 2][0:n, 0, 4 * q:4 * q + 4, 0:n],
                                           lvl[0:n, l, 0:n].unsqueeze(1).to_broadcast([n, 4, n]), ALU.mult).then_inc(q_["mt_ready"], 1)
            pool.wait_ge(q_["o_projected"], PT)
            link(pool.memset(SsT, 0.0))
            pool.wait_ge(q_["yx_read"], ix(PT, 2, 1) + 1)
            pool.wait_ge(q_["w_projected"], ix(PT, 2, 1) + 1)
            pool.wait_ge(q_["yx_projected"], ix2(PT, 2, 1) + 1)
            pool.nop().then_inc(q_["sst_zero"], 1)
            for h in range(HB):
                if h == 0:
                    pool.wait_ge(q_["kt_read"], TILES)
                if h >= 2:
                    pool.wait_ge(q_["ss_projected"], h - 1)
                spread(pool, h, 1).then_inc(q_["kp_spread"], 1)


            pool.wait_ge(q_["routing"], 3)
            pool.wait_ge(q_["x1_stored"], 16 * TILES)
            for e_ in range(NE + 1):
                if e_ >= 2:
                    pool.wait_ge(q_["xs_turned"], e_ - 1)
                else:
                    pool.wait_ge(q_["routed"], 1)
                pool.indirect_dma_start(out=xs[e_ % 2], out_offset=None, in_=dr["x1_rows"], in_offset=bass.IndirectOffsetOnAxis(ap=idxu[:, e_ % NE:e_ % NE + 1], axis=0)).then_inc(xs_loaded[e_ % 2], 16)
            pool.wait_ge(q_["y_stored"], 16 * NE + 16)
            pool.wait_ge(q_["slots_ready"], 1)
            for i in range(TILES):
                n = rows(i)
                for dst, ix_ in zip(ya[i], (slotAu, slotBu)):
                    pool.indirect_dma_start(out=dst[0:n], out_offset=None, in_=dr["y_slots"], in_offset=bass.IndirectOffsetOnAxis(ap=ix_[0:n, i:i + 1], axis=0)).then_inc(ya_loaded[i], 16)
            for i in range(TILES):
                n = rows(i)
                pool.wait_ge(q_["y_gained"], i + 1)
                pool.tensor_tensor(xln[0:n, i, :], xln[0:n, i, :], l2b[0:n], ALU.add).then_inc(q_["y_ready"], 1)

        @block.scalar
        def _(act):
            step = [0]

            def link(ins):
                step[0] += 1
                ins.then_inc(q_["act_step"], 1)
                act.wait_ge(q_["act_step"], step[0])

            act.wait_ge(q_["gw_zero"], 1)
            for v, name in ((0, "b_i"), (1, "b_f")):
                act.dma_start(gw[:, :, 32 * v:32 * v + HA], dr["w_in"][0, :, 4 * DA + HA * v:4 * DA + HA * v + HA].rearrange("(k p) c -> p k c", p=128)).then_inc(q_["gate_loaded"], 16)
                act.dma_start(gbias[0:HA, v:v + 1], dr[name].rearrange("a h -> h a"), allow_slow_non_contiguous=True).then_inc(q_["gate_loaded"], 16)
            act.dma_start(m0r[0:HA, :], dr["state_mlstm_m"][0].rearrange("b h -> h b"), allow_slow_non_contiguous=True).then_inc(q_["gate_loaded"], 16)
            act.dma_start(shrows[0:NB, :, :], dr["state_rwkv_shift"][0].rearrange("b (a f) -> b a f", f=128)).then_inc(q_["hist_loaded"], 16)
            act.dma_start(cvrows[0:24, :, :], dr["state_mlstm_conv"][0].rearrange("b w (a f) -> (b w) a f", f=128)).then_inc(q_["hist_loaded"], 16)
            act.dma_start(nrows[0:NB * HA, :], dr["state_mlstm_n"][0].rearrange("b h d -> (b h) d")).then_inc(q_["hist_loaded"], 16)
            for k, (name, at) in enumerate((("mu_shift", MU), ("conv_w", CWR), ("conv_b", CBR), ("k_k", KKR),
                                            ("k_a", KAR), ("w0", W0R), ("a0", A0R), ("r_k", RKR))):
                src = dr[name]
                n = int(np.prod(src.shape)) // 128
                act.dma_start(prow[at:at + n, :], flat(src, n)).then_inc(q_["prm_loaded"], 16)
            act.wait_ge(q_["x_moments"], 1)
            act.activation(rstd, mv[:, :, 1], ACT.Sqrt).then_inc(q_["x_std"], 1)
            act.wait_ge(q_["x_scales"], 1)
            for i in range(TILES):
                xi = x[0:rows(i), i, :]
                act.activation(xi, xi, ACT.Identity, bias=mv[0:rows(i), i, 0:1], scale=rstd[0:rows(i), i:i + 1]).then_inc(q_["x_normed"], 1)
            for i in range(TILES):
                act.wait_ge(q_["x_turned"], i + 1)
                for q in range(2):
                    v = bank[2 * (i % 2) + q].rearrange("p (a b) -> p a b", a=4)[:, :, 0:rows(i)]
                    ins = act.copy(xT[:, 4 * q:4 * q + 4, cols(i)], v)
                ins.then_inc(q_["xt_ready"], 1)

            def to_raw(n):
                k = raw_of(n)
                act.wait_ge(q_["slot_projected"], n + 1)
                if k >= 2:
                    act.wait_ge(q_["raw_used"], k - 1)
                    act.wait_ge(q_["raw_collected"], k - 1)
                elif k == 0:
                    act.wait_ge(q_["masks_ready"], 1)
                    act.wait_ge(q_["cols_ready"], 1)
                rw, A, B = raw[k % 2], bank[2 * (n % 2)], bank[2 * (n % 2) + 1]
                if n < 22:
                    sv = rw[:, 513:585].rearrange("p (b t) -> p b t", b=NB)
                    act.copy(sv[:, :, 0], shiftc[:, shift_tile(n), :])
                    act.copy(rw[:, 1:513], A[:, :])
                    act.copy(sv[:, :, 1:9], B[:, 0:NS].rearrange("p (b t) -> p b t", b=NB)).then_inc(q_["slot_read"], 1)
                else:
                    sv = rw[:, 515:603].rearrange("p (b t) -> p b t", b=NB)
                    c = 4 * ((n - 22) % 2) + (n - 22) // 2
                    if k < 16:
                        act.copy(rw[:, 0:3], resets[:, 0:SEQ:128][:, 0:3])
                    act.copy(sv[:, :, 0:3], convc[:, c, :].rearrange("p (b w) -> p b w", b=NB))
                    act.copy(rw[:, 3:515], A[:, :])
                    act.copy(sv[:, :, 3:11], B[:, 0:NS].rearrange("p (b t) -> p b t", b=NB)).then_inc(q_["slot_read"], 1)

            act.wait_ge(q_["gate_steps"], 1)
            act.activation(ta_[0:HA, :], ta_[0:HA, :], ACT.Exp).then_inc(q_["gate_exps"], 1)
            act.wait_ge(q_["gate_steps"], 2)
            act.activation(tb_[0:HA, :], ta_[0:HA, :], ACT.Ln).then_inc(q_["gate_exps"], 1)
            to_raw(0)
            act.wait_ge(q_["gate_steps"], 3)
            act.activation(wint[0:HA, :], wint[0:HA, :], ACT.Exp)
            act.activation(wsr[0:HA, :], wsr[0:HA, :], ACT.Exp)
            act.activation(emt[0:HA, :], mm[0:HA, :], ACT.Exp, scale=-1.0)
            act.activation(wold[0:HA, :], wold[0:HA, :], ACT.Exp).then_inc(q_["gate_exps"], 1)
            to_raw(1)
            act.wait_ge(q_["gates_on_pe"], 3)
            for a in range(3):
                act.copy(colg[:, a, 0:PT, :], bank[5][:, 20 * a:20 * a + 16].rearrange("p (i h) -> p i h", h=HA))
                act.copy(colg[0:NS, a, PT, :], bank[5][0:NS, 20 * a + 16:20 * a + 20])
            act.copy(woldb, bank[5][:, 64:112].rearrange("p (h c) -> p h c", h=HA)).then_inc(q_["gate_exps"], 1)
            act.wait_ge(q_["shifted"], 2)
            act.activation(wlal[0:64, :], wlal[0:64, :], ACT.Tanh)
            act.activation(sgl, sgl, ACT.Tanh, scale=0.5).then_inc(q_["lora_in"], 1)

            def exps(j):
                act.wait_ge(q_["decay_args"], j + 1)
                act.activation(E1, tmp, ACT.Exp)
                act.activation(E2, L, ACT.Exp)
                act.activation(E3, L, ACT.Exp, scale=-1.0)
                act.activation(em[:, j, :], lmid[:, j, :], ACT.Exp).then_inc(q_["decays"], 1)

            def post(j):
                act.wait_ge(q_["post_projected"], j + 1)
                act.copy(bon[:, 0:PT, 2 * j:2 * j + 2], bank[7][:, 0:8].rearrange("p (i h) -> p i h", h=2))
                act.copy(bon[0:NS, PT, 2 * j:2 * j + 2], bank[7][0:NS, 8:10])
                act.copy(vtok[:, 0:PT, 128 * j:128 * j + 128], bank[6].rearrange("p (i f) -> p i f", i=PT))
                act.copy(vtok[0:NS, PT, 128 * j:128 * j + 128], bank[7][0:NS, 128:256]).then_inc(q_["post_read"], 1)

            def to_heads(j, what):
                n = slot_of(j, what)
                act.wait_ge(q_["slot_projected"], n + 1)
                A, B = bank[2 * (n % 2)].rearrange("p (i f) -> p i f", i=PT), bank[2 * (n % 2) + 1][0:NS, 0:128]
                if what == MV:
                    act.copy(vext[:, 0:PT, j, 0:128], A)
                    act.copy(vext[0:NS, PT, j, 0:128], B).then_inc(q_["slot_read"], 1)
                else:
                    if j == 0:
                        act.wait_ge(q_["x_kept"], 16 * TILES)
                    act.activation(hg[:, 0:PT, 128 * j:128 * j + 128], A, ACT.Tanh, scale=0.5)
                    act.activation(hg[0:NS, PT, 128 * j:128 * j + 128], B, ACT.Tanh, scale=0.5).then_inc(q_["slot_read"], 1)

            for j in range(NJ):
                to_raw(slot_of(j, R_))
                to_raw(slot_of(j, K_))
                to_heads(j, MV)
                if j:
                    post(j - 1)
                to_raw(slot_of(j, V_))
                act.wait_ge(q_["lora_projected"], j + 1)
                if j:
                    act.wait_ge(q_["rwkv_made"], j)
                for dst, A, B, hb in ((ld, bank[4], bank[5][:, 0:NS], HW0), (a_, bank[6], bank[7][:, 256:256 + NS], HA0)):
                    act.activation(dst[:, 0:SEQ], A[:, :], ACT.Tanh, bias=dprm[:, hb + j:hb + j + 1], scale=0.5)
                    ins = act.activation(dst[:, SEQ:N], B, ACT.Tanh, bias=dprm[:, hb + j:hb + j + 1], scale=0.5)
                ins.then_inc(q_["tanhs"], 1)
                to_heads(j, MO)
                exps(j)
                act.wait_ge(q_["norms_projected"], j + 1)
                act.activation(nrm[:, 0:SEQ], bank[4][:, :], ACT.Sqrt)
                act.activation(nrm[:, SEQ:N], bank[5][:, 0:NS], ACT.Sqrt).then_inc(q_["norms"], 1)

            def silu_tanh(k):
                act.wait_ge(q_["raw_used"], 15 + k)
                act.activation(th, zc, ACT.Tanh, scale=0.5).then_inc(q_["silu_tanh"], 1)

            def head_std(h):
                act.wait_ge(q_["ha_moments"], h + 1)
                act.activation(rstd, mv[:, :, 1], ACT.Sqrt).then_inc(q_["ha_std"], 1)

            def unit(h):
                act.wait_ge(q_["k_turned"], h + 1)
                if h:
                    act.wait_ge(q_["unit_projected"], h)
                for i in range(TILES):
                    n = rows(i)
                    src = bank[6][:, 128 * i:128 * i + 128] if i < PT else bank[7][0:NS, 0:128]
                    ins = act.activation(kw[0:n, i, :], src, ACT.Copy, scale=colg[0:n, 1, i, h:h + 1])
                ins.then_inc(q_["k_tokens"], 1)
                if h:
                    head_std(h - 1)
                if h < HA - 2:
                    to_raw(26 + 2 * h)
                act.wait_ge(q_["scores"], h + 1)
                for i in range(TILES):
                    n = rows(i)
                    src = bank[6][:, 128 * i:128 * i + 128] if i < PT else bank[7][0:NS, 128:192]
                    ins = act.activation(dm[0:n, i, 0:n], src, ACT.Exp, bias=colg[0:n, 0, i, h:h + 1])
                ins.then_inc(q_["weights"], 1)
                if h < HA - 1:
                    silu_tanh(2 * h + 2)
                act.wait_ge(q_["numerator"], 2 * h + 1)
                if h:
                    act.wait_ge(q_["ha_done"], h)
                act.copy(hh[:, 0:3, :], bank[4][:, 0:387].rearrange("p (i c) -> p i c", i=3))
                act.wait_ge(q_["numerator"], 2 * h + 2)
                act.copy(hh[:, 3, :], bank[5][:, 0:129])
                act.copy(hh[0:NS, PT, :], bank[5][0:NS, 129:258]).then_inc(q_["num_read"], 1)
                if h < HA - 1:
                    silu_tanh(2 * h + 3)
                if h < HA - 2:
                    to_raw(27 + 2 * h)

            to_raw(22)
            to_raw(23)
            post(NJ - 1)
            act.activation(ec, ec, ACT.Exp).then_inc(q_["ec_ready"], 1)
            silu_tanh(0)
            to_raw(24)
            silu_tanh(1)
            to_raw(25)
            for h in range(HA):
                unit(h)



            def recur(i, what):
                if what is None:
                    return
                n = rows(i)
                if what == "Z":
                    act.wait_ge(q_["z_projected"], i + 1)
                    act.copy(Zs[0:n], bank[6][0:n, :]).then_inc(q_["z_read"], 1)
                if what == "O":
                    act.wait_ge(q_["o_projected"], i + 1)
                    act.copy(hg[0:n, i, DA:D], bank[6 if i < PT else 4][0:n, :]).then_inc(q_["o_read"], 1)
                if what == "G":
                    act.wait_ge(q_["hb_moments"], i + 1)
                    act.activation(sqs[0:n], sqs[0:n], ACT.Sqrt, scale=1.0 / DHB).then_inc(q_["hb_std"], 1)

            for i in range(TILES):
                act.wait_ge(q_["kt_turned"], i + 1)
                n = rows(i)
                if i >= 2:
                    act.wait_ge(q_["s_projected"], i - 1)
                for w in range(2):
                    ins = act.copy(kpt[i % 2][0:n, w, :], bank[2 + w][0:n, :])
                ins.then_inc(q_["kt_read"], 1)
                for l in range(LV(i)):
                    for q in range(2):
                        if i == 0 and l == 3 and q == 0:
                            head_std(HA - 1)
                        if l:
                            hi, lo = block_of(n, l)
                            act.wait_ge(q_["w_projected"], ix(i, l, q) + 1)
                            act.copy(W[q][hi, :, lo], bank[q][hi, :].rearrange("p (h t) -> p h t", h=4)[:, :, lo]).then_inc(q_["w_read"], 1)
                    recur(i - 1, hooks(i, l))
            recur(PT - 1, "G")
            for j in range(NJ):
                act.wait_ge(q_["st_turned"], j + 1)
                act.wait_ge(q_["sst_zero"], 1)
                act.copy(SsT[0:64, j, :, 0:64], bank[2 * (j % 2)][0:64, :].rearrange("p (b v) -> p b v", b=NB))
                act.copy(SsT[64:128, j, :, 64:128], bank[2 * (j % 2) + 1][64:128, :].rearrange("p (b v) -> p b v", b=NB)).then_inc(q_["st_read"], 1)
            act.wait_ge(q_["zt_projected"], 1)
            act.copy(zt, bank[6].rearrange("p (j v t) -> p j v t", j=NJ, v=2)).then_inc(q_["zt_ready"], 1)
            recur(PT, "Z")
            recur(PT, "O")
            recur(PT, "G")


            def h_copy(i):
                n = rows(i)
                act.wait_ge(q_["h_turned"], i + 1)
                if i == 0:
                    act.wait_ge(q_["ss_projected"], HB)
                for q in range(2):
                    v = bank[4 + 2 * (i % 2) + q].rearrange("p (a b) -> p a b", a=4)[:, :, 0:n]
                    ins = act.copy(hT[q][:, :, cols(i)], v)
                ins.then_inc(q_["ht_ready"], 1)

            def row_std(stat, n):
                act.wait_ge(q_["ln_moments"], stat)
                act.activation(rstd[0:n, 0:1], mv[0:n, 0, 1:2], ACT.Sqrt).then_inc(q_["ln_std"], 1)

            h_copy(0)
            h_copy(1)
            for i in range(TILES):
                if i + 2 < TILES:
                    h_copy(i + 2)
                row_std(i + 1, rows(i))
            for i in range(TILES):
                n = rows(i)
                act.wait_ge(q_["x1_in_psum"], i + 1)
                for q in range(2):
                    v = bank[4 + 2 * (i % 2) + q].rearrange("p (a b) -> p a b", a=4)[:, :, 0:n]
                    ins = act.copy(x1T[:, 4 * q:4 * q + 4, cols(i)], v)
                ins.then_inc(q_["x1_turned"], 1)
            act.wait_ge(q_["routing"], 1)
            act.activation(probs, probs, ACT.Exp).then_inc(q_["probs_exp"], 1)

            def xs_copy(e_, p_):
                act.wait_ge(q_["xs_turned"], e_ + 1)
                for q in range(2):
                    ins = act.copy(xsT[p_][:, 4 * q:4 * q + 4, :], bank[6 + q].rearrange("p (k c) -> p k c", k=4))
                ins.then_inc(q_["xst_ready"], 1)

            xs_copy(0, 0)
            act.nop().then_inc(q_["y_slots_ready"], 1)
            act.nop().then_inc(q_["y_stored"], 16)
            with act.Fori(0, NE // 2) as it:
                for p_ in range(2):
                    for hf in range(2):
                        act.wait_ge(q_["hidden"], 4 * it + 2 * p_ + hf + 1)
                        act.wait_ge(q_["hid_ready"], 4 * it + 2 * p_ + hf + 1)
                        act.activation(hsl, bank[2 * p_ + hf][:, 0:256].rearrange("p (f c) -> p f c", f=2), ACT.Silu).then_inc(q_["hid_silu"], 1)
                    xs_copy(2 * it + p_ + 1, 1 - p_)
                    act.wait_ge(q_["down"], 2 * it + p_ + 2)
                    act.wait_ge(q_["y_stored"], 32 * it + 16 * p_ + 16)
                    act.copy(ysb[0][:, 0:512], bank[4][:, :])
                    act.copy(ysb[0][:, 512:1024], bank[5][:, :]).then_inc(q_["y_slots_ready"], 1)
                    act.wait_ge(q_["y_slots_ready"], 2 * it + p_ + 2)
                    act.dma_start(dr["y_slots"].rearrange("(e c) d -> e c d", c=CAP)[bass.ds(2 * it + p_, 1)].rearrange("a c d -> (a c) d"), ysb[0]).then_inc(q_["y_stored"], 16)
            act.wait_ge(q_["slots_ready"], 1)
            over = act.value_load(flagu[0:1, 0:1], min_val=0, max_val=1)
            with act.If(over):
                act.wait_ge(q_["combined"], TILES)
                for i in range(TILES):
                    n = rows(i)
                    act.wait_ge(q_["all_turned"], i + 1)
                    for q in range(2):
                        v = bank[6 + q].rearrange("p (a b) -> p a b", a=4)[:, :, 0:n]
                        ins = act.copy(dxT[:, 4 * q:4 * q + 4, cols(i)], v)
                    ins.then_inc(q_["all_xt"], 1)
                with act.Fori(0, NE) as it:
                    for f in range(NF):
                        act.wait_ge(q_["all_hidden"], NF * it + f + 1)
                        act.wait_ge(q_["all_hid"], NF * it + f + 1)
                        act.activation(dhs[:, 0:SEQ], bank[0][:, :], ACT.Silu)
                        act.activation(dhs[:, SEQ:N], bank[1][:, 0:NS], ACT.Silu).then_inc(q_["all_silu"], 1)
            for i in range(TILES):
                n = rows(i)
                act.wait_ge(q_["ln_moments"], TILES + i + 1)
                act.activation(rstd[0:n, i:i + 1], mv[0:n, i, 1:2], ACT.Sqrt).then_inc(q_["ln_std"], 1)
                act.wait_ge(q_["y_scales"], i + 1)
                y = xln[0:n, i, :]
                act.activation(y, y, ACT.Identity, bias=mv[0:n, i, 0:1], scale=rstd[0:n, i:i + 1]).then_inc(q_["y_normed"], 1)
        @block.vector
        def _(dve):
            step = [0]

            def link(ins):
                step[0] += 1
                ins.then_inc(q_["dve_step"], 1)
                dve.wait_ge(q_["dve_step"], step[0])

            dve.memset(gw, 0.0).then_inc(q_["gw_zero"], 1)
            link(dve.memset(mv, 1.0))
            link(dve.memset(colg, 1.0))
            dve.memset(hg[64:128, PT, :], 0.0)
            st2 = st6
            for i in range(TILES):
                dve.wait_ge(x_loaded[i], 16)
                n = rows(i)
                for q in range(2):
                    ins = dve.bn_stats(out=st2[0:n, q, :], in_=x[0:n, i, 512 * q:512 * q + 512])
                link(ins)
                link(dve.bn_aggr(out=mv[0:n, i, :], in_=st2[0:n]))
            link(dve.tensor_scalar(mv[:, :, 1], mv[:, :, 1], 1e-5, None, ALU.add))
            dve.nop().then_inc(q_["x_moments"], 1)
            dve.wait_ge(q_["x_std"], 1)
            link(dve.reciprocal(rstd, rstd))
            dve.scalar_tensor_tensor(out=mv[:, :, 0], in0=mv[:, :, 0], scalar=-1.0, in1=rstd, op0=ALU.mult, op1=ALU.mult).then_inc(q_["x_scales"], 1)
            dve.wait_ge(q_["ln0_loaded"], 32)
            for i in range(TILES):
                n = rows(i)
                xi = x[0:n, i, :]
                dve.wait_ge(q_["x_normed"], i + 1)
                link(dve.tensor_tensor(xi, xi, ln_g[0:n], ALU.mult))
                dve.tensor_tensor(xi, xi, ln_b[0:n], ALU.add).then_inc(q_["ln0_done"], 1)
            dve.wait_ge(q_["gates_on_pe"], 1)
            dve.tensor_copy(prmc, bank[4][:, 0:NPRM])
            dve.tensor_copy(shiftc, bank[4][:, 74:186].rearrange("p (a b) -> p a b", a=14))
            dve.tensor_copy(convc, bank[4][:, 186:378].rearrange("p (a b) -> p a b", a=8))
            dve.tensor_copy(ncol, bank[4][:, 378:410]).then_inc(q_["cols_ready"], 1)
            dve.wait_ge(q_["cols_ready"], 1)
            dve.tensor_scalar(dprm[:, HW0:HW0 + 4], prmc[:, W0R:W0R + 4], 0.5, None, ALU.mult)
            dve.tensor_scalar(dprm[:, HA0:HA0 + 4], prmc[:, A0R:A0R + 4], 0.5, None, ALU.mult)
            link(dve.tensor_scalar(dprm[:, OMKA:OMKA + 4], prmc[:, KAR:KAR + 4], -1.0, 1.0, ALU.mult, ALU.add))

            def shift(n, dst):
                dve.wait_ge(q_["slot_read"], n + 1)
                k = raw_of(n)
                rw, m = raw[k % 2], P(MU + shift_tile(n))
                rs = rw[:, 513:585].rearrange("p (b t) -> p b t", b=NB)
                link(dve.tensor_tensor(dt[:, 0:584], rw[:, 0:584], rw[:, 1:585], ALU.subtract))
                ds = dt[:, 513:585].rearrange("p (b t) -> p b t", b=NB)
                dve.scalar_tensor_tensor(out=dst[:, 0:SEQ], in0=dt[:, 0:SEQ], scalar=m, in1=rw[:, 1:513], op0=ALU.mult, op1=ALU.add)
                dve.scalar_tensor_tensor(out=sa(dst), in0=ds[:, :, 0:LS], scalar=m, in1=rs[:, :, 1:9], op0=ALU.mult, op1=ALU.add).then_inc(q_["raw_used"], 1)
                dve.wait_ge(q_["raw_used"], k + 1)

            def gate_rows():
                R = slice(0, HA)
                dve.wait_ge(q_["gates_on_pe"], 2)
                dve.wait_ge(q_["gate_loaded"], 80)
                dve.tensor_scalar(LI[R, 0:SEQ], bank[6][R, :], gbias[R, 0:1], None, ALU.add)
                dve.tensor_scalar(LI[R, SEQ:N], bank[7][R, 0:NS], gbias[R, 0:1], None, ALU.add)
                dve.tensor_copy(LF[R, 0:SEQ], bank[6][32:32 + HA, :])
                link(dve.tensor_copy(LF[R, SEQ:N], bank[7][32:32 + HA, 0:NS]))
                link(dve.tensor_scalar(LF[R], LF[R], gbias[R, 1:2], None, ALU.add))
                dve.scalar_tensor_tensor(out=ta_[R], in0=LF[R], scalar=-1.0, in1=LF[R], op0=ALU.mult, op1=ALU.min).then_inc(q_["gate_steps"], 1)
                dve.wait_ge(q_["gate_exps"], 1)
                dve.tensor_scalar(ta_[R], ta_[R], 1.0, None, ALU.add).then_inc(q_["gate_steps"], 1)
                dve.wait_ge(q_["gate_exps"], 2)
                link(dve.scalar_tensor_tensor(out=LF[R], in0=LF[R], scalar=0.0, in1=tb_[R], op0=ALU.min, op1=ALU.subtract))
                dve.wait_ge(q_["masks_ready"], 1)
                dve.tensor_tensor_scan(bb[R], resets[R], LF[R], 0.0, ALU.mult, ALU.add)
                dve.tensor_copy(d0[R], LF[R])
                dve.tensor_copy(d1[R], LI[R])
                link(dve.tensor_tensor(mprev[R, 4:12], LF[R, SEQ:N:LS], m0r[R], ALU.add))
                link(dve.tensor_tensor(d1[R, SEQ:N:LS], mprev[R, 4:12], LI[R, SEQ:N:LS], ALU.max))
                link(dve.memset(d0[R, SEQ:N:LS], NEG))
                link(dve.tensor_tensor_scan(mm[R], d0[R], d1[R], 0.0, ALU.add, ALU.max))
                dve.memset(mprev[R, 0:1], 0.0)
                dve.tensor_copy(mprev[R, 1:4], mm[R, 127:384:128])
                dve.tensor_copy(mprev[R, 4:12], m0r[R])
                for dst, src in ((blast, bb), (mlast, mm)):
                    dve.tensor_copy(dst[R, 0:4], src[R, 127:SEQ:128])
                    ins = dve.tensor_copy(dst[R, 4:12], src[R, SEQ + LS - 1:N:LS])
                link(ins)
                dve.tensor_copy(mrow[R], mlast[R])
                link(dve.tensor_tensor(blast[R], blast[R], mlast[R], ALU.subtract))
                dve.tensor_tensor(wold[R], blast[R], mprev[R], ALU.add)
                link(dve.tensor_tensor(rbm[R], bb[R], mm[R], ALU.subtract))
                dve.tensor_tensor(pr(wint[R]), pr(rbm[R]), wide(mprev[R, 0:4], 128), ALU.add)
                dve.tensor_tensor(sa(wint[R]), sa(rbm[R]), wide(mprev[R, 4:12], LS), ALU.add)
                link(dve.tensor_tensor(LI[R], LI[R], bb[R], ALU.subtract))
                dve.tensor_tensor(pr(wsr[R]), pr(LI[R]), wide(blast[R, 0:4], 128), ALU.add)
                dve.tensor_tensor(sa(wsr[R]), sa(LI[R]), wide(blast[R, 4:12], LS), ALU.add).then_inc(q_["gate_steps"], 1)

            gate_rows()
            dve.wait_ge(q_["gn_loaded"], 96)
            dve.wait_ge(q_["gates_on_pe"], 3)
            shift(0, wlal)
            shift(1, sgl)
            dve.nop().then_inc(q_["shifted"], 2)
            dve.wait_ge(q_["lora_in"], 1)
            dve.tensor_scalar(sgl, sgl, 0.5, 0.5, ALU.mult, ALU.add)

            c1 = 0.5 * SQRT_E
            for j in range(NJ):
                if j:
                    dve.wait_ge(q_["post_projected"], j)
                shift(slot_of(j, R_), r_)
                shift(slot_of(j, K_), kr)
                link(dve.tensor_scalar(kk, kr, P(KKR + j), None, ALU.mult))
                dve.tensor_tensor(sq, kk, kk, ALU.mult).then_inc(q_["squares"], 1)
                dve.wait_ge(q_["tanhs"], j + 1)
                dve.tensor_scalar(a_, a_, 0.5, 0.5, ALU.mult, ALU.add)
                link(dve.tensor_scalar(ld, ld, -c1, -c1, ALU.mult, ALU.add))
                link(dve.tensor_tensor_scan(L, resets, ld, 0.0, ALU.mult, ALU.add))
                dve.tensor_copy(ec[:, j, 4:12], L[:, SEQ + LS - 1:N:LS])
                link(dve.tensor_copy(lmid[:, j, :], L[:, 63:SEQ:128]))
                link(dve.tensor_tensor(pr(L), pr(L), wide(lmid[:, j, :], 128), ALU.subtract))
                dve.tensor_copy(ec[:, j, 0:4], L[:, 127:SEQ:128])
                dve.tensor_tensor(tmp, L, ld, ALU.subtract).then_inc(q_["decay_args"], 1)
                shift(slot_of(j, V_), vr)
                dve.wait_ge(q_["norms"], j + 1)
                link(dve.tensor_scalar(nrm, nrm, 1e-12, None, ALU.max))
                link(dve.reciprocal(nrm, nrm))
                link(dve.tensor_tensor(kk, kk, nrm, ALU.mult))
                dve.wait_ge(q_["decays"], j + 1)
                dve.tensor_tensor(arr[:, j, 0, :], kk, E1, ALU.mult)
                dve.tensor_tensor(arr[:, j, 1, :], r_, E2, ALU.mult)
                link(dve.tensor_tensor(tmp, kk, a_, ALU.mult))
                link(dve.scalar_tensor_tensor(out=nbeta[:, j, :], in0=tmp, scalar=-1.0, in1=E3, op0=ALU.mult, op1=ALU.mult))
                link(dve.tensor_scalar(tmp, a_, P(KAR + j), dprm[:, OMKA + j:OMKA + j + 1], ALU.mult, ALU.add))
                link(dve.tensor_tensor(kr2, kr, tmp, ALU.mult))
                dve.tensor_tensor(kap[:, j, :], kr2, E3, ALU.mult)
                dve.scalar_tensor_tensor(out=nrm, in0=r_, scalar=P(RKR + j), in1=kr2, op0=ALU.mult, op1=ALU.mult).then_inc(q_["rwkv_made"], 1)

            def conv_tap(h, p_, t):
                n, k = 22 + 2 * h + p_, 14 + 2 * h + p_
                rw, c = raw[k % 2], 4 * p_ + h
                if t == 0:
                    dve.wait_ge(q_["slot_read"], n + 1)
                    link(dve.tensor_scalar(zc[:, 0:600], rw[:, 0:600], P(CWR + c), P(CBR + c), ALU.mult, ALU.add))
                    return
                ins = dve.scalar_tensor_tensor(out=zc[:, 0:600], in0=rw[:, t:600 + t], scalar=P(CWR + 8 * t + c), in1=zc[:, 0:600],
                                               op0=ALU.mult, op1=ALU.add)
                if t < CW - 1:
                    link(ins)
                else:
                    ins.then_inc(q_["raw_used"], 1)

            def conv_silu(h, p_):
                dst = (kT if p_ else qT)[h % 2]
                dve.wait_ge(q_["silu_tanh"], 2 * h + p_ + 1)
                sc = 0.5 * (DHA ** -0.5 if p_ else 1.0)
                link(dve.tensor_scalar(th, th, sc, sc, ALU.mult, ALU.add))
                if h >= 2:
                    dve.wait_ge(q_["unit_projected"], h - 1)
                dve.tensor_tensor(dst[:, 0:SEQ], th[:, 0:SEQ], zc[:, 0:SEQ], ALU.mult)
                sv = [a[:, 515:603].rearrange("p (b t) -> p b t", b=NB)[:, :, 0:LS] for a in (th, zc)]
                dve.tensor_tensor(sa(dst), sv[0], sv[1], ALU.mult).then_inc(q_["qk_ready"], 1)
                dve.wait_ge(q_["qk_ready"], 2 * h + p_ + 1)

            def conv(h, p_):
                for t in range(CW):
                    conv_tap(h, p_, t)
                conv_silu(h, p_)

            def head_norm(h, part):
                hv = hh[:, :, 0:128]
                if part == 0:
                    dve.wait_ge(q_["num_read"], h + 1)
                    link(dve.scalar_tensor_tensor(out=den, in0=hh[:, :, 128], scalar=-1.0, in1=hh[:, :, 128], op0=ALU.mult, op1=ALU.max))
                    link(dve.tensor_tensor(den, den, colg[:, 2, :, h], ALU.max))
                    link(dve.reciprocal(rec, den))
                    link(dve.tensor_tensor(hv, hv, wide(rec, 128), ALU.mult))
                if part == 1:
                    for i in range(TILES):
                        link(dve.bn_stats(out=st2[:, i % 2, :], in_=hh[:, i, 0:128]))
                        ins = dve.bn_aggr(out=mv[:, i, :], in_=st2[:, i % 2, :])
                    link(ins)
                    dve.tensor_scalar(mv[:, :, 1], mv[:, :, 1], 1e-6, None, ALU.add).then_inc(q_["ha_moments"], 1)
                    link(dve.tensor_tensor(hv, hv, wide(mv[:, :, 0], 128), ALU.subtract))
                if part == 2:
                    dve.wait_ge(q_["ha_std"], h + 1)
                    link(dve.reciprocal(rstd, rstd))
                    link(dve.tensor_tensor(hv, hv, wide(rstd, 128), ALU.mult))
                if part == 3:
                    link(dve.tensor_tensor(hv, hv, gn_a[:, 128 * h:128 * h + 128].unsqueeze(1).to_broadcast([128, TILES, 128]), ALU.mult))
                    hgh = hg[:, :, 128 * h:128 * h + 128]
                    dve.tensor_tensor(hgh, hgh, hv, ALU.mult).then_inc(q_["ha_done"], 1)

            def unit(h):
                if h:
                    dve.wait_ge(q_["unit_projected"], h)
                dve.wait_ge(q_["rows_spread"], h + 1)
                dve.tensor_tensor(qt[:, 0:SEQ], qT[h % 2][:, 0:SEQ], bank[4][:, :], ALU.mult)
                link(dve.tensor_tensor(qt[:, SEQ:N], qT[h % 2][:, SEQ:N], bank[5][:, 0:NS], ALU.mult))
                dve.wait_ge(q_["ones_set"], 2)
                o0 = arr_off(qpad)
                diag = arena[:, o0:o0 + NB * 72].rearrange("p (b t) -> p b t", t=72)[:, :, 0:LS]
                dve.tensor_copy(diag, sa(qt)).then_inc(q_["q_scaled"], 1)
                if h:
                    for part in range(4):
                        head_norm(h - 1, part)
                if h < HA - 1:
                    for t in range(CW):
                        conv_tap(h + 1, 0, t)
                dve.tensor_tensor(vpad[0:NS], vext[0:NS, PT, h, :].unsqueeze(1).to_broadcast([NS, NB, 129]),
                                  seqmask[0:NS].unsqueeze(2).to_broadcast([NS, NB, 129]), ALU.mult)
                dve.wait_ge(q_["c0_loaded"], 16 * (h + 1))
                dve.tensor_copy(C0[:, :, 128], ncol.rearrange("p (b h) -> p b h", h=HA)[:, :, h]).then_inc(q_["v_spread"], 1)
                dve.wait_ge(q_["weights"], h + 1)
                dve.tensor_tensor(sT[:, 0:PT, :], bank[4].rearrange("p (i t) -> p i t", i=PT), dm[:, 0:PT, :], ALU.mult)
                dve.tensor_tensor(sT[0:NS, PT, 0:NS], bank[5][0:NS, NS:2 * NS], dm[0:NS, PT, 0:NS], ALU.mult).then_inc(q_["weighted"], 1)
                if h:
                    dve.wait_ge(q_["cs_stored"], 32 * h)
                dve.wait_ge(q_["c_delta"], h + 1)
                for i in range(PT):
                    dl = bank[6][:, 129 * i:129 * i + 129] if i < 3 else bank[7][:, 256:385]
                    if i == 0:
                        ins = dve.tensor_copy(C[:, 0, :], dl)
                    else:
                        ins = dve.scalar_tensor_tensor(out=C[:, i, :], in0=C[:, i - 1, :], scalar=woldb[:, h, i:i + 1], in1=dl, op0=ALU.mult, op1=ALU.add)
                    ins.then_inc(q_["c_state"], 1)
                    dve.wait_ge(q_["c_state"], PT * h + i + 1)
                dve.tensor_copy(nnew[:, NB, h:h + 1], C[:, PT - 1, 128:129])
                if h < HA - 1:
                    conv_silu(h + 1, 0)
                    for t in range(CW):
                        conv_tap(h + 1, 1, t)
                dve.wait_ge(q_["cs_delta"], h + 1)
                for b in range(NB):
                    src = (bank[5], bank[6], bank[7])[b // 3][:, 129 * (b % 3):129 * (b % 3) + 129]
                    ins = dve.scalar_tensor_tensor(out=C0[:, b, :], in0=C0[:, b, :], scalar=woldb[:, h, PT + b:PT + b + 1], in1=src, op0=ALU.mult, op1=ALU.add)
                ins.then_inc(q_["cs_new"], 1)
                dve.wait_ge(q_["cs_new"], h + 1)
                dve.tensor_copy(nnew[:, 0:NB, h], C0[:, :, 128]).then_inc(q_["n_new"], 1)
                if h < HA - 1:
                    conv_silu(h + 1, 1)

            dve.wait_ge(q_["post_projected"], NJ)
            link(dve.memset(hh, 1.0))
            conv(0, 0)
            conv(0, 1)
            dve.wait_ge(q_["slot_read"], slot_of(NJ - 1, MO) + 1)
            dve.wait_ge(q_["gn_loaded"], 96)
            link(dve.tensor_scalar(hg[:, :, 0:DA], hg[:, :, 0:DA], 0.5, 0.5, ALU.mult, ALU.add))
            for h in range(HA):
                unit(h)


            dve.wait_ge(q_["outs_turned"], 1)
            for a, n in enumerate((126, 96, 96, 24)):
                dve.tensor_copy(outs[0:n, a, :], bank[5][0:n, 128 * a:128 * a + 128])
            dve.tensor_copy(outs[0:36, 4, :], bank[4][0:36, 0:128]).then_inc(q_["outs_ready"], 1)
            dve.wait_ge(q_["ec_ready"], 1)
            dve.tensor_tensor(pend, em, ec[:, :, 0:PT], ALU.mult)
            dve.memset(S, 0.0)
            link(dve.memset(Sh, 0.0))

            def recur(i, what):
                if what is None:
                    return
                n = rows(i)
                fv = hg[0:n, i, DA:D]
                hv = fv.rearrange("p (h v) -> p h v", h=HB)
                gv = gtk[0:n].rearrange("p (h v) -> p h v", h=HB)
                if what == "U":
                    dve.wait_ge(q_["u_projected"], i + 1)
                    dve.tensor_copy(Us[0:n], bank[7][0:n, :]).then_inc(q_["u_read"], 1)
                if what == "O" and i < PT:
                    dve.wait_ge(q_["s_projected"], i + 1)
                    link(dve.tensor_tensor(S, S, wide(pend[:, :, i], 128), ALU.mult))
                    pv = bank[7].rearrange("p (j v) -> p j v", j=NJ)
                    dve.tensor_tensor(S[0:64, :, 0:64], S[0:64, :, 0:64], pv[0:64, :, 0:64], ALU.add)
                    link(dve.tensor_tensor(S[64:128, :, 64:128], S[64:128, :, 64:128], pv[64:128, :, 64:128], ALU.add))
                    if i < PT - 1:
                        dve.tensor_tensor(Sh, S, wide(em[:, :, i + 1], 128), ALU.mult)
                    dve.nop().then_inc(q_["state"], 1)
                if what == "G":
                    dve.wait_ge(q_["o_read"], i + 1)
                    link(dve.tensor_reduce(ssum[0:n], hv, AX.X, ALU.add))
                    link(dve.tensor_scalar(ssum[0:n], ssum[0:n], 1.0 / DHB, None, ALU.mult))
                    link(dve.tensor_tensor(hv, hv, wide(ssum[0:n], DHB), ALU.subtract))
                    link(dve.tensor_tensor(gv, hv, hv, ALU.mult))
                    link(dve.tensor_reduce(sqs[0:n], gv, AX.X, ALU.add))
                    dve.tensor_scalar(sqs[0:n], sqs[0:n], DHB * 64e-5, None, ALU.add).then_inc(q_["hb_moments"], 1)
                if what == "H":
                    link(dve.tensor_tensor(gv, vtok[0:n, i, :].rearrange("p (h v) -> p h v", h=HB), wide(bon[0:n, i, :], DHB), ALU.mult))
                    link(dve.tensor_tensor(gtk[0:n], gtk[0:n], lnx_b[0:n], ALU.add))
                    dve.wait_ge(q_["hb_std"], i + 1)
                    link(dve.reciprocal(sqs[0:n], sqs[0:n]))
                    link(dve.tensor_tensor(hv, hv, wide(sqs[0:n], DHB), ALU.mult))
                    link(dve.tensor_tensor(fv, fv, lnx_g[0:n], ALU.mult))
                    link(dve.tensor_tensor(fv, fv, gtk[0:n], ALU.add))
                    dve.wait_ge(q_["g_projected"], i + 1)
                    dve.tensor_tensor(fv, fv, bank[7][0:n, :], ALU.mult).then_inc(q_["hb_done"], 1)

            for i in range(TILES):
                n = rows(i)
                tri = tri_p if i < PT else tri_s
                if i >= 2:
                    dve.wait_ge(q_["o_projected"], i - 1)
                for s_ in range(4):
                    q, w = s_ // 2, s_ % 2
                    dve.wait_ge(q_["grams"], 4 * i + s_ + 1)
                    for odd in range(2):
                        src = bank[2 * (s_ % 3) + odd][0:n, :].rearrange("p (h v t) -> p h v t", h=2, v=2)[:, :, :, 0:n]
                        dst = G[i % 2][0:n, w, 4 * q + odd:4 * q + 4:2, :].rearrange("p h (v t) -> p h v t", v=2)[:, :, :, 0:n]
                        ins = dve.tensor_tensor(dst, src, tri[0:n].unsqueeze(1).to_broadcast([n, 2, 2, n]), ALU.mult)
                    ins.then_inc(q_["gram_read"], 1)
                for l in range(LV(i)):
                    for q in range(2):
                        k = ix(i, l, q)
                        Yq = Y[i % 2][0:n, 4 * q:4 * q + 4, 0:n]
                        if l == 0:
                            idn = ident[0:n, 0:n].unsqueeze(1).to_broadcast([n, 4, n])
                            dve.wait_ge(q_["mt_ready"], k + 1)
                            dve.tensor_tensor(Yq, MT[q][0:n, :, 0:n], idn, ALU.add)
                            dve.wait_ge(q_["w_projected"], k + 1)
                            dve.tensor_tensor(X[q][0:n, :, 0:n], bank[q][0:n, :].rearrange("p (h t) -> p h t", h=4)[:, :, 0:n], idn, ALU.add).then_inc(q_["yx_read"], 1)
                        else:
                            dve.wait_ge(q_["yx_projected"], ix2(i, l, q) + 1)
                            pv = [bank[b_][0:n, :].rearrange("p (h t) -> p h t", h=4)[:, :, 0:n] for b_ in (2 + q, 4 + q)]
                            if l == 6:
                                Yq, pv[0] = Yq[0:64, :, 64:128], pv[0][0:64, :, 64:128]
                            ins = dve.tensor_tensor(Yq, Yq, pv[0], ALU.add)
                            if l < LV(i) - 1:
                                ins = dve.tensor_tensor(X[q][0:n, :, 0:n], X[q][0:n, :, 0:n], pv[1], ALU.add)
                            ins.then_inc(q_["yx_read"], 1)
                    if i == 0 and 1 <= l <= 4:
                        head_norm(HA - 1, l - 1)
                    recur(i - 1, hooks(i, l))
                    if hooks(i, l) == "G":
                        recur(i - 1, "H")
            recur(PT - 1, "G")
            recur(PT - 1, "H")
            dve.wait_ge(q_["sst_zero"], 1)
            dve.wait_ge(q_["ps_projected"], 1)
            for h2 in range(2):
                r = slice(64 * h2, 64 * h2 + 64)
                ins = dve.tensor_copy(pS[r], bank[5][r, 0:256].rearrange("p (j k) -> p j k", j=NJ))
            ins.then_inc(q_["ps_ready"], 1)
            recur(PT, "U")
            dve.tensor_tensor(SsT[:, :, :, :], SsT[:, :, :, :], ec[:, :, 4:12].unsqueeze(3).to_broadcast([128, NJ, NB, 128]), ALU.mult).then_inc(q_["sst_scaled"], 1)
            dve.wait_ge(q_["kt_read"], TILES)
            for h in range(2):
                spread(dve, h, 0).then_inc(q_["kb_spread"], 1)
            for h in range(HB):
                r = slice(64 * (h % 2), 64 * (h % 2) + 64)
                dve.wait_ge(q_["ss_projected"], h + 1)
                dve.tensor_copy(Sld[r, h // 2, :, :], bank[h % 4][r, :].rearrange("p (b k) -> p b k", b=NB)).then_inc(q_["ss_read"], 1)
                if h < HB - 2:
                    spread(dve, h + 2, 0).then_inc(q_["kb_spread"], 1)
            recur(PT, "G")
            recur(PT, "H")

            def norm_rows(y, n, stat):
                for q in range(2):
                    ins = dve.bn_stats(out=st2[0:n, q, :], in_=y[:, 512 * q:512 * q + 512])
                link(ins)
                link(dve.bn_aggr(out=mv[0:n, 0, :], in_=st2[0:n]))
                dve.tensor_scalar(mv[0:n, 0, 1:2], mv[0:n, 0, 1:2], 1e-5, None, ALU.add).then_inc(q_["ln_moments"], 1)
                link(dve.scalar_tensor_tensor(out=y, in0=y, scalar=mv[0:n, 0, 0:1], in1=l1g[0:n], op0=ALU.subtract, op1=ALU.mult))
                dve.wait_ge(q_["ln_std"], stat)
                link(dve.reciprocal(rstd[0:n, 0:1], rstd[0:n, 0:1]))
                dve.scalar_tensor_tensor(out=y, in0=y, scalar=rstd[0:n, 0:1], in1=l1b[0:n], op0=ALU.mult, op1=ALU.add).then_inc(q_["ln1_done"], 1)

            dve.wait_ge(q_["x_back"], 16 * (TILES + 6))
            for i in range(TILES):
                n = rows(i)
                y = xln[0:n, i, :]
                dve.wait_ge(q_["mix_projected"], i + 1)
                for q in range(2):
                    b_ = 2 * (i % 2) + q
                    yq = y[:, 512 * q:512 * q + 512]
                    ins = dve.scalar_tensor_tensor(out=yq, in0=yq, scalar=ALPHA, in1=bank[b_][0:n, :], op0=ALU.mult, op1=ALU.add)
                ins.then_inc(q_["mix_read"], 1)
                dve.wait_ge(q_["mix_read"], i + 1)
                norm_rows(y, n, i + 1)
            dve.wait_ge(q_["ln1_done"], TILES)
            link(dve.memset(probs, 0.0))
            dve.wait_ge(q_["routed"], 1)
            lv = bank[4][:, 0:TILES * NE].rearrange("p (i e) -> p i e", i=TILES)
            dve.tensor_copy(probs[:, 0:PT, :], lv[:, 0:PT, :])
            link(dve.tensor_copy(probs[0:NS, PT, :], lv[0:NS, PT, :]))
            link(dve.tensor_reduce(one5, probs, AX.X, ALU.max))
            dve.tensor_tensor(probs, probs, wide(one5, NE), ALU.subtract).then_inc(q_["routing"], 1)
            dve.wait_ge(q_["probs_exp"], 1)
            link(dve.tensor_reduce(one5, probs, AX.X, ALU.add))
            link(dve.reciprocal(one5, one5))
            link(dve.tensor_tensor(probs, probs, wide(one5, NE), ALU.mult))
            link(dve.tensor_tensor(sl, probs, brr.unsqueeze(1).to_broadcast([128, TILES, NE]), ALU.add))

            def grp(ap):
                return ap.rearrange("p i (g e) -> p (i g) e", g=NG)

            def f1(ap):
                return ap.rearrange("p i g -> p (i g)")

            def first_of(dst, src, top, scratch, n):
                link(dve.tensor_tensor(dst, src, wide(top, n), ALU.is_ge))
                link(dve.tensor_tensor(dst, dst, downcount[:, EG - n:EG].unsqueeze(1).to_broadcast([128, dst.shape[1], n]), ALU.mult))
                link(dve.tensor_reduce(scratch, dst, AX.X, ALU.max))
                link(dve.tensor_tensor(dst, dst, wide(scratch, n), ALU.is_equal))

            link(dve.tensor_reduce(f1(gmax), grp(sl), AX.X, ALU.max))
            first_of(grp(t80a), grp(sl), f1(gmax), f1(gsum), EG)
            link(dve.scalar_tensor_tensor(out=t80b, in0=t80a, scalar=NEG, in1=sl, op0=ALU.mult, op1=ALU.add))
            link(dve.tensor_reduce(f1(gsum), grp(t80b), AX.X, ALU.max))
            link(dve.tensor_tensor(gmax, gmax, gsum, ALU.add))
            link(dve.tensor_copy(f1(gtop), f1(gsum)))
            first_of(grp(gate), grp(t80b), f1(gtop), f1(gsum), EG)
            link(dve.tensor_tensor(gate, gate, t80a, ALU.add))
            link(dve.tensor_reduce(one5, gmax, AX.X, ALU.max))
            first_of(gtop, gmax, one5, slotA, NG)
            link(dve.tensor_tensor(grp(gate), grp(gate), wide(f1(gtop), EG), ALU.mult))
            link(dve.memset(gate[64:128, PT, :], 0.0))
            dve.tensor_copy(s01, gate).then_inc(q_["routing"], 1)
            link(dve.tensor_tensor(gate, gate, probs, ALU.mult))
            link(dve.tensor_reduce(one5, gate, AX.X, ALU.add))
            link(dve.tensor_scalar(one5, one5, 1e-37, None, ALU.max))
            link(dve.reciprocal(one5, one5))
            link(dve.tensor_tensor(gate, gate, wide(one5, NE), ALU.mult))
            dve.wait_ge(q_["routed"], 2)
            rk = bank[5][:, 0:TILES * NE].rearrange("p (i e) -> p i e", i=TILES)
            link(dve.tensor_reduce(flagf, bank[5][:, TILES * NE:TILES * NE + NE], AX.X, ALU.max))
            dve.tensor_scalar(flagu, flagf, CAP + 0.5, None, ALU.is_gt)
            link(dve.scalar_tensor_tensor(out=inb, in0=rk, scalar=CAP - 0.5, in1=s01, op0=ALU.is_lt, op1=ALU.mult))
            link(dve.tensor_tensor(t80a, rk, slot0.unsqueeze(1).to_broadcast([128, TILES, NE]), ALU.add))
            link(dve.tensor_tensor(sl, t80a, inb, ALU.mult))
            link(dve.scalar_tensor_tensor(out=t80b, in0=rk, scalar=1.0, in1=inb, op0=ALU.add, op1=ALU.mult))
            link(dve.tensor_scalar(ranks, t80b, -1.0, None, ALU.add))
            for i in range(TILES):
                if i >= 3:
                    dve.wait_ge(q_["onehot_used"], i - 2)
                dve.tensor_tensor(onehot[i % 3], places.unsqueeze(1).to_broadcast([128, NE, CAP]), ranks[:, i, :].unsqueeze(2).to_broadcast([128, NE, CAP]), ALU.is_equal).then_inc(q_["onehot"], 1)
            dve.wait_ge(q_["onehot_used"], TILES)
            iv = bank[6][:, 0:2 * NE].rearrange("p (e c) -> p e c", c=2)
            link(dve.tensor_scalar(idxf, iv[:, :, 1], 128.0, None, ALU.mult))
            dve.tensor_tensor(idxu, idxf, iv[:, :, 0], ALU.add).then_inc(q_["routing"], 1)
            link(dve.tensor_reduce(slotA, sl, AX.X, ALU.max))
            link(dve.tensor_reduce(slotB, sl, AX.X, ALU.add))
            link(dve.tensor_tensor(slotB, slotB, slotA, ALU.subtract))
            link(dve.tensor_tensor(t80a, sl, wide(slotA, NE), ALU.is_equal))
            link(dve.tensor_tensor(t80a, t80a, inb, ALU.mult))
            link(dve.tensor_tensor(t80b, inb, t80a, ALU.subtract))
            link(dve.tensor_tensor(t80a, t80a, gate, ALU.mult))
            link(dve.tensor_tensor(t80b, t80b, gate, ALU.mult))
            link(dve.tensor_reduce(gA, t80a, AX.X, ALU.add))
            link(dve.tensor_reduce(gB, t80b, AX.X, ALU.add))
            dve.tensor_scalar(slotAu, slotA, -1.0, 0.0, ALU.add, ALU.max)
            dve.tensor_scalar(slotBu, slotB, -1.0, 0.0, ALU.add, ALU.max).then_inc(q_["slots_ready"], 1)
            link(dve.tensor_tensor(s01, s01, inb, ALU.subtract))
            link(dve.tensor_tensor(s01, s01, gate, ALU.mult))
            dve.wait_ge(q_["x1_turned"], TILES)
            dve.wait_ge(q_["x1_stored"], 16 * TILES)
            for i in range(TILES):
                n = rows(i)
                ins = dve.tensor_scalar(xln[0:n, i, :], xln[0:n, i, :], ALPHA, None, ALU.mult)
            link(ins)
            dve.nop().then_inc(q_["hid_ready"], 1)
            with dve.Fori(0, NE // 2) as it:
                for p_ in range(2):
                    for hf in range(2):
                        dve.wait_ge(q_["hid_silu"], 4 * it + 2 * p_ + hf + 1)
                        dve.wait_ge(q_["down"], 2 * it + p_ + 1)
                        dve.tensor_tensor(hid[:, 2 * hf:2 * hf + 2, :], hsl, bank[2 * p_ + hf][:, 256:512].rearrange("p (f c) -> p f c", f=2), ALU.mult).then_inc(q_["hid_ready"], 1)
            def combine(i):
                n = rows(i)
                dve.wait_ge(ya_loaded[i], 32 + (16 * (NE // 2 + 1 - i) if i < 2 else 0))
                y = xln[0:n, i, :]
                link(dve.scalar_tensor_tensor(out=y, in0=ya[i][0][0:n], scalar=gA[0:n, i:i + 1], in1=y, op0=ALU.mult, op1=ALU.add))
                dve.scalar_tensor_tensor(out=y, in0=ya[i][1][0:n], scalar=gB[0:n, i:i + 1], in1=y, op0=ALU.mult, op1=ALU.add).then_inc(q_["combined"], 1)
                dve.wait_ge(q_["combined"], i + 1)

            def last_moments(i):
                n = rows(i)
                y = xln[0:n, i, :]
                for q in range(2):
                    ins = dve.bn_stats(out=st2[0:n, q, :], in_=y[:, 512 * q:512 * q + 512])
                link(ins)
                link(dve.bn_aggr(out=mv[0:n, i, :], in_=st2[0:n]))
                dve.tensor_scalar(mv[0:n, i, 1:2], mv[0:n, i, 1:2], 1e-5, None, ALU.add).then_inc(q_["ln_moments"], 1)

            def last_scales(i):
                n = rows(i)
                dve.wait_ge(q_["ln_std"], TILES + i + 1)
                link(dve.reciprocal(rstd[0:n, i:i + 1], rstd[0:n, i:i + 1]))
                dve.scalar_tensor_tensor(out=mv[0:n, i, 0:1], in0=mv[0:n, i, 0:1], scalar=-1.0, in1=rstd[0:n, i:i + 1], op0=ALU.mult, op1=ALU.mult).then_inc(q_["y_scales"], 1)

            def last_gain(i):
                n = rows(i)
                dve.wait_ge(q_["y_normed"], i + 1)
                dve.tensor_tensor(xln[0:n, i, :], xln[0:n, i, :], l2g[0:n], ALU.mult).then_inc(q_["y_gained"], 1)

            def last_norms(ready):
                for i in range(TILES):
                    ready(i)
                    last_moments(i)
                    if i:
                        last_gain(i - 1)
                    last_scales(i)
                last_gain(PT)

            over = dve.value_load(flagu[0:1, 0:1], min_val=0, max_val=1)
            steps_before = step[0]
            with dve.If(over):
                for i in range(TILES):
                    combine(i)
                dve.nop().then_inc(q_["all_hid"], 1)
                dve.nop().then_inc(q_["all_read"], 1)
                with dve.Fori(0, NE) as it:
                    dve.wait_ge(q_["all_read"], TILES * it + 1)
                    dve.tensor_copy(dgc.unsqueeze(2), s01[:, :, bass.ds(it, 1)]).then_inc(q_["all_gate"], 1)
                    dve.wait_ge(q_["all_gate"], it + 1)
                    for f in range(NF):
                        dve.wait_ge(q_["all_silu"], NF * it + f + 1)
                        dve.tensor_tensor(dhid[:, f, 0:SEQ], dhs[:, 0:SEQ], bank[2][:, :], ALU.mult)
                        dve.tensor_tensor(dhid[:, f, SEQ:N], dhs[:, SEQ:N], bank[3][:, 0:NS], ALU.mult).then_inc(q_["all_hid"], 1)
                    for i in range(TILES):
                        n = rows(i)
                        dve.wait_ge(q_["all_down"], TILES * it + i + 2)
                        for q in range(2):
                            yq = xln[0:n, i, 512 * q:512 * q + 512]
                            ins = dve.scalar_tensor_tensor(out=yq, in0=bank[4 + q][0:n, :], scalar=dgc[0:n, i:i + 1], in1=yq, op0=ALU.mult, op1=ALU.add)
                        ins.then_inc(q_["all_read"], 1)
                dve.wait_ge(q_["all_read"], TILES * NE + 1)
                last_norms(lambda i: None)
            step[0] = steps_before
            with dve.Else():
                last_norms(combine)

        @block.tensor
        def _(pe):
            pe.wait_ge(q_["ident_ready"], 1)
            for i in range(TILES):
                n = rows(i)
                pe.wait_ge(q_["ln0_done"], i + 1)
                if i >= 2:
                    pe.wait_ge(q_["xt_ready"], i - 1)
                for k in range(KD):
                    ins = pe.transpose(bank[2 * (i % 2) + k // 4][:, 128 * (k % 4):128 * (k % 4) + n], x[0:n, i, 128 * k:128 * k + 128], ident[0:n, 0:n])
                ins.then_inc(q_["x_turned"], 1)
            pe.wait_ge(q_["prm_loaded"], 128)
            pe.wait_ge(q_["hist_loaded"], 48)
            pe.transpose(bank[4][:, 0:NPRM], prow[0:NPRM, :], ident[0:NPRM, 0:NPRM])
            for t in range(14):
                pe.transpose(bank[4][:, 74 + 8 * t:82 + 8 * t], shrows[0:NB, t, :], ident[0:NB, 0:NB])
            for t in range(8):
                pe.transpose(bank[4][:, 186 + 24 * t:210 + 24 * t], cvrows[0:24, t, :], ident[0:24, 0:24])
            pe.transpose(bank[4][:, 378:410], nrows[0:32, :], ident[0:32, 0:32]).then_inc(q_["gates_on_pe"], 1)
            pe.wait_ge(q_["xt_ready"], TILES)
            pe.wait_ge(q_["gate_loaded"], 80)
            for k in range(KD):
                pe.matmul(bank[6][0:64, :], gw[:, k, :], xT[:, k, 0:SEQ], start=k == 0, stop=k == KD - 1)
                ins = pe.matmul(bank[7][0:64, 0:NS], gw[:, k, :], xT[:, k, SEQ:N], start=k == 0, stop=k == KD - 1)
            ins.then_inc(q_["gates_on_pe"], 1)

            def slot(n):
                pe.wait_ge(w_loaded[n % NW], 16 * (n // NW + 1))
                if n >= 2:
                    pe.wait_ge(q_["slot_read"], n - 1)
                A, B = bank[2 * (n % 2)], bank[2 * (n % 2) + 1]
                w = wring[:, n % NW]
                if 2 <= n < 22 and (n - 2) % 5 in (MV, MO):
                    for i in range(TILES):
                        dst = A[:, 128 * i:128 * i + 128] if i < PT else B[0:NS, 0:128]
                        for k in range(KD):
                            ins = pe.matmul(dst, xT[:, k, cols(i)], w[:, k, :], start=k == 0, stop=k == KD - 1)
                else:
                    for k in range(KD):
                        pe.matmul(A[:, :], w[:, k, :], xT[:, k, 0:SEQ], start=k == 0, stop=k == KD - 1)
                        ins = pe.matmul(B[:, 0:NS], w[:, k, :], xT[:, k, SEQ:N], start=k == 0, stop=k == KD - 1)
                ins.then_inc(q_["slot_projected"], 1)

            def both(A, B, lhs, rhs):
                pe.matmul(A, lhs, rhs[:, 0:SEQ], start=True, stop=True)
                return pe.matmul(B, lhs, rhs[:, SEQ:N], start=True, stop=True)

            slot(0)
            slot(1)
            pe.wait_ge(q_["gate_exps"], 3)
            for a, src in enumerate((LI, wsr, emt)):
                for i in range(TILES):
                    pe.transpose(bank[5][0:rows(i), 20 * a + 4 * i:20 * a + 4 * i + 4], src[0:HA, cols(i)], ident[0:HA, 0:HA])
            for h in range(HA):
                ins = pe.matmul(bank[5][:, 64 + 12 * h:76 + 12 * h], sel[0:HA, h, :], wold[0:HA, :], start=True, stop=True)
            ins.then_inc(q_["gates_on_pe"], 1)
            pe.wait_ge(q_["gate_exps"], 4)

            def post(j):
                pe.wait_ge(q_["rwkv_made"], j + 1)
                for i in range(TILES):
                    pe.matmul(bank[7][0:rows(i), 2 * i:2 * i + 2], nrm[:, cols(i)], headsel, start=True, stop=True)
                for i in range(TILES):
                    dst = bank[6][:, 128 * i:128 * i + 128] if i < PT else bank[7][0:NS, 128:256]
                    ins = pe.transpose(dst, vr[:, cols(i)], ident)
                ins.then_inc(q_["post_projected"], 1)

            for j in range(NJ):
                slot(slot_of(j, R_))
                slot(slot_of(j, K_))
                slot(slot_of(j, MV))
                if j:
                    post(j - 1)
                slot(slot_of(j, V_))
                if j == 0:
                    pe.wait_ge(q_["lora_in"], 1)
                else:
                    pe.wait_ge(q_["norms"], j)
                    pe.wait_ge(q_["post_read"], j)
                both(bank[4][:, :], bank[5][:, 0:NS], w2a2[0:64, 128 * j:128 * j + 128], wlal[0:64])
                both(bank[6][:, :], bank[7][:, 256:256 + NS], w2a2[64:128, 128 * j:128 * j + 128], wlal[64:128]).then_inc(q_["lora_projected"], 1)
                slot(slot_of(j, MO))
                pe.wait_ge(q_["squares"], j + 1)
                pe.wait_ge(q_["tanhs"], j + 1)
                both(bank[4][:, :], bank[5][:, 0:NS], blockones, sq).then_inc(q_["norms_projected"], 1)

            def unit(h):
                if h == 0:
                    pe.wait_ge(q_["post_read"], NJ)
                    pe.wait_ge(q_["norms"], NJ)
                else:
                    pe.wait_ge(q_["cs_new"], h)
                    pe.wait_ge(q_["num_read"], h)
                pe.wait_ge(q_["gate_exps"], 3)
                both(bank[4][:, :], bank[5][:, 0:NS], sel[0:HA, h, :], wint[0:HA]).then_inc(q_["rows_spread"], 1)
                pe.wait_ge(q_["qk_ready"], 2 * h + 2)
                for i in range(TILES):
                    dst = bank[6][:, 128 * i:128 * i + 128] if i < PT else bank[7][0:NS, 0:128]
                    ins = pe.transpose(dst, kT[h % 2][:, cols(i)], ident)
                ins.then_inc(q_["k_turned"], 1)
                if h < HA - 2:
                    slot(26 + 2 * h)
                pe.wait_ge(q_["q_scaled"], h + 1)
                pe.wait_ge(q_["k_tokens"], h + 1)
                for i in range(TILES):
                    n = rows(i)
                    kq = bank[4][:, 128 * i:128 * i + 128] if i < PT else bank[5][0:NS, NS:2 * NS]
                    dd = bank[6][:, 128 * i:128 * i + 128] if i < PT else bank[7][0:NS, 128:192]
                    pe.matmul(kq, kT[h % 2][:, cols(i)], qT[h % 2][:, cols(i)], start=True, stop=True)
                    pe.matmul(dd, sel[0:HA, h, 0:n], rbm[0:HA, cols(i)], start=True, stop=False)
                    ins = pe.matmul(dd, ident[0:n, 0:n], neg_p if i < PT else neg_s[0:NS], start=False, stop=True)
                ins.then_inc(q_["scores"], 1)
                if h < HA - 2:
                    slot(27 + 2 * h)
                pe.wait_ge(q_["weights"], h + 1)
                for i in range(PT):
                    dl = bank[6][:, 129 * i:129 * i + 129] if i < 3 else bank[7][:, 256:385]
                    ins = pe.matmul(dl, kw[:, i, :], vext[:, i, h, :], start=True, stop=True)
                ins.then_inc(q_["c_delta"], 1)
                pe.wait_ge(q_["weighted"], h + 1)
                for i in range(TILES):
                    dst = bank[4 + i // 3][0:rows(i), 129 * (i % 3):129 * (i % 3) + 129]
                    if i == 0:
                        ins = pe.matmul(dst, sT[:, 0, :], vext[:, 0, h, :], start=True, stop=True)
                    elif i < PT:
                        pe.matmul(dst, sT[:, i, :], vext[:, i, h, :], start=True, stop=False)
                        pe.wait_ge(q_["c_state"], PT * h + i)
                        ins = pe.matmul(dst, qt[:, cols(i)], C[:, i - 1, :], start=False, stop=True)
                    else:
                        pe.wait_ge(q_["v_spread"], h + 1)
                        for b in range(NB):
                            pe.matmul(dst, qpad[:, b, :], C0[:, b, :], start=b == 0, stop=False)
                        ins = pe.matmul(dst, sT[0:NS, PT, 0:NS], vext[0:NS, PT, h, :], start=False, stop=True)
                    if i in (2, PT):
                        ins.then_inc(q_["numerator"], 1)
                pe.wait_ge(q_["c_state"], PT * (h + 1))
                pe.wait_ge(q_["num_read"], h + 1)
                for dst, b0, b1 in ((bank[6], 3, 6), (bank[7], 6, 8), (bank[5], 0, 3)):
                    ins = pe.matmul(dst[:, 0:129 * (b1 - b0)], kw[0:NS, PT, :], vpad[0:NS, b0:b1, :], start=True, stop=True)
                ins.then_inc(q_["cs_delta"], 1)
                pe.nop().then_inc(q_["unit_projected"], 1)

            slot(22)
            slot(23)
            post(NJ - 1)
            slot(24)
            slot(25)
            for h in range(HA):
                unit(h)

            pe.wait_ge(q_["raw_collected"], 22)
            pe.wait_ge(q_["n_new"], HA)
            pe.wait_ge(q_["num_read"], HA)
            pe.transpose(bank[5][0:126, 0:128], shnew.rearrange("p b t -> p (b t)"), ident)
            cv = cvnew.rearrange("p b w c -> p (b w c)")
            pe.transpose(bank[5][0:96, 128:256], cv[:, 0:96], ident)
            pe.transpose(bank[5][0:96, 256:384], cv[:, 96:192], ident)
            pe.transpose(bank[5][0:24, 384:512], cv[:, 192:216], ident)
            pe.transpose(bank[4][0:36, 0:128], nnew.rearrange("p b h -> p (b h)"), ident).then_inc(q_["outs_turned"], 1)
            pe.wait_ge(q_["outs_ready"], 1)

            def recur(i, what):
                if what is None:
                    return
                n = rows(i)
                H = [slice(64 * h, 64 * h + 64) for h in range(HB)]
                Gi, Yi = G[i % 2], Y[i % 2]
                V = vtok[0:n, i, :]
                if what == "Z" and i < PT:
                    if i:
                        pe.wait_ge(q_["state"], i)
                        pe.wait_ge(q_["o_read"], i)
                    for j in range(NJ):
                        if i:
                            pe.matmul(bank[6][:, 128 * j:128 * j + 128], arr[:, j, 0, cols(i)], Sh[:, j, :], start=j == 0, stop=False, skip_group_check=True)
                        for h in (2 * j, 2 * j + 1):
                            ins = pe.matmul(bank[6][:, H[h]], Gi[:, 1, h, 0:128], V[:, H[h]], start=i + h == 0, stop=True, skip_group_check=True)
                    ins.then_inc(q_["z_projected"], 1)
                if what == "Z" and i == PT:
                    for j in range(NJ):
                        for b in range(NB):
                            dst = bank[6].rearrange("p (j v b t) -> p j v b t", j=NJ, v=2, b=NB)[:, j, :, b, :]
                            ins = pe.matmul(dst, SsT[:, j, b, :], arr[:, j, :, SEQ + LS * b:SEQ + LS * b + LS], start=True, stop=True)
                    ins.then_inc(q_["zt_projected"], 1)
                    pe.wait_ge(q_["zt_ready"], 1)
                    for v, dst in ((0, bank[6]), (1, bank[4])):
                        for j in range(NJ):
                            pe.matmul(dst[0:n, 128 * j:128 * j + 128], zt[:, j, v, :], ident, start=j == 0, stop=False, skip_group_check=True)
                    for h in range(HB):
                        ins = pe.matmul(bank[6][0:n, H[h]], Gi[0:n, 1, h, 0:n], V[:, H[h]], start=False, stop=True, skip_group_check=True)
                    ins.then_inc(q_["z_projected"], 1)
                if what == "U":
                    pe.wait_ge(q_["z_read"], i + 1)
                    if i:
                        pe.wait_ge(q_["hb_done"], i)
                    for h in range(HB):
                        ins = pe.matmul(bank[7][0:n, H[h]], Yi[0:n, h, 0:n], Zs[0:n, H[h]], start=True, stop=True)
                    ins.then_inc(q_["u_projected"], 1)
                if what == "O":
                    pe.wait_ge(q_["u_read"], i + 1)
                    ob = bank[6 if i < PT else 4]
                    for j in range(NJ):
                        if 0 < i < PT:
                            pe.matmul(ob[:, 128 * j:128 * j + 128], arr[:, j, 1, cols(i)], Sh[:, j, :], start=j == 0, stop=False, skip_group_check=True)
                        for h in (2 * j, 2 * j + 1):
                            pe.matmul(ob[0:n, H[h]], Gi[0:n, 1, h, 128:128 + n], V[:, H[h]], start=i + h == 0, stop=False, skip_group_check=True)
                            ins = pe.matmul(ob[0:n, H[h]], Gi[0:n, 0, h, 128:128 + n], Us[0:n, H[h]], start=False, stop=True, skip_group_check=True)
                    ins.then_inc(q_["o_projected"], 1)
                    if i < PT:
                        for j in range(NJ):
                            c_ = slice(128 * j, 128 * j + 128)
                            pe.matmul(bank[7][:, c_], kpt[i % 2][:, 1, c_], V[:, c_], start=True, stop=False)
                            ins = pe.matmul(bank[7][:, c_], kpt[i % 2][:, 0, c_], Us[:, c_], start=False, stop=True)
                        ins.then_inc(q_["s_projected"], 1)
                if what == "G":
                    if i < PT:
                        pe.wait_ge(q_["state"], i + 1)
                    pe.matmul(bank[7][0:n, :], sgl[:, cols(i)], g2w, start=True, stop=True).then_inc(q_["g_projected"], 1)

            for i in range(TILES):
                n = rows(i)
                pe.wait_ge(q_["ktmp_made"], i + 1)
                if i:
                    pe.wait_ge(q_["yx_read"], ix(i - 1, LV(i - 1) - 1, 1) + 1)
                for w in range(2):
                    for j in range(NJ):
                        ins = pe.transpose(bank[2 + w][0:n, 128 * j:128 * j + 128], ktmp[:, w, j, 0:n], ident)
                ins.then_inc(q_["kt_turned"], 1)
                for s_ in range(4):
                    q, w = s_ // 2, s_ % 2
                    if s_ == 1:
                        pe.wait_ge(q_["kt_read"], i + 1)
                    if s_ == 3:
                        pe.wait_ge(q_["gram_read"], 4 * i + 1)
                    for h in range(4 * q, 4 * q + 4):
                        r = slice(64 * (h % 2), 64 * (h % 2) + 64)
                        j = h // 2
                        dst = bank[2 * (s_ % 3) + h % 2][0:n, 256 * (j % 2):256 * (j % 2) + 256].rearrange("p (v t) -> p v t", v=2)[:, :, 0:n]
                        ins = pe.matmul(dst, (kap if w else nbeta)[r, j, cols(i)], arr[r, j, :, cols(i)], start=True, stop=True)
                    ins.then_inc(q_["grams"], 1)
                pe.wait_ge(q_["gram_read"], 4 * i + 4)
                for l in range(LV(i)):
                    for q in range(2):
                        k = ix(i, l, q)
                        pe.wait_ge(q_["mt_ready"], k + 1)
                        if l:
                            pe.wait_ge(q_["yx_read"], k - 1)
                        hi, lo = block_of(n, l)
                        for h in range(4):
                            if l == 0:
                                ins = pe.transpose(bank[q][0:n, 128 * h:128 * h + n], MT[q][0:n, h, 0:n], ident[0:n, 0:n])
                            else:
                                ins = pe.matmul(bank[q][hi, 128 * h:128 * h + lo.stop], MT[q][lo, h, hi], X[q][lo, h, lo], start=True, stop=True)
                        ins.then_inc(q_["w_projected"], 1)
                    for q in range(2):
                        if l:
                            pe.wait_ge(q_["w_read"], ix2(i, l, q) + 1)
                            for h in range(4):
                                yh = Y[i % 2][0:n, 4 * q + h, 0:n]
                                ins = pe.matmul(bank[2 + q][lo, 128 * h + hi.start:128 * h + hi.stop], W[q][hi, h, lo], yh[hi, hi], start=True, stop=True)
                                if l < LV(i) - 1:
                                    ins = pe.matmul(bank[4 + q][0:n, 128 * h:128 * h + n], yh, W[q][0:n, h, 0:n], start=True, stop=True)
                            ins.then_inc(q_["yx_projected"], 1)
                    recur(i - 1, hooks(i, l))
            recur(PT - 1, "G")
            pe.wait_ge(q_["sst_loaded"], 16 * HB)
            pe.wait_ge(q_["yx_read"], ix(PT, 2, 1) + 1)
            for j in range(NJ):
                if j >= 2:
                    pe.wait_ge(q_["st_read"], j - 1)
                for b in range(NB):
                    for h2 in range(2):
                        r = slice(64 * h2, 64 * h2 + 64)
                        ins = pe.matmul(bank[2 * (j % 2) + h2][r, 64 * b:64 * b + 64], Sld[r, j, b, :], ident[r, r], start=True, stop=True)
                ins.then_inc(q_["st_turned"], 1)
            for h in range(HB):
                r = slice(64 * (h % 2), 64 * (h % 2) + 64)
                ins = pe.matmul(bank[5][r, 64 * (h // 2):64 * (h // 2) + 64], S[:, h // 2, r], ident[:, r], start=True, stop=True)
            ins.then_inc(q_["ps_projected"], 1)
            pe.wait_ge(q_["st_read"], NJ)
            pe.wait_ge(q_["o_read"], PT)
            recur(PT, "Z")
            recur(PT, "U")
            recur(PT, "O")
            pe.wait_ge(q_["sst_scaled"], 1)
            for h in range(HB):
                r = slice(64 * (h % 2), 64 * (h % 2) + 64)
                j, H = h // 2, slice(64 * h, 64 * h + 64)
                pe.wait_ge(q_["kp_spread"], h + 1)
                pe.wait_ge(q_["kb_spread"], h + 1)
                if h >= 4:
                    pe.wait_ge(q_["ss_read"], h - 3)
                dst = bank[h % 4]
                for b in range(NB):
                    pe.matmul(dst[r, 64 * b:64 * b + 64], SsT[:, j, b, r], ident[:, r], start=b == 0, stop=False, skip_group_check=True)
                pe.matmul(dst[r, :], vtok[0:NS, PT, H], kppad[h % 2][0:NS, 1], start=False, stop=False, skip_group_check=True)
                ins = pe.matmul(dst[r, :], Us[0:NS, H], kppad[h % 2][0:NS, 0], start=False, stop=True, skip_group_check=True)
                ins.then_inc(q_["ss_projected"], 1)
            recur(PT, "G")

            def turn_h(i):
                n = rows(i)
                if i == 0:
                    pe.wait_ge(q_["o_read"], TILES)
                    pe.wait_ge(q_["ps_ready"], 1)
                if i == 1:
                    pe.wait_ge(q_["hb_done"], TILES)
                if i >= 2:
                    pe.wait_ge(q_["ht_ready"], i - 1)
                for k in range(KD):
                    ins = pe.transpose(bank[4 + 2 * (i % 2) + k // 4][:, 128 * (k % 4):128 * (k % 4) + n], hg[0:n, i, 128 * k:128 * k + 128], ident[0:n, 0:n])
                ins.then_inc(q_["h_turned"], 1)

            def mix(i):
                n = rows(i)
                pe.wait_ge(q_["ht_ready"], i + 1)
                if i >= 2:
                    pe.wait_ge(q_["mix_read"], i - 1)
                else:
                    pe.wait_ge(q_["ss_read"], HB)
                for q in range(2):
                    for k in range(KD):
                        ins = pe.matmul(bank[2 * (i % 2) + q][0:n, :], hT[k // 4][:, k % 4, cols(i)], wout[:, k, 512 * q:512 * q + 512], start=k == 0, stop=k == KD - 1)
                ins.then_inc(q_["mix_projected"], 1)

            turn_h(0)
            pe.wait_ge(q_["wout_loaded"], 16)
            mix(0)
            turn_h(1)
            for i in range(1, TILES):
                if i + 1 < TILES:
                    turn_h(i + 1)
                mix(i)
            for i in range(TILES):
                n = rows(i)
                pe.wait_ge(q_["ln1_done"], i + 1)
                if i >= 2:
                    pe.wait_ge(q_["x1_turned"], i - 1)
                else:
                    pe.wait_ge(q_["ht_ready"], TILES)
                for k in range(KD):
                    ins = pe.transpose(bank[4 + 2 * (i % 2) + k // 4][:, 128 * (k % 4):128 * (k % 4) + n], xln[0:n, i, 128 * k:128 * k + 128], ident[0:n, 0:n])
                ins.then_inc(q_["x1_in_psum"], 1)
            pe.wait_ge(q_["x1_turned"], TILES)
            for i in range(TILES):
                for k in range(KD):
                    ins = pe.matmul(bank[4][0:rows(i), NE * i:NE * i + NE], x1T[:, k, cols(i)], wrt[:, k, :], start=k == 0, stop=k == KD - 1)
            ins.then_inc(q_["routed"], 1)
            pe.wait_ge(q_["routing"], 2)
            for i in range(TILES):
                for i2 in range(i + 1):
                    pe.matmul(bank[5][:, NE * i:NE * i + NE], ones if i2 < i else tri_p[:, 0, :], s01[:, i2, :], start=i2 == 0, stop=i2 == i)
            for i in range(TILES):
                ins = pe.matmul(bank[5][:, NE * TILES:NE * TILES + NE], ones, s01[:, i, :], start=i == 0, stop=i == PT)
            ins.then_inc(q_["routed"], 1)
            for i in range(TILES):
                pe.wait_ge(q_["onehot"], i + 1)
                for e_ in range(NE):
                    ins = pe.matmul(bank[6][0:CAP, 2 * e_:2 * e_ + 2], onehot[i % 3][:, e_, :], tokid[:, i, :], start=i + e_ == 0, stop=i == PT, skip_group_check=True)
                ins.then_inc(q_["onehot_used"], 1)
            pe.wait_ge(q_["routing"], 3)

            def turn(e_, p_):
                pe.wait_ge(xs_loaded[p_], 8 * (e_ - p_) + 16)
                for k in range(KD):
                    ins = pe.transpose(bank[6 + k // 4][:, 128 * (k % 4):128 * (k % 4) + CAP], xs[p_][:, 128 * k:128 * k + 128], ident)
                ins.then_inc(q_["xs_turned"], 1)

            turn(0, 0)
            pe.nop().then_inc(q_["down"], 1)
            with pe.Fori(0, NE // 2) as it:
                for p_ in range(2):
                    wg, wu, wd = wexp[p_]
                    pe.wait_ge(wgu_loaded[p_], 32 * it + W0 + 32)
                    pe.wait_ge(q_["xst_ready"], 2 * it + p_ + 1)
                    for hf in range(2):
                        dst = bank[2 * p_ + hf]
                        for g_, w in enumerate((wg, wu)):
                            for f2 in range(2):
                                f = 2 * hf + f2
                                for k in range(KD):
                                    ins = pe.matmul(dst[:, 256 * g_ + 128 * f2:256 * g_ + 128 * f2 + CAP], w[:, k, 128 * f:128 * f + 128], xsT[p_][:, k, :], start=k == 0, stop=k == KD - 1)
                        ins.then_inc(q_["hidden"], 1)
                    if p_ == 0:
                        turn(2 * it + 1, 1)
                    else:
                        turn(2 * it + 2, 0)
                    pe.wait_ge(wd_loaded[p_], 16 * it + W0 + 16)
                    pe.wait_ge(q_["y_slots_ready"], 2 * it + p_ + 1)
                    for f in range(NF):
                        if f % 2 == 0:
                            pe.wait_ge(q_["hid_ready"], 4 * it + 2 * p_ + f // 2 + 2)
                        for q in range(2):
                            ins = pe.matmul(bank[4 + q][0:CAP, :], hid[:, f, :], wd[:, f, 512 * q:512 * q + 512], start=f == 0, stop=f == NF - 1)
                    ins.then_inc(q_["down"], 1)
            over = pe.value_load(flagu[0:1, 0:1], min_val=0, max_val=1)
            with pe.If(over):
                for i in range(TILES):
                    n = rows(i)
                    pe.wait_ge(q_["all_x"], 16 * TILES)
                    if i:
                        pe.wait_ge(q_["all_xt"], i)
                    for k in range(KD):
                        ins = pe.transpose(bank[6 + k // 4][:, 128 * (k % 4):128 * (k % 4) + n], dx[0:n, i, 128 * k:128 * k + 128], ident[0:n, 0:n])
                    ins.then_inc(q_["all_turned"], 1)
                pe.wait_ge(q_["all_xt"], TILES)
                pe.nop().then_inc(q_["all_down"], 1)
                with pe.Fori(0, NE) as it:
                    wg, wu, wd = dw
                    pe.wait_ge(q_["all_w"], 48 * it + 48)
                    for f in range(NF):
                        pe.wait_ge(q_["all_hid"], NF * it + f + 1)
                        for k in range(KD):
                            for w, A, B in ((wg, bank[0], bank[1]), (wu, bank[2], bank[3])):
                                pe.matmul(A[:, :], w[:, k, 128 * f:128 * f + 128], dxT[:, k, 0:SEQ], start=k == 0, stop=k == KD - 1)
                                ins = pe.matmul(B[:, 0:NS], w[:, k, 128 * f:128 * f + 128], dxT[:, k, SEQ:N], start=k == 0, stop=k == KD - 1)
                        ins.then_inc(q_["all_hidden"], 1)
                    pe.wait_ge(q_["all_hid"], NF * it + NF + 1)
                    for i in range(TILES):
                        n = rows(i)
                        pe.wait_ge(q_["all_read"], TILES * it + i + 1)
                        for q in range(2):
                            for f in range(NF):
                                ins = pe.matmul(bank[4 + q][0:n, :], dhid[:, f, cols(i)], wd[:, f, 512 * q:512 * q + 512], start=f == 0, stop=f == NF - 1)
                        ins.then_inc(q_["all_down"], 1)


def flat(src, n):
    v = src[0] if len(src.shape) > 1 else src
    if len(v.shape) == 2:
        w = v.shape[1]
        return v.rearrange("a (b f) -> (a b) f", f=128) if w >= 128 else v.rearrange("(a b) c -> a (b c)", b=128 // w)
    return v.rearrange("(a f) -> a f", f=128)


def brow(v, n):
    return v.rearrange("(a n) -> a n", a=1).to_broadcast([128, n])


def arr_off(ap):
    return ap.offset


INS = ["x_prompt", "x_sample", "state_mlstm_C", "state_mlstm_n", "state_mlstm_m", "state_mlstm_conv", "state_rwkv_S",
       "state_rwkv_shift", "ln0_g", "ln0_b", "w_in", "conv_w", "conv_b", "b_i", "b_f", "gn_a_g", "mu_shift", "w0", "w2",
       "a0", "a2", "g2", "k_k", "k_a", "r_k", "lnx_g", "lnx_b", "w_out", "ln1_g", "ln1_b", "w_router", "b_router",
       "we_gate", "we_up", "we_down", "ln2_g", "ln2_b"]
OUTS = [("y_prompt", (1, SEQ, D)), ("y_sample", (NB, LS, D)),
        ("p_C", (1, 1, HA, DHA, DHA)), ("p_n", (1, 1, HA, DHA)), ("p_m", (1, 1, HA)),
        ("p_conv", (1, 1, CW - 1, 2 * DA)), ("p_S", (1, 1, HB, DHB, DHB)), ("p_shift", (1, 1, 14 * 128)),
        ("s_C", (1, NB, HA, DHA, DHA)), ("s_n", (1, NB, HA, DHA)), ("s_m", (1, NB, HA)),
        ("s_conv", (1, NB, CW - 1, 2 * DA)), ("s_S", (1, NB, HB, DHB, DHB)), ("s_shift", (1, NB, 14 * 128))]


def kernel(**inputs):
    import concourse.bacc as bacc
    from concourse.bass_utils import run_bass_kernel_spmd

    nc = bacc.Bacc("TRN2", target_bir_lowering=False, num_devices=1)
    arrays, dr = {}, {}
    for name in INS:
        arrays[name] = np.ascontiguousarray(inputs[name])
        dr[name] = nc.dram_tensor(name, arrays[name].shape, F32, kind="ExternalInput").ap()
    for name, shape in OUTS:
        dr[name] = nc.dram_tensor(name, shape, F32, kind="ExternalOutput").ap()
    for name, shape in SCRATCH.items():
        dr[name] = nc.dram_tensor(name, shape, F32, kind="Internal").ap()
    build(nc, dr)
    got = run_bass_kernel_spmd(nc, [arrays], core_ids=[0]).results[0]
    return tuple(got[name] for name, _ in OUTS)
```
